# Optimizing a Trainium2 kernel written in Bass

```python
import math
import jax, jax.numpy as jnp
from jax import lax
import numpy as np

D_MODEL = 1024
BATCH = 1
SEQ = 1024
DEPTH = 1

CHUNK = 64
N_META = 16
SSD_PAD = (-N_META) % CHUNK
D_MIX = 2 * D_MODEL
D_A = D_MIX // 4
D_B = D_MIX // 2
D_C = D_MIX // 4
CONV_A_K = 3
SSM_HEAD_DIM = 64
SSM_HEADS = D_B // SSM_HEAD_DIM
SSM_GROUPS = 2
SSM_HPG = SSM_HEADS // SSM_GROUPS
SSM_STATE = 128
SSM_CONV_K = 4
CONF_K = 31
NORM_EPS = 1e-6
LN_EPS = 1e-5

IN_SIZES = [D_A, D_A, D_A, D_A,
            D_B, D_B, SSM_GROUPS * SSM_STATE, SSM_GROUPS * SSM_STATE, SSM_HEADS,
            D_C, D_C, D_C]
N_IN = int(sum(IN_SIZES))
IN_SPLITS = [int(v) for v in np.cumsum(IN_SIZES)[:-1]]

kernel_name = "hybrid_conv_ssd_conformer_trunk"

def rmsnorm(x, g):
    xf = x.astype(jnp.float32)
    y = xf * lax.rsqrt(jnp.mean(xf * xf, axis=-1, keepdims=True) + NORM_EPS)
    return (y * g.astype(jnp.float32)).astype(x.dtype)

def layernorm(x, g, b):
    xf = x.astype(jnp.float32)
    mu = jnp.mean(xf, axis=-1, keepdims=True)
    var = jnp.mean(jnp.square(xf - mu), axis=-1, keepdims=True)
    y = (xf - mu) * lax.rsqrt(var + LN_EPS)
    return (y * g.astype(jnp.float32) + b.astype(jnp.float32)).astype(x.dtype)

def causal_dwconv(x, w, b=None):
    k, c = w.shape
    out = lax.conv_general_dilated(
        x, w.astype(x.dtype).reshape(k, 1, c), window_strides=(1,), padding=[(k - 1, 0)],
        dimension_numbers=('NWC', 'WIO', 'NWC'), feature_group_count=c)
    if b is not None:
        out = out + b.astype(x.dtype)
    return out

def ssd_scan(x, b_mat, c_mat, dt_raw, dt_bias, a_log, d_skip):
    in_dtype = x.dtype
    f32 = jnp.float32
    bsz, l, _ = x.shape
    dt = jax.nn.softplus(dt_raw.astype(f32) + dt_bias.astype(f32))
    a = -jnp.exp(a_log.astype(f32))
    xg = x.astype(f32).reshape(bsz, l, SSM_GROUPS, SSM_HPG, SSM_HEAD_DIM)
    dtg = dt.reshape(bsz, l, SSM_GROUPS, SSM_HPG)
    xdt = xg * dtg[..., None]
    da = dtg * a.reshape(SSM_GROUPS, SSM_HPG)
    bm = b_mat.astype(f32).reshape(bsz, l, SSM_GROUPS, SSM_STATE)
    cm = c_mat.astype(f32).reshape(bsz, l, SSM_GROUPS, SSM_STATE)

    def front_pad(t):
        return jnp.pad(t, [(0, 0), (SSD_PAD, 0)] + [(0, 0)] * (t.ndim - 2))

    xdt, da, bm, cm = front_pad(xdt), front_pad(da), front_pad(bm), front_pad(cm)
    lp = l + SSD_PAD
    nc = lp // CHUNK
    xdt = xdt.reshape(bsz, nc, CHUNK, SSM_GROUPS, SSM_HPG, SSM_HEAD_DIM)
    bm = bm.reshape(bsz, nc, CHUNK, SSM_GROUPS, SSM_STATE)
    cm = cm.reshape(bsz, nc, CHUNK, SSM_GROUPS, SSM_STATE)
    da = da.reshape(bsz, nc, CHUNK, SSM_GROUPS, SSM_HPG).transpose(0, 3, 4, 1, 2)
    a_cum = jnp.cumsum(da, axis=-1)

    causal = jnp.tril(jnp.ones((CHUNK, CHUNK), dtype=bool))
    seg = a_cum[..., :, None] - a_cum[..., None, :]
    decay = jnp.exp(jnp.where(causal, seg, -jnp.inf))
    cb = jnp.einsum('bclgn,bcsgn->bcgls', cm, bm)
    y_diag = jnp.einsum('bcgls,bgecls,bcsgep->bclgep', cb, decay, xdt)

    decay_states = jnp.exp(a_cum[..., -1:] - a_cum)
    states = jnp.einsum('bclgn,bgecl,bclgep->bcgepn', bm, decay_states, xdt)
    chunk_decay = jnp.exp(a_cum[..., -1])

    def step(carry, inp):
        st, dec = inp
        new = carry * dec[..., None, None] + st
        return new, carry

    init = jnp.zeros((bsz, SSM_GROUPS, SSM_HPG, SSM_HEAD_DIM, SSM_STATE), f32)
    _, prev = lax.scan(step, init, (jnp.moveaxis(states, 1, 0), jnp.moveaxis(chunk_decay, 3, 0)))
    prev = jnp.moveaxis(prev, 0, 1)

    y_off = jnp.einsum('bclgn,bcgepn,bgecl->bclgep', cm, prev, jnp.exp(a_cum))
    y = (y_diag + y_off).reshape(bsz, lp, SSM_GROUPS, SSM_HPG, SSM_HEAD_DIM)[:, SSD_PAD:]
    y = y + xg * d_skip.astype(f32).reshape(SSM_GROUPS, SSM_HPG)[..., None]
    return y.reshape(bsz, l, D_B).astype(in_dtype)

def hybrid_mixer(h, w_in, w_out, conv_a_w, ssm_conv_w, ssm_conv_b, dt_bias, a_log, d_skip,
                 ssm_norm_g, conf_conv_w, conf_conv_b, conf_ln_g, conf_ln_b):
    proj = jnp.einsum('bld,dn->bln', h, w_in.astype(h.dtype))
    (a_b, a_c, a_x, a_z, b_z, b_x, b_bm, b_cm, b_dt, c_a, c_g, c_z) = jnp.split(proj, IN_SPLITS, axis=-1)

    y_a = a_b * causal_dwconv(a_c * a_x, conv_a_w) * jax.nn.silu(a_z)

    xbc = jax.nn.silu(causal_dwconv(jnp.concatenate([b_x, b_bm, b_cm], axis=-1), ssm_conv_w, ssm_conv_b))
    xs, bs, cs = jnp.split(xbc, [D_B, D_B + SSM_GROUPS * SSM_STATE], axis=-1)
    y_b = ssd_scan(xs, bs, cs, b_dt, dt_bias, a_log, d_skip)
    y_b = rmsnorm(y_b * jax.nn.silu(b_z), ssm_norm_g)

    u = c_a * jax.nn.sigmoid(c_g)
    u = causal_dwconv(u, conf_conv_w, conf_conv_b)
    u = layernorm(u, conf_ln_g, conf_ln_b)
    y_c = jax.nn.silu(u) * jax.nn.silu(c_z)

    y = jnp.concatenate([y_a, y_b, y_c], axis=-1)
    return jnp.einsum('blm,md->bld', y, w_out.astype(y.dtype))

def setup_inputs(seed: int = 0) -> dict:
    key = jax.random.key(seed)
    ks = jax.random.split(key, 20)
    f32 = jnp.float32
    x = jax.random.normal(ks[0], (BATCH, SEQ, D_MODEL), f32)
    meta = jax.random.normal(ks[1], (N_META, D_MODEL), f32)
    pre_g = 1.0 + 0.05 * jax.random.normal(ks[2], (DEPTH, D_MODEL), f32)
    post_g = 1.0 + 0.05 * jax.random.normal(ks[3], (DEPTH, D_MODEL), f32)
    w_in = jax.random.normal(ks[4], (DEPTH, D_MODEL, N_IN), f32) * D_MODEL ** -0.5
    w_out = jax.random.normal(ks[5], (DEPTH, D_MIX, D_MODEL), f32) * D_MIX ** -0.5
    conv_a_w = jax.random.normal(ks[6], (DEPTH, CONV_A_K, D_A), f32) * CONV_A_K ** -0.5
    n_xbc = D_B + 2 * SSM_GROUPS * SSM_STATE
    ssm_conv_w = jax.random.normal(ks[7], (DEPTH, SSM_CONV_K, n_xbc), f32) * SSM_CONV_K ** -0.5
    ssm_conv_b = 0.02 * jax.random.normal(ks[8], (DEPTH, n_xbc), f32)
    dt0 = jnp.exp(jax.random.uniform(ks[9], (DEPTH, SSM_HEADS), f32, math.log(1e-3), math.log(1e-1)))
    dt_bias = dt0 + jnp.log(-jnp.expm1(-dt0))
    a_log = jnp.log(jax.random.uniform(ks[10], (DEPTH, SSM_HEADS), f32, 1.0, 16.0))
    d_skip = 1.0 + 0.1 * jax.random.normal(ks[11], (DEPTH, SSM_HEADS), f32)
    ssm_norm_g = 1.0 + 0.05 * jax.random.normal(ks[12], (DEPTH, D_B), f32)
    conf_conv_w = jax.random.normal(ks[13], (DEPTH, CONF_K, D_C), f32) * CONF_K ** -0.5
    conf_conv_b = 0.02 * jax.random.normal(ks[14], (DEPTH, D_C), f32)
    conf_ln_g = 1.0 + 0.05 * jax.random.normal(ks[15], (DEPTH, D_C), f32)
    conf_ln_b = 0.02 * jax.random.normal(ks[16], (DEPTH, D_C), f32)
    return {"x": x, "meta": meta, "pre_g": pre_g, "post_g": post_g, "w_in": w_in, "w_out": w_out,
            "conv_a_w": conv_a_w, "ssm_conv_w": ssm_conv_w, "ssm_conv_b": ssm_conv_b,
            "dt_bias": dt_bias, "a_log": a_log, "d_skip": d_skip, "ssm_norm_g": ssm_norm_g,
            "conf_conv_w": conf_conv_w, "conf_conv_b": conf_conv_b,
            "conf_ln_g": conf_ln_g, "conf_ln_b": conf_ln_b}

def reference(x, meta, pre_g, post_g, w_in, w_out, conv_a_w, ssm_conv_w, ssm_conv_b,
              dt_bias, a_log, d_skip, ssm_norm_g, conf_conv_w, conf_conv_b, conf_ln_g, conf_ln_b):
    bsz = x.shape[0]
    meta_b = jnp.broadcast_to(meta.astype(x.dtype)[None], (bsz, N_META, D_MODEL))
    h = jnp.concatenate([meta_b, x], axis=1)
    for i in range(DEPTH):
        m = hybrid_mixer(rmsnorm(h, pre_g[i]), w_in[i], w_out[i], conv_a_w[i], ssm_conv_w[i],
                         ssm_conv_b[i], dt_bias[i], a_log[i], d_skip[i], ssm_norm_g[i],
                         conf_conv_w[i], conf_conv_b[i], conf_ln_g[i], conf_ln_b[i])
        h = h + rmsnorm(m, post_g[i])
    return h[:, N_META:]


_drawn_inputs = setup_inputs


def setup_inputs(seed=0):
    import zlib

    import numpy as np

    out = dict(_drawn_inputs(seed))
    spreads = {}
    factors = {'ssm_conv_b': 3.322,
     'conf_conv_b': 8.0,
     'conf_ln_g': 5.828,
     'conf_ln_b': 27.045,
     'ssm_norm_g': 3.367}
    for name, (base, spread) in spreads.items():
        noise = np.random.default_rng([zlib.crc32(name.encode()), seed]).standard_normal(out[name].shape)
        drawn = base * np.exp(spread * noise) if base else spread * noise
        out[name] = __import__('jax').numpy.asarray(drawn.astype(out[name].dtype))
    for name, factor in factors.items():
        out[name] = (out[name] * factor).astype(out[name].dtype)
    return out
```

```python
from contextlib import ExitStack

import concourse.bass as bass
from concourse import mybir

ALU = mybir.AluOpType
ACT = mybir.ActivationFunctionType
F32 = mybir.dt.float32
F32R = mybir.dt.float32r

P = 128
D = 1024
META = 16
SEQ = 1024
L = META + SEQ
KD = D // P
TOK = SEQ // P
D_A = D_C = 512
D_B = 1024
N_A, N_B, N_C = D_A // P, D_B // P, D_C // P
N_Y = N_A + N_B + N_C
HEADS, HD = 16, 64
GROUPS = 2
HPG = HEADS // GROUPS
GT = N_B // GROUPS
KA, KS, KC = 3, 4, 31
HALF = 512
NORM_EPS, LN_EPS = 1e-6, 1e-5

FULL = [(0, 348), (348, 346), (694, 346)]
REAL = [(META, HALF), (META + HALF, HALF)]


CREDIT = 1


class Phase:

    def __init__(self, before, rounds, slots, chunks, banks=None):
        self.rounds, self.slots, self.chunks = rounds, slots, chunks
        self.tile0 = before.tile0 + before.rounds * len(before.slots) if before else 0
        self.chunk0 = before.chunk0 + before.rounds * before.per_round if before else 0
        self.loads0 = [before.loads0[s] + before.rounds * before.slots.count(s) if before else 0 for s in range(3)]
        self.per_round = sum(map(len, chunks))
        self.banks = banks or [q % 3 for q in range(self.per_round)]

    def tile(self, i, p):
        return self.tile0 + i * len(self.slots) + p

    def chunk(self, i, q):
        return self.chunk0 + i * self.per_round + q

    def first(self, p):
        return sum(map(len, self.chunks[:p]))

    def loads(self, i, p):
        s = self.slots[p]
        return self.loads0[s] + i * self.slots.count(s) + self.slots[:p + 1].count(s)


PH_DT = Phase(None, 1, [2], [FULL])
PH_C0 = Phase(PH_DT, 1, [0, 1], [FULL] * 2)
PH_XC = Phase(PH_C0, 3, [0, 1, 2, 0, 1], [FULL] * 5)
PH_X3 = Phase(PH_XC, 1, [0, 1, 2], [FULL] * 3)
PH_AS = Phase(PH_X3, 4, [0, 1, 0, 1], [FULL, FULL, REAL, REAL], [0, 1, 2, 0, 1, 2, 0, 1, 2, 3])
PH_Z = Phase(PH_AS, 4, [0, 1, 2], [REAL] * 3)
PH_OUT = Phase(PH_Z, 2, [0, 1] * 4, [[]] * 8)
N_TILES = PH_OUT.tile(2, 0)
N_CHUNKS = PH_OUT.chunk0
OUT_K = [4, 5, 6, 7, 8, 9, 10, 11, 0, 1, 2, 3, 12, 13, 14, 15]


PRM = {}
for _name, _n in [("pre_g", KD), ("ssm_w", 12 * (KS + 1)), ("conf_w", 4 * (KC + 1)),
                  ("ln_g", 4), ("ln_b", 4), ("gain", N_Y), ("d_skip", N_B), ("a_log", HEADS),
                  ("conv_a", 4 * KA), ("dt_bias", 1), ("norm_eps", 1), ("ln_eps", 1)]:
    PRM[_name] = (sum(n for _, n in PRM.values()), _n)
N_PRM = sum(n for _, n in PRM.values())


def hybrid_mixer_kernel(nc, xT, x, w_tiles, params, post_g, acum_dram, out):
    ctx = ExitStack()

    BASE = 288

    def at(name, offset, shape, dtype=F32):
        return nc.alloc_sbuf_tensor_at(name, shape, dtype, offset=4 * (BASE + offset))

    h_hi = at("h_hi", 0, [P, KD, L], F32R)
    h_lo = at("h_lo", KD * L, [P, KD, L], F32R)
    y_hi = at("y_hi", 0, [P, N_Y, SEQ], F32R)
    o = 2 * KD * L
    YA, XBC = o, o + N_A * SEQ
    YC = XBC + 12 * L
    y_a = at("y_a", YA, [P, N_A, SEQ])
    xbc = at("xbc", XBC, [P, 12, L])
    y_c = at("y_c", YC, [P, N_C, SEQ])
    lo_a = at("lo_a", YA, [P, N_A, SEQ], F32R)
    lo_b = at("lo_b", XBC, [P, N_B, L], F32R)
    lo_c = at("lo_c", YC, [P, N_C, SEQ], F32R)
    z_c = at("z_c", XBC + N_B * L, [P, N_C, SEQ])
    part = at("part", XBC + N_B * L, [P, TOK, HALF])
    o = YC + N_C * SEQ
    w_raw = at("w_raw", o, [P, 3, 1024])
    w_lo = at("w_lo", o, [P, 3, 1024], F32R)
    w_hi = at("w_hi", o + 3072, [P, 3, 1024], F32R)
    o += 6144
    small = {}
    for name, shape in [("ones_d", [P, P]), ("ones_c", [P, P]), ("ones", [P, P]), ("tri", [P, P]), ("ident", [P, P]),
                        ("mask4", [P, 4, P]), ("prm", [P, N_PRM]), ("cur_ssm", [P, 8]), ("cur_conf", [P, KC + 1]),
                        ("cur_a", [P, 4]), ("dts", [P, 4, TOK + 1, HEADS]), ("cur_dt", [P, 4, HEADS]),
                        ("a_neg", [P, HEADS]), ("dt_dec", [P, HEADS]), ("r_b", [P, TOK]), ("ssq", [P, TOK]),
                        ("r_out", [P, TOK]), ("credits", [P, 16])]:
        n = 1
        for s in shape[1:]:
            n *= s
        small[name] = at(name, o, shape)
        o += (n + 7) // 8 * 8
    ones_d, ones_c, ones, tri, ident, mask4 = (small[n] for n in ("ones_d", "ones_c", "ones", "tri", "ident", "mask4"))
    prm, cur_ssm, cur_conf, cur_a = (small[n] for n in ("prm", "cur_ssm", "cur_conf", "cur_a"))
    dts, cur_dt, a_neg, dt_dec, r_b, ssq, r_out, credits = (
        small[n] for n in ("dts", "cur_dt", "a_neg", "dt_dec", "r_b", "ssq", "r_out", "credits"))
    W = o

    x_ch = [at(f"x_ch{b}", W + 5568 * b, [P, KD, 348]) for b in range(2)]
    sq_ch = at("sq_ch", W + 2784, [P, KD, 348])
    rs_ch = [at(f"rs_ch{b}", W + 8360 + 352 * b, [P, 348]) for b in range(2)]
    dt_cm = at("dt_cm", W + 9088, [HEADS, L])
    acum_rows = at("acum_rows", W, [HEADS, SEQ])
    NDT = (TOK + 1) * HEADS
    sp = [at(f"sp{n}", W + 10144 + NDT * n, [P, NDT]) for n in range(6)]
    xr = [at(f"xr{b}", W + 1048 * b, [P, KS - 1 + L]) for b in range(2)]
    acc = [at(f"acc{b}", W + 2096 + 1040 * b, [P, L]) for b in range(2)]
    PAD_C = KC - 1 - META
    UC = [W + 4176, W + 8368]
    uc2 = at("uc", UC[0], [P, UC[1] - UC[0] + PAD_C + L])
    sg = at("sg", W + 5232, [P, L])
    e = [at(f"e{g}", W + 1024 * g, [P, HPG, P]) for g in range(2)]
    xdt0 = at("xdt0", W + 1024, [META, HEADS, HD])
    xs_st = at("xs_st", W + 2048, [P, N_B, P])
    bc_st = at("bc_st", W + 3072, [P, 4, P])
    b_cb = at("b_cb", W + 3584, [P, 4, P])
    ea = at("ea", W + 4096, [P, N_B, P])
    xd = [at("xd0", W + 5120, [P, HPG, HD]), at("xd1", W + 8368, [P, HPG, HD])]
    xdd = [at("xdd0", W + 5632, [P, HPG, HD]), at("xdd1", W + 8880, [P, HPG, HD])]
    PAD_A = KA - 1
    t1 = at("t1", W + 6272, [P, PAD_A + SEQ + 8])
    t2 = at("t2", W + 7320, [P, L])
    ytmp = at("ytmp", W + 9392, [P, GT, P])
    state = at("state", W + 9904, [P, HEADS, HD])
    zt = [at(f"zt{b}", W + 1024 * b, [P, SEQ]) for b in range(2)]
    sqb = at("sqb", W + 2048, [P, SEQ])
    sqs = at("sqs", W + 3072, [P, SEQ])
    csq = at("csq", W + 4096, [P, N_C, SEQ])
    c_rs = at("c_rs", W + 8192, [P, SEQ])
    ob = at("ob", W, [P, TOK, D])
    x_tm = [at(f"x_tm{b}", W + 8192 + 1024 * b, [P, D]) for b in range(2)]
    pg = at("pg", W + 10240, [P, D])
    junk = at("junk", 0, [P, D])

    ps = ctx.enter_context(nc.psum_tensor("ps", [P, 8, HALF], F32))
    bX, bS, bY, bO = 4, 5, 6, 7

    def prm_col(name, j=0, n=1):
        return prm[:, PRM[name][0] + j:PRM[name][0] + j + n]

    def sem(name):
        return ctx.enter_context(nc.semaphore(name))

    prm_in, w_in = sem("prm_in"), [sem(f"w_in{s}") for s in range(3)]
    xch_in = [sem("xch_in0"), sem("xch_in1")]
    consts = sem("consts")
    sq_done, stat_done, sd_done, hn_done, hhi_done, h_ready = map(
        sem, ("sq_done", "stat_done", "sd_done", "hn_done", "hhi_done", "h_ready"))
    whi_done, wlo_done = sem("whi_done"), sem("wlo_done")
    in_done, in_evac = sem("in_done"), sem("in_evac")
    dve_step = sem("dve_step")
    dtT_done, dt_abs, dt_act, sp_abs, dt_den, dt_ready = map(
        sem, ("dtT_done", "dt_abs", "dt_act", "sp_abs", "dt_den", "dt_ready"))
    cum_done, cum_copied, diff_done, dec_done, cumT_done, rows_ready, rows_saved = map(
        sem, ("cum_done", "cum_copied", "diff_done", "dec_done", "cumT_done", "rows_ready", "rows_saved"))
    metaT_done, meta_ready = map(sem, ("metaT_done", "meta_ready"))
    ssm_conv, ssm_silu, u_done, conf_done = map(sem, ("ssm_conv", "ssm_silu", "u_done", "conf_done"))
    e_in, ea_in = [sem("e_in0"), sem("e_in1")], sem("ea_in")
    staged, seg_done, exp_done, ea_exp = map(sem, ("staged", "seg_done", "exp_done", "ea_exp"))
    turn_done, bcb_done, xd_done, m_done, scan_done, y_done, st_done = map(
        sem, ("turn_done", "bcb_done", "xd_done", "m_done", "scan_done", "y_done", "st_done"))
    au_done, aconv_done, ab_done, ya_done = map(sem, ("au_done", "aconv_done", "ab_done", "ya_done"))
    cmean_done, cmid_done, csq_done, cvar_done, csd_done, cnorm_done, csilu_done, yc_done = map(
        sem, ("cmean_done", "cmid_done", "csq_done", "cvar_done", "csd_done", "cnorm_done", "csilu_done", "yc_done"))
    zb_done, sqs_done, bms_done, bsd_done, rb_done = map(sem, ("zb_done", "sqs_done", "bms_done", "bsd_done", "rb_done"))
    yhi_done, ylo_done, out_done, pass_done, part_done, sum_done = map(
        sem, ("yhi_done", "ylo_done", "out_done", "pass_done", "part_done", "sum_done"))
    ssq_done, osd_done, xtm_in, pg_in, fin_done, saved = (
        sem("ssq_done"), sem("osd_done"), [sem("xtm_in0"), sem("xtm_in1")], sem("pg_in"), sem("fin_done"),
        [sem("saved0"), sem("saved1")])

    def y_f32(k, a=0, n=SEQ):
        if k < N_A:
            return y_a[:, k, a:a + n]
        if k < N_A + N_B:
            return xbc[:, k - N_A, META + a:META + a + n]
        return y_c[:, k - N_A - N_B, a:a + n]

    def y_rest(k, a=0, n=SEQ):
        if k < N_A:
            return lo_a[:, k, a:a + n]
        if k < N_A + N_B:
            return lo_b[:, k - N_A, META + a:META + a + n]
        return lo_c[:, k - N_A - N_B, a:a + n]

    def banks(b, n):
        return ps[:, b:b + n, :].rearrange("p b c -> p (b c)")

    block = ctx.enter_context(nc.Block())

    @block.sync
    def _(eng):
        def load_w(slot, tile):
            src = w_tiles[tile] if isinstance(tile, int) else w_tiles[bass.ds(tile, 1)].rearrange("o p n -> p (o n)")
            eng.dma_start(w_raw[:, slot, :], src).then_inc(w_in[slot], 16)

        eng.dma_start(prm[:], params).then_inc(prm_in, 16)
        for n, (a, w) in enumerate(FULL):
            if n == 2:
                eng.wait_ge(h_ready, 1)
            eng.dma_start(x_ch[n % 2][:, :, 0:w], xT[:, :, a:a + w]).then_inc(xch_in[n % 2], 16)
            if n == 0:
                load_w(PH_DT.slots[0], 0)
                load_w(PH_C0.slots[0], 1)

        def next_w(ph, i, p):
            eng.wait_ge(in_done, ph.chunk(i, ph.first(p)))
            last = p + 1 == len(ph.slots)
            load_w(0 if last else ph.slots[p + 1], ph.tile(i, p + 1))

        for p in range(2):
            next_w(PH_C0, 0, p)
        with eng.Fori(0, PH_XC.rounds) as i:
            for p in range(5):
                next_w(PH_XC, i, p)
        for p in range(3):
            next_w(PH_X3, 0, p)
        eng.wait_ge(rows_ready, 1)
        eng.dma_start(acum_dram, acum_rows[:]).then_inc(rows_saved, 16)
        eng.wait_ge(rows_saved, 16)
        eng.wait_ge(scan_done, CREDIT)

        def load_decays(m):
            for g in range(GROUPS):
                eng.wait_ge(scan_done, CREDIT + m * GROUPS)
                src = acum_dram[HPG * g:HPG * (g + 1), bass.ds(m * P, P)]
                eng.dma_start(e[g][:], src.partition_broadcast(P)).then_inc(e_in[g], 16)
            eng.wait_ge(y_done, CREDIT + m * GROUPS)
            for h in range(2):
                src = acum_dram[h:HEADS:2, bass.ds(m * P, P)]
                eng.dma_start(ea[HD * h:HD * (h + 1)], src.partition_broadcast(HD)).then_inc(ea_in, 16)

        with eng.Fori(0, PH_AS.rounds) as j:
            load_decays(j * 2)
            next_w(PH_AS, j, 0)
            next_w(PH_AS, j, 1)
            load_decays(j * 2 + 1)
            next_w(PH_AS, j, 2)
            next_w(PH_AS, j, 3)
        with eng.Fori(0, PH_Z.rounds) as j:
            for p in range(3):
                next_w(PH_Z, j, p)
        for n in range(1, 16):
            eng.wait_ge(in_done, N_CHUNKS)
            if n >= 2:
                if (n - 2) % 4 == 3:
                    eng.wait_ge(pass_done, TOK * ((n - 2) // 4 + 1))
                else:
                    eng.wait_ge(out_done, n - 1 - (n - 2) // 4)
            load_w(n % 2, PH_OUT.tile0 + n)
        eng.wait_ge(cnorm_done, 1)
        eng.dma_start(pg[:], post_g.partition_broadcast(P)).then_inc(pg_in, 16)
        for t in range(TOK):
            if t >= 2:
                eng.wait_ge(fin_done, t - 1)
                eng.wait_ge(saved[t % 2], 16 * (t // 2))
            eng.dma_start(x_tm[t % 2][:], x[0, t * P:(t + 1) * P, :]).then_inc(xtm_in[t % 2], 16)
            if t >= 1:
                eng.wait_ge(fin_done, t)
                eng.dma_start(out[0, (t - 1) * P:t * P, :], x_tm[(t - 1) % 2][:]).then_inc(saved[(t - 1) % 2], 16)
        eng.wait_ge(fin_done, TOK)
        eng.dma_start(out[0, SEQ - P:SEQ, :], x_tm[(TOK - 1) % 2][:]).then_inc(saved[(TOK - 1) % 2], 16)
        for s in saved:
            eng.wait_ge(s, 16 * (TOK // 2))

    @block.gpsimd
    def _(eng):
        eng.memset(ones_d[:], 1.0 / D).then_inc(consts, 1)
        eng.memset(ones_c[:], 1.0 / D_C).then_inc(consts, 1)
        eng.memset(ones[:], 1.0).then_inc(consts, 1)
        eng.memset(ident[:], 0.0).then_inc(consts, 1)
        eng.memset(tri[:], 1.0).then_inc(consts, 1)
        eng.memset(mask4[:], 1.0).then_inc(consts, 1)
        eng.memset(sp[0][:], -1e4).then_inc(consts, 1)
        eng.wait_ge(consts, 7)
        eng.affine_select(out=ident[:], in_=ident[:], compare_op=ALU.not_equal, fill=1.0, base=0,
                          pattern=[[-1, P]], channel_multiplier=1).then_inc(consts, 1)
        eng.affine_select(out=tri[:], in_=tri[:], compare_op=ALU.is_ge, fill=0.0, base=0,
                          pattern=[[1, P]], channel_multiplier=-1).then_inc(consts, 1)
        eng.affine_select(out=mask4[:, 2:4, :], in_=mask4[:, 2:4, :], compare_op=ALU.is_ge, fill=0.0, base=0,
                          pattern=[[0, 2], [1, P]], channel_multiplier=-1).then_inc(consts, 1)

    @block.scalar
    def _(eng):
        act = eng.activation

        def split_w(slot, loads, n=1):
            eng.wait_ge(w_in[slot], loads * 16)
            act(w_hi[:, slot, :], w_raw[:, slot, :], ACT.Copy).then_inc(whi_done, 1)

        def split_next(ph, i, p):
            if p + 1 < len(ph.slots):
                split_w(ph.slots[p + 1], ph.loads(i, p + 1))
            else:
                split_w(0, ph.loads0[0] + (i + 1) * ph.slots.count(0) + 1)

        def evac(ph, i, q, dst, func=ACT.Copy, rows=P, bias=0.0):
            p = next(p for p in range(len(ph.slots) - 1, -1, -1) if q >= ph.first(p))
            a, w = ph.chunks[p][q - ph.first(p)]
            eng.wait_ge(in_done, ph.chunk(i, q) + 1)
            act(dst, ps[0:rows, ph.banks[q], 0:w], func, bias=bias).then_inc(in_evac, 1)

        for n, (a, w) in enumerate(FULL):
            eng.wait_ge(xch_in[n % 2], 16 * (n // 2 + 1))
            if n >= 1:
                eng.wait_ge(stat_done, n)
            act(sq_ch[:, :, 0:w], x_ch[n % 2][:, :, 0:w], ACT.Square).then_inc(sq_done, 1)
            if n == 0:
                split_w(PH_DT.slots[0], 1)
                eng.wait_ge(prm_in, 16)
                act(credits[:, 8:9], prm[:, 0:1], ACT.Copy).then_inc(ssm_silu, 1)
            eng.wait_ge(stat_done, n + 1)
            if n == 2:
                eng.wait_ge(hn_done, 1)
            act(rs_ch[n % 2][:, 0:w], ps[:, 4 + n, 0:w], ACT.Sqrt, bias=prm_col("norm_eps")).then_inc(sd_done, 1)
            eng.wait_ge(hn_done, n + 1)
            act(h_hi[:, :, a:a + w], x_ch[n % 2][:, :, 0:w], ACT.Copy).then_inc(hhi_done, 1)
        split_w(0, 1)
        for q, (a, w) in enumerate(FULL):
            evac(PH_DT, 0, q, dt_cm[:, a:a + w], ACT.Identity, HEADS, prm[0:HEADS, PRM["dt_bias"][0]:PRM["dt_bias"][0] + 1])
        eng.wait_ge(dt_abs, 1)
        act(sp[1][:], sp[0][:], ACT.Abs).then_inc(sp_abs, 1)
        eng.wait_ge(sp_abs, 1)
        act(sp[2][:], sp[1][:], ACT.Exp, scale=-1.0).then_inc(dt_act, 1)
        act(a_neg[:], prm_col("a_log", 0, HEADS), ACT.Exp).then_inc(dt_act, 1)

        def gate_tile(ph, i, p, n):
            split_next(ph, i, p)
            if not isinstance(n, int):
                eng.wait_ge(u_done, n)
            for q, (a, w) in enumerate(FULL):
                evac(ph, i, ph.first(p) + q, sg[:, a:a + w], ACT.Sigmoid)

        def value_tile(ph, i, p, n, where):
            split_next(ph, i, p)
            for q, (a, w) in enumerate(FULL):
                evac(ph, i, ph.first(p) + q, uc2[:, bass.ds(where + (PAD_C + a), w)])

        def ssm_tile(ph, i, r, n):
            split_next(ph, i, n)
            eng.wait_ge(ssm_conv, CREDIT + 3 * r + (1 if n == 2 else 0))
            for q, (a, w) in enumerate(FULL):
                evac(ph, i, 3 * n + q, xr[n % 2][:, KS - 1 + a:KS - 1 + a + w])

        def ssm_act(r, n):
            eng.wait_ge(ssm_conv, CREDIT + 3 * r + n + 1)
            act(xbc[:, bass.ds(3 * r + n, 1), :].rearrange("p o l -> p (o l)"), acc[n % 2][:], ACT.Silu).then_inc(ssm_silu, 1)

        gate_tile(PH_C0, 0, 0, 0)
        value_tile(PH_C0, 0, 1, 0, 0)
        with eng.Fori(0, PH_XC.rounds) as i:
            ssm_tile(PH_XC, i, i, 0)
            ssm_tile(PH_XC, i, i, 1)
            ssm_act(i, 0)
            ssm_tile(PH_XC, i, i, 2)
            ssm_act(i, 1)
            gate_tile(PH_XC, i, 3, i + 1)
            ssm_act(i, 2)
            eng.wait_ge(conf_done, CREDIT + i)
            value_tile(PH_XC, i, 4, i + 1, ((i + 1) % 2) * (UC[1] - UC[0]))
        ssm_tile(PH_X3, 0, 3, 0)
        ssm_tile(PH_X3, 0, 3, 1)
        ssm_act(3, 0)
        ssm_tile(PH_X3, 0, 3, 2)
        ssm_act(3, 1)
        ssm_act(3, 2)

        eng.wait_ge(diff_done, 1)
        act(dts[:, 2], dts[:, 2], ACT.Exp).then_inc(dec_done, 1)
        act(dts[:, 3], dts[:, 3], ACT.Exp).then_inc(dec_done, 1)

        eng.wait_ge(ssm_silu, CREDIT + 12)
        with eng.Fori(0, PH_AS.rounds) as j:
            ph = PH_AS

            def stage(m):
                eng.wait_ge(scan_done, CREDIT + m * GROUPS)
                eng.wait_ge(y_done, CREDIT + m * GROUPS)
                act(bc_st[:], xbc[:, N_B:12, bass.ds(m * P + META, P)], ACT.Copy).then_inc(staged, 1)
                act(xs_st[:], xbc[:, 0:N_B, bass.ds(m * P + META, P)], ACT.Copy).then_inc(staged, 1)

            def exps(m):
                for g in range(GROUPS):
                    eng.wait_ge(seg_done, m * GROUPS + g + 1)
                    act(e[g][:], e[g][:], ACT.Exp).then_inc(exp_done, 1)

            def exp_off(m):
                eng.wait_ge(ea_in, (m + 1) * 32)
                act(ea[:], ea[:], ACT.Exp).then_inc(ea_exp, 1)

            m = j * 2
            stage(m)
            split_next(ph, j, 0)
            eng.wait_ge(ya_done, CREDIT + j)
            for q in range(3):
                a, w = FULL[q]
                lo, s = max(a, META - PAD_A), META - PAD_A
                eng.wait_ge(in_done, ph.chunk(j, q) + 1)
                act(t1[:, lo - s:a + w - s], ps[:, ph.banks[q], lo - a:w], ACT.Copy).then_inc(in_evac, 1)
                if q == 1:
                    exps(m)
            exp_off(m)
            split_next(ph, j, 1)
            eng.wait_ge(ab_done, CREDIT + j)
            for q in range(3):
                a, w = FULL[q]
                evac(ph, j, 3 + q, t2[:, a:a + w])
                if q == 1:
                    stage(m + 1)
            split_next(ph, j, 2)
            eng.wait_ge(au_done, j + 1)
            for q in range(2):
                a, w = REAL[q]
                evac(ph, j, 6 + q, t2[:, a:a + w])
                if q == 0:
                    exps(m + 1)
            exp_off(m + 1)
            split_next(ph, j, 3)
            eng.wait_ge(aconv_done, j + 1)
            for q in range(2):
                a, w = REAL[q]
                evac(ph, j, 8 + q, t1[:, a - META:a - META + w], ACT.Silu)

        for n in range(N_C):
            eng.wait_ge(cmid_done, n + 1)
            act(csq[:, n, :], y_c[:, n, :], ACT.Square).then_inc(csq_done, 1)
        with eng.Fori(0, PH_Z.rounds) as j:
            ph = PH_Z
            for p in range(3):
                split_next(ph, j, p)
                if p < 2:
                    eng.wait_ge(zb_done, CREDIT + 2 * j)
                for q in range(2):
                    a, w = REAL[q]
                    if p < 2:
                        evac(ph, j, 2 * p + q, zt[p][:, a - META:a - META + w], ACT.Silu)
                    else:
                        evac(ph, j, 4 + q, z_c[:, bass.ds(j, 1), a - META:a - META + w].rearrange("p o l -> p (o l)"), ACT.Silu)
        eng.wait_ge(bms_done, 1)
        act(r_b[:], ps[:, bX, 0:TOK], ACT.Sqrt, bias=prm_col("norm_eps")).then_inc(bsd_done, 1)
        eng.wait_ge(cvar_done, 1)
        act(c_rs[:], banks(bY, 2), ACT.Sqrt, bias=prm_col("ln_eps")).then_inc(csd_done, 1)

        def head(n):
            k = OUT_K[n]
            act(y_hi[:, k, :], y_f32(k), ACT.Copy, scale=prm_col("gain", k)).then_inc(yhi_done, 1)

        def out_w(n):
            split_w(n % 2, PH_OUT.loads0[n % 2] + n // 2 + 1)

        eng.wait_ge(in_done, N_CHUNKS)
        for n in range(8):
            head(n)
        out_w(1)
        for n in range(N_C):
            eng.wait_ge(cnorm_done, n + 1)
            act(y_c[:, n, :], y_c[:, n, :], ACT.Silu, scale=prm_col("ln_g", n), bias=prm_col("ln_b", n)).then_inc(csilu_done, 1)
        for n in range(8, 12):
            head(n)
        out_w(2)
        for n in range(12, 16):
            eng.wait_ge(yc_done, n - 11)
            head(n)
        eng.wait_ge(rb_done, 1)
        for h in range(2):
            for n in range(3 if h == 0 else 9, 5 + 8 * h):
                out_w(n)
            for t in range(TOK):
                eng.wait_ge(pass_done, 16 * h + t + 1)
                if h:
                    eng.wait_ge(sum_done, CREDIT + t + 1)
                act(part[:, t, :], ps[:, t, :], ACT.Copy, scale=r_b[:, t:t + 1]).then_inc(part_done, 1)
            for n in range(5 + 8 * h, 9 + 7 * h):
                out_w(n)
        for t in range(TOK):
            eng.wait_ge(sum_done, CREDIT + TOK + t + 1)
            act(junk[:], ob[:, t, :], ACT.Square, accum_out=ssq[:, t:t + 1]).then_inc(ssq_done, 1)
            eng.wait_ge(ssq_done, t + 1)
            act(r_out[:, t:t + 1], ssq[:, t:t + 1], ACT.Sqrt, scale=1.0 / D, bias=prm_col("norm_eps")).then_inc(osd_done, 1)

    @block.tensor
    def _(eng):
        mm = eng.matmul

        def chunk(ph, i, p, q, bank, a, w):
            s = ph.slots[p]
            if q == ph.first(p):
                eng.wait_ge(wlo_done, ph.tile(i, p) + 1)
            if not (isinstance(i, int) and ph.chunk(i, q) < 3):
                eng.wait_ge(in_evac, ph.chunk(i, q) - 2)
            for k in range(KD):
                hi, lo = w_hi[:, s, k * P:(k + 1) * P], w_lo[:, s, k * P:(k + 1) * P]
                dst = ps[:, bank, 0:w]
                mm(dst, hi, h_hi[:, k, a:a + w], start=(k == 0), stop=False)
                mm(dst, hi, h_lo[:, k, a:a + w], start=False, stop=False)
                last = mm(dst, lo, h_hi[:, k, a:a + w], start=False, stop=(k == KD - 1))
            last.then_inc(in_done, 1)

        def tile(ph, i, p, between=()):
            for n, (a, w) in enumerate(ph.chunks[p]):
                q = ph.first(p) + n
                chunk(ph, i, p, q, ph.banks[q], a, w)
                if n < len(between) and between[n]:
                    between[n]()

        eng.wait_ge(consts, 10)
        for n, (a, w) in enumerate(FULL):
            eng.wait_ge(sq_done, n + 1)
            for k in range(KD):
                last = mm(ps[:, 4 + n, 0:w], ones_d[:], sq_ch[:, k, 0:w], start=(k == 0), stop=(k == KD - 1))
            last.then_inc(stat_done, 1)
            if n >= 1:
                eng.wait_ge(h_ready, n)
                a0, w0 = FULL[n - 1]
                chunk(PH_DT, 0, 0, n - 1, n - 1, a0, w0)
        eng.wait_ge(h_ready, 3)
        chunk(PH_DT, 0, 0, 2, 2, *FULL[2])
        eng.wait_ge(in_evac, 3)
        eng.transpose(ps[0:META, bO, 0:HEADS], dt_cm[:, 0:META], ident[0:HEADS, 0:HEADS])
        for m in range(TOK):
            last = eng.transpose(ps[:, bO, HEADS * (m + 1):HEADS * (m + 2)], dt_cm[:, META + m * P:META + (m + 1) * P],
                                 ident[0:HEADS, 0:HEADS])
        last.then_inc(dtT_done, 1)

        for p in range(2):
            tile(PH_C0, 0, p)
        with eng.Fori(0, PH_XC.rounds) as i:
            for p in range(5):
                tile(PH_XC, i, p)
        for p in range(3):
            tile(PH_X3, 0, p)

        eng.wait_ge(dt_ready, 1)
        mm(ps[:, bX, 0:NDT], tri[:], sp[3][:], start=True, stop=True)
        mm(ps[:, bX, 256:256 + NDT], ones[:], sp[3][:], start=True, stop=True).then_inc(cum_done, 1)
        eng.wait_ge(ssm_silu, CREDIT + 12)
        for g in range(GROUPS):
            eng.transpose(ps[0:META, bO, P * g:P * (g + 1)], xbc[:, N_B + g, 0:META], ident[:])
        for t in range(GT):
            last = eng.transpose(ps[0:META, 3, P * t:P * (t + 1)], xbc[:, t, 0:META], ident[:])
        eng.wait_ge(cum_copied, 1)
        for m in range(TOK):
            last = eng.transpose(ps[0:HEADS, bS + m // 4, P * (m % 4):P * (m % 4 + 1)], dts[:, 1, m + 1, :], ident[:])
        last.then_inc(cumT_done, 1)
        eng.wait_ge(diff_done, 1)
        for t in range(GT):
            last = eng.transpose(ps[0:META, bX, P * t:P * (t + 1)], xbc[:, GT + t, 0:META], ident[:])
        last.then_inc(metaT_done, 1)
        eng.wait_ge(meta_ready, 1)
        eng.wait_ge(rows_ready, 1)
        for g in range(GROUPS):
            last = mm(ps[:, bS + g, :], b_cb[0:META, g, :], xdt0[:, HPG * g:HPG * (g + 1), :].rearrange("p h d -> p (h d)"),
                      start=True, stop=True)
        last.then_inc(scan_done, 1)

        with eng.Fori(0, PH_AS.rounds) as j:
            def turn(m, g):
                if g == 0:
                    eng.wait_ge(staged, 2 * m + 2)
                    eng.wait_ge(st_done, m * GROUPS + 1)
                    for b in range(GROUPS):
                        eng.transpose(ps[:, bS, P * b:P * (b + 1)], bc_st[:, b, :], ident[:])
                    for b in range(GROUPS):
                        last = mm(ps[:, bS, P * (2 + b):P * (3 + b)], bc_st[:, b, :], bc_st[:, 2 + b, :], start=True, stop=True)
                eng.wait_ge(xd_done, CREDIT + m * GROUPS + g)
                for t in range(GT):
                    last = eng.transpose(ps[:, bX, P * t:P * (t + 1)], xs_st[:, GT * g + t, :], ident[:])
                last.then_inc(turn_done, 1)

            def scan(m, g):
                eng.wait_ge(m_done, m * GROUPS + g + 1)
                eng.wait_ge(y_done, CREDIT + m * GROUPS + g)
                for h in range(HPG):
                    mm(ps[HD * (h % 2):HD * (h % 2 + 1), bY, P * (h // 2):P * (h // 2 + 1)], xd[g][:, h, :], e[g][:, h, :],
                       start=True, stop=True)
                if g == 0:
                    eng.wait_ge(bcb_done, m + 1)
                eng.wait_ge(st_done, m * GROUPS + g + 1)
                for t in range(GT):
                    mm(ps[:, bO, P * t:P * (t + 1)],
                       state[:, HPG * g + 2 * t:HPG * g + 2 * t + 2, :].rearrange("p h d -> p (h d)"),
                       bc_st[:, 2 + g, :], start=True, stop=True)
                mm(ps[:, bS, :], b_cb[:, g, :], xdd[g][:].rearrange("p h d -> p (h d)"),
                   start=True, stop=True).then_inc(scan_done, 1)

            m = j * 2
            tile(PH_AS, j, 0, [lambda: turn(m, 0), lambda: turn(m, 1), None])
            tile(PH_AS, j, 1, [lambda: scan(m, 0), lambda: scan(m, 1), lambda: turn(m + 1, 0)])
            tile(PH_AS, j, 2, [lambda: turn(m + 1, 1), None])
            tile(PH_AS, j, 3, [lambda: scan(m + 1, 0), lambda: scan(m + 1, 1)])

        eng.wait_ge(conf_done, CREDIT + N_C)
        eng.wait_ge(st_done, 2 * TOK + 1)
        eng.wait_ge(y_done, CREDIT + 2 * TOK)
        for h in range(2):
            for n in range(N_C):
                last = mm(ps[:, bX + h, :], ones_c[:], y_c[:, n, HALF * h:HALF * (h + 1)], start=(n == 0), stop=(n == N_C - 1))
        last.then_inc(cmean_done, 1)
        with eng.Fori(0, PH_Z.rounds) as j:
            for p in range(3):
                tile(PH_Z, j, p)
        eng.wait_ge(csq_done, N_C)
        for h in range(2):
            for n in range(N_C):
                last = mm(ps[:, bY + h, :], ones_c[:], csq[:, n, HALF * h:HALF * (h + 1)], start=(n == 0), stop=(n == N_C - 1))
        last.then_inc(cvar_done, 1)
        eng.wait_ge(sqs_done, CREDIT + N_B)
        for t in range(TOK):
            last = mm(ps[:, bX, t:t + 1], sqs[:, P * t:P * (t + 1)], ones_d[:, 0:1], start=True, stop=True)
        last.then_inc(bms_done, 1)

        eng.wait_ge(in_evac, N_CHUNKS)
        eng.wait_ge(bsd_done, 1)
        eng.wait_ge(csd_done, 1)
        with eng.Fori(0, 2) as h:
            for n in range(8):
                s = PH_OUT.slots[n]
                eng.wait_ge(wlo_done, PH_OUT.tile(h, n) + 1)
                for kk in range(2):
                    k = OUT_K[2 * n + kk]
                    opens = 2 * n + kk in (0, 8)
                    closes = 2 * n + kk in (7, 15)
                    eng.wait_ge(ylo_done, 2 * n + kk + 1)
                    for t in range(TOK):
                        if opens:
                            if n == 0:
                                eng.wait_ge(sum_done, CREDIT + h * (t + 1))
                            else:
                                eng.wait_ge(part_done, 8 * h + t + 1)
                        hi, lo = w_hi[:, s, HALF * kk:HALF * (kk + 1)], w_lo[:, s, HALF * kk:HALF * (kk + 1)]
                        yh = y_hi[:, k, P * t:P * (t + 1)]
                        mm(ps[:, t, :], yh, hi, start=opens, stop=False)
                        mm(ps[:, t, :], yh, lo, start=False, stop=False)
                        last = mm(ps[:, t, :], y_rest(k, P * t, P), hi, start=False, stop=closes)
                        if closes:
                            last.then_inc(pass_done, 1)
                        elif kk == 1 and t == TOK - 1:
                            last.then_inc(out_done, 1)

    @block.vector
    def _(eng):
        class Steps:

            def __init__(self):
                self.done, self.i, self.per, self.n = 0, None, 0, 0

            def enter(self, i, per):
                self.done, self.i, self.per, self.n = self.done + self.n, i, per, 0

            def leave(self, rounds):
                assert self.n == self.per, (self.n, self.per)
                self.done, self.i, self.n = self.done + rounds * self.per, None, 0

            def value(self):
                v = self.done + self.n
                return v if self.i is None else self.i * self.per + v

        steps = Steps()

        def step(ins):
            ins.then_inc(dve_step, 1)
            steps.n += 1

        def after():
            eng.wait_ge(dve_step, steps.value())

        def rest_w(slot, tile):
            eng.wait_ge(whi_done, tile + 1)
            eng.tensor_tensor(w_lo[:, slot, :], w_raw[:, slot, :], w_hi[:, slot, :].bitcast(F32), ALU.subtract).then_inc(wlo_done, 1)

        def rest_next(ph, i, p):
            rest_w(ph.slots[p + 1] if p + 1 < len(ph.slots) else 0, ph.tile(i, p + 1))

        for n, s in enumerate((y_done, xd_done, ssm_conv, conf_done, ya_done, ab_done, zb_done, sum_done)):
            eng.memset(credits[:, n:n + 1], 0.0).then_inc(s, 1)
        eng.wait_ge(prm_in, 16)
        for n, (a, w) in enumerate(FULL):
            if n == 1:
                rest_w(PH_DT.slots[0], 0)
            r = rs_ch[n % 2][:, 0:w]
            eng.wait_ge(sd_done, n + 1)
            step(eng.reciprocal(r, r))
            after()
            for k in range(KD):
                last = eng.scalar_tensor_tensor(x_ch[n % 2][:, k, 0:w], x_ch[n % 2][:, k, 0:w], prm_col("pre_g", k), r,
                                                ALU.mult, ALU.mult)
            last.then_inc(hn_done, 1)
            eng.wait_ge(hhi_done, n + 1)
            eng.tensor_tensor(h_lo[:, :, a:a + w], x_ch[n % 2][:, :, 0:w], h_hi[:, :, a:a + w].bitcast(F32),
                              ALU.subtract).then_inc(h_ready, 1)
        rest_w(0, 1)
        eng.wait_ge(h_ready, 3)
        for b in range(2):
            step(eng.memset(xr[b][:, 0:KS - 1], 0.0))
            step(eng.memset(uc2[:, UC[b] - UC[0]:UC[b] - UC[0] + PAD_C], 0.0))
        eng.wait_ge(dtT_done, 1)
        eng.wait_ge(consts, 10)
        step(eng.tensor_copy(sp[0][0:META, 0:HEADS], ps[0:META, bO, 0:HEADS]))
        eng.tensor_copy(sp[0][:, HEADS:NDT], ps[:, bO, HEADS:NDT]).then_inc(dt_abs, 1)
        eng.wait_ge(dt_abs, 1)
        after()
        step(eng.tensor_scalar(sp[5][:], sp[0][:], 0.0, None, ALU.max))
        eng.wait_ge(dt_act, 1)
        step(eng.tensor_scalar(sp[1][:], sp[2][:], 2.0, None, ALU.add))
        after()
        step(eng.reciprocal(sp[1][:], sp[1][:]))
        after()
        step(eng.tensor_tensor(sp[1][:], sp[1][:], sp[2][:], ALU.mult))
        after()
        step(eng.tensor_tensor(sp[2][:], sp[1][:], sp[1][:], ALU.mult))
        after()
        step(eng.tensor_scalar(sp[3][:], sp[2][:], 1.0 / 15, None, ALU.mult))
        for c in (13, 11, 9, 7, 5, 3):
            after()
            step(eng.scalar_tensor_tensor(sp[3][:], sp[3][:], 1.0 / c, sp[2][:], ALU.add, ALU.mult))
        after()
        step(eng.scalar_tensor_tensor(sp[3][:], sp[3][:], 1.0, sp[1][:], ALU.add, ALU.mult))
        after()
        dt_all = dts[:, 0].rearrange("p c h -> p (c h)")
        step(eng.scalar_tensor_tensor(dt_all, sp[3][:], 2.0, sp[5][:], ALU.mult, ALU.add))
        after()
        eng.wait_ge(dt_act, 2)
        eng.scalar_tensor_tensor(sp[3][:].rearrange("p (c h) -> p c h", h=HEADS), dts[:, 0], -1.0,
                                 a_neg[:].unsqueeze(1).broadcast_to([P, TOK + 1, HEADS]), ALU.mult, ALU.mult).then_inc(dt_ready, 1)

        def conf_start(r):
            step(eng.tensor_copy(cur_conf[:], prm[:, bass.ds(r * (KC + 1) + PRM["conf_w"][0], KC + 1)]))

        def conf_taps(r, k0, k1):
            dst = y_c[:, bass.ds(r, 1), :].rearrange("p o l -> p (o l)")
            buf = (r % 2) * (UC[1] - UC[0])
            for k in range(k0, k1):
                src = uc2[:, bass.ds(buf + k, SEQ)]
                after()
                if k == 0:
                    step(eng.tensor_scalar(dst, src, cur_conf[:, 0:1], cur_conf[:, KC:KC + 1], ALU.mult, ALU.add))
                elif k < KC - 1:
                    step(eng.scalar_tensor_tensor(dst, src, cur_conf[:, k:k + 1], dst, ALU.mult, ALU.add))
                else:
                    eng.scalar_tensor_tensor(dst, src, cur_conf[:, k:k + 1], dst, ALU.mult, ALU.add).then_inc(conf_done, 1)

        def ssm_taps(ph, i, r, n):
            step(eng.tensor_copy(cur_ssm[:, 0:KS + 1], prm[:, bass.ds(r * (3 * (KS + 1)) + (PRM["ssm_w"][0] + n * (KS + 1)), KS + 1)]))
            eng.wait_ge(in_evac, ph.chunk(i, 3 * n + 3))
            eng.wait_ge(ssm_silu, CREDIT + 3 * r + (1 if n == 2 else 0))
            src, dst = xr[n % 2], acc[n % 2][:]
            after()
            step(eng.tensor_scalar(dst, src[:, 0:L], cur_ssm[:, 0:1], cur_ssm[:, KS:KS + 1], ALU.mult, ALU.add))
            for k in range(1, KS - 1):
                after()
                step(eng.scalar_tensor_tensor(dst, src[:, k:k + L], cur_ssm[:, k:k + 1], dst, ALU.mult, ALU.add))
            after()
            eng.scalar_tensor_tensor(dst, src[:, KS - 1:KS - 1 + L], cur_ssm[:, KS - 1:KS], dst, ALU.mult, ALU.add).then_inc(ssm_conv, 1)

        def gated(ph, i, p, n, buf):
            eng.wait_ge(in_evac, ph.chunk(i, ph.first(p) + 3))
            u = uc2[:, bass.ds(buf + PAD_C, L)]
            eng.tensor_tensor(u, u, sg[:], ALU.mult).then_inc(u_done, 1)
            eng.wait_ge(u_done, n + 1)

        rest_next(PH_C0, 0, 0)
        rest_next(PH_C0, 0, 1)
        gated(PH_C0, 0, 1, 0, 0)
        XC_STEPS = 1 + (KC - 1) + 3 * KS
        with eng.Fori(0, PH_XC.rounds) as i:
            steps.enter(i, XC_STEPS)
            ph = PH_XC
            rest_next(ph, i, 0)
            conf_start(i)
            conf_taps(i, 0, 8)
            rest_next(ph, i, 1)
            ssm_taps(ph, i, i, 0)
            conf_taps(i, 8, 15)
            rest_next(ph, i, 2)
            ssm_taps(ph, i, i, 1)
            conf_taps(i, 15, 22)
            rest_next(ph, i, 3)
            ssm_taps(ph, i, i, 2)
            conf_taps(i, 22, KC)
            rest_next(ph, i, 4)
            gated(ph, i, 4, i + 1, ((i + 1) % 2) * (UC[1] - UC[0]))
        steps.leave(PH_XC.rounds)
        ph = PH_X3
        rest_next(ph, 0, 0)
        conf_start(3)
        conf_taps(3, 0, 8)
        rest_next(ph, 0, 1)
        ssm_taps(ph, 0, 3, 0)
        conf_taps(3, 8, 15)
        rest_next(ph, 0, 2)
        ssm_taps(ph, 0, 3, 1)
        conf_taps(3, 15, 19)
        ssm_taps(ph, 0, 3, 2)

        eng.wait_ge(cum_done, 1)
        flat = [dts[:, n].rearrange("p c h -> p (c h)") for n in range(4)]
        eng.tensor_copy(flat[1], ps[:, bX, 0:NDT]).then_inc(cum_copied, 1)
        step(eng.tensor_copy(flat[3], ps[:, bX, 256:256 + NDT]))
        eng.wait_ge(cum_copied, 1)
        after()
        eng.tensor_tensor(flat[2], flat[3], flat[1], ALU.subtract).then_inc(diff_done, 1)
        eng.wait_ge(cumT_done, 1)
        eng.tensor_copy(acum_rows[:], ps[0:HEADS, bS:bS + 2, :].rearrange("p b c -> p (b c)")).then_inc(rows_ready, 1)
        eng.wait_ge(dec_done, 2)
        step(eng.tensor_tensor(dt_dec[0:META, :], dts[0:META, 0, 0, :], dts[0:META, 2, 0, :], ALU.mult))
        eng.wait_ge(metaT_done, 1)
        step(eng.tensor_copy(b_cb[0:META, 0:2, :].rearrange("p g n -> p (g n)"), ps[0:META, bO, 0:2 * P]))
        after()
        for g, b in enumerate((3, bX)):
            ins = eng.tensor_tensor(xdt0[:, HPG * g:HPG * (g + 1), :], ps[0:META, b, :].rearrange("p (h d) -> p h d", d=HD),
                                    dt_dec[0:META, HPG * g:HPG * (g + 1)].unsqueeze(2).broadcast_to([META, HPG, HD]), ALU.mult)
            if g:
                ins.then_inc(meta_ready, 1)
            else:
                step(ins)
        eng.wait_ge(scan_done, CREDIT)
        eng.tensor_copy(state[:].rearrange("p h d -> p (h d)"), banks(bS, 2)).then_inc(st_done, 1)
        conf_taps(3, 19, KC)

        AS_STEPS = 2 * (1 + GROUPS * (1 + 3)) + 1 + (KA - 1)
        with eng.Fori(0, PH_AS.rounds) as j:
            steps.enter(j, AS_STEPS)
            ph = PH_AS
            m = j * 2

            def segs(m, g):
                eng.wait_ge(e_in[g], m * 16 + 16)
                for h in range(HPG):
                    ins = eng.tensor_scalar(e[g][:, h, :], e[g][:, h, :], cur_dt[:, 1, HPG * g + h:HPG * g + h + 1], 0.0,
                                            ALU.subtract, ALU.min)
                ins.then_inc(seg_done, 1)

            def prepare(m, g):
                if g == 0:
                    eng.wait_ge(turn_done, m * GROUPS + 1)
                    eng.tensor_tensor(b_cb[:], ps[:, bS, :].rearrange("p (a c) -> p a c", a=4), mask4[:], ALU.mult).then_inc(bcb_done, 1)
                eng.wait_ge(turn_done, m * GROUPS + g + 1)
                hs = slice(HPG * g, HPG * (g + 1))
                eng.tensor_tensor(xd[g][:], ps[:, bX, :].rearrange("p (h d) -> p h d", d=HD),
                                  cur_dt[:, 0, hs].unsqueeze(2).broadcast_to([P, HPG, HD]), ALU.mult).then_inc(xd_done, 1)
                eng.wait_ge(xd_done, CREDIT + m * GROUPS + g + 1)
                step(eng.tensor_tensor(xdd[g][:], xd[g][:], cur_dt[:, 2, hs].unsqueeze(2).broadcast_to([P, HPG, HD]), ALU.mult))
                eng.wait_ge(exp_done, m * GROUPS + g + 1)
                eng.wait_ge(bcb_done, m + 1)
                eng.tensor_tensor(e[g][:], e[g][:], b_cb[:, 2 + g, :].unsqueeze(1).broadcast_to([P, HPG, P]), ALU.mult).then_inc(m_done, 1)

            def current(m):
                eng.wait_ge(st_done, m * GROUPS + 1)
                step(eng.tensor_copy(cur_dt[:], dts[:, :, bass.ds(m + 1, 1), :].rearrange("p a o h -> p a (o h)")))
                after()

            def finish(m, g):
                eng.wait_ge(scan_done, CREDIT + m * GROUPS + g + 1)
                if g == 0:
                    eng.wait_ge(ea_exp, m + 1)
                step(eng.tensor_tensor(ytmp[:], ps[:, bO, :].rearrange("p (t l) -> p t l", t=GT), ea[:, GT * g:GT * (g + 1), :], ALU.mult))
                st = state[:, HPG * g:HPG * (g + 1), :]
                step(eng.tensor_tensor(st, st, cur_dt[:, 3, HPG * g:HPG * (g + 1)].unsqueeze(2).broadcast_to([P, HPG, HD]), ALU.mult))
                after()
                step(eng.tensor_tensor(ytmp[:], ytmp[:], ps[:, bY, :].rearrange("p (t l) -> p t l", t=GT), ALU.add))
                eng.tensor_tensor(st, st, ps[:, bS, :].rearrange("p (h d) -> p h d", d=HD), ALU.add).then_inc(st_done, 1)
                after()
                for t in range(GT):
                    dst = xbc[:, GT * g + t, bass.ds(m * P + META, P)]
                    ins = eng.scalar_tensor_tensor(dst, xs_st[:, GT * g + t, :], prm_col("d_skip", GT * g + t), ytmp[:, t, :],
                                                   ALU.mult, ALU.add)
                ins.then_inc(y_done, 1)

            current(m)
            segs(m, 0)
            segs(m, 1)
            rest_next(ph, j, 0)
            prepare(m, 0)
            prepare(m, 1)
            rest_next(ph, j, 1)
            finish(m, 0)
            finish(m, 1)
            current(m + 1)
            segs(m + 1, 0)
            segs(m + 1, 1)
            rest_next(ph, j, 2)
            step(eng.tensor_copy(cur_a[:, 0:KA], prm[:, bass.ds(j * KA + PRM["conv_a"][0], KA)]))
            eng.wait_ge(in_evac, ph.chunk(j, 6))
            s = META - PAD_A
            eng.tensor_tensor(t1[:, 0:PAD_A + SEQ], t1[:, 0:PAD_A + SEQ], t2[:, s:L], ALU.mult).then_inc(au_done, 1)
            prepare(m + 1, 0)
            prepare(m + 1, 1)
            ya = y_a[:, bass.ds(j, 1), :].rearrange("p o l -> p (o l)")
            eng.wait_ge(au_done, j + 1)
            after()
            step(eng.tensor_scalar(ya, t1[:, 0:SEQ], cur_a[:, 0:1], None, ALU.mult))
            after()
            step(eng.scalar_tensor_tensor(ya, t1[:, 1:1 + SEQ], cur_a[:, 1:2], ya, ALU.mult, ALU.add))
            after()
            eng.scalar_tensor_tensor(ya, t1[:, 2:2 + SEQ], cur_a[:, 2:3], ya, ALU.mult, ALU.add).then_inc(aconv_done, 1)
            rest_next(ph, j, 3)
            eng.wait_ge(in_evac, ph.chunk(j, 8))
            eng.wait_ge(aconv_done, j + 1)
            eng.tensor_tensor(ya, ya, t2[:, META:L], ALU.mult).then_inc(ab_done, 1)
            finish(m + 1, 0)
            finish(m + 1, 1)
            eng.wait_ge(in_evac, ph.chunk(j, 10))
            eng.wait_ge(ab_done, CREDIT + j + 1)
            eng.tensor_tensor(ya, ya, t1[:, 0:SEQ], ALU.mult).then_inc(ya_done, 1)
        steps.leave(PH_AS.rounds)

        eng.wait_ge(cmean_done, 1)
        for n in range(N_C):
            eng.tensor_tensor(y_c[:, n, :], y_c[:, n, :], banks(bX, 2), ALU.subtract).then_inc(cmid_done, 1)
        eng.memset(sqs[:], 0.0).then_inc(sqs_done, 1)
        with eng.Fori(0, PH_Z.rounds) as j:
            steps.enter(j, 2)
            ph = PH_Z
            for p in range(3):
                rest_next(ph, j, p)
                if p < 2:
                    eng.wait_ge(in_evac, ph.chunk(j, 2 * p + 2))
                    yb = xbc[:, bass.ds(2 * j + p, 1), META:L].rearrange("p o l -> p (o l)")
                    eng.tensor_tensor(yb, yb, zt[p][:], ALU.mult).then_inc(zb_done, 1)
                    eng.wait_ge(zb_done, CREDIT + 2 * j + p + 1)
                    eng.wait_ge(sqs_done, CREDIT + 2 * j + p)
                    step(eng.tensor_tensor(sqb[:], yb, yb, ALU.mult))
                    after()
                    eng.tensor_tensor(sqs[:], sqs[:], sqb[:], ALU.add).then_inc(sqs_done, 1)
        steps.leave(PH_Z.rounds)
        eng.wait_ge(bsd_done, 1)
        eng.reciprocal(r_b[:], r_b[:]).then_inc(rb_done, 1)

        def rest(n):
            k = OUT_K[n]
            eng.wait_ge(yhi_done, n + 1)
            eng.scalar_tensor_tensor(y_rest(k), y_f32(k), prm_col("gain", k), y_hi[:, k, :].bitcast(F32),
                                     ALU.mult, ALU.subtract).then_inc(ylo_done, 1)

        def out_w(n):
            rest_w(n % 2, PH_OUT.tile0 + n)

        for n in range(2):
            rest(n)
        eng.wait_ge(csd_done, 1)
        step(eng.reciprocal(c_rs[:], c_rs[:]))
        for n in range(2, 8):
            rest(n)
        after()
        for n in range(N_C):
            eng.tensor_tensor(y_c[:, n, :], y_c[:, n, :], c_rs[:], ALU.mult).then_inc(cnorm_done, 1)
        out_w(1)
        for n in range(8, 12):
            rest(n)
        out_w(2)
        for n in range(N_C):
            eng.wait_ge(csilu_done, n + 1)
            eng.tensor_tensor(y_c[:, n, :], y_c[:, n, :], z_c[:, n, :], ALU.mult).then_inc(yc_done, 1)
            rest(12 + n)
        for h in range(2):
            for n in range(3 if h == 0 else 9, 9 + 7 * h):
                out_w(n)
            for t in range(TOK):
                eng.wait_ge(pass_done, 16 * h + 8 + t + 1)
                eng.wait_ge(part_done, 8 * h + t + 1)
                eng.tensor_tensor(ob[:, t, HALF * h:HALF * (h + 1)], ps[:, t, :], part[:, t, :], ALU.add).then_inc(sum_done, 1)
        eng.wait_ge(pg_in, 16)
        for t in range(TOK):
            r = r_out[:, t:t + 1]
            eng.wait_ge(osd_done, t + 1)
            step(eng.reciprocal(r, r))
            after()
            step(eng.scalar_tensor_tensor(ob[:, t, :], ob[:, t, :], r, pg[:], ALU.mult, ALU.mult))
            eng.wait_ge(xtm_in[t % 2], 16 * (t // 2 + 1))
            after()
            eng.tensor_tensor(x_tm[t % 2][:], ob[:, t, :], x_tm[t % 2][:], ALU.add).then_inc(fin_done, 1)

    ctx.close()


def kernel(**inputs):
    import numpy as np
    import concourse.bacc as bacc
    from concourse import mybir as mb
    from concourse.bass_utils import run_bass_kernel_spmd

    f = {k: np.asarray(v) for k, v in inputs.items()}
    x = np.ascontiguousarray(f["x"])
    tokens = np.concatenate([f["meta"], x[0]], axis=0)
    x_cm = np.ascontiguousarray(tokens.T.reshape(KD, P, L).transpose(1, 0, 2))

    w_in = f["w_in"][0]
    a_b, a_c, a_x, a_z, b_z, b_x, _, _, dt, c_a, c_g, c_z = (
        0, 512, 1024, 1536, 2048, 3072, 4096, 4352, 4608, 4624, 5136, 5648)
    cols = [dt, c_g, c_a]
    for i in range(4):
        cols += [b_x + P * (3 * i + n) for n in range(3)]
        if i < 3:
            cols += [c_g + P * (i + 1), c_a + P * (i + 1)]
    for j in range(4):
        cols += [a + P * j for a in (a_c, a_x, a_b, a_z)]
    for j in range(4):
        cols += [b_z + P * (2 * j), b_z + P * (2 * j + 1), c_z + P * j]
    tiles = [w_in[:, c:c + P].reshape(KD, P, P).transpose(1, 0, 2).reshape(P, KD * P) for c in cols]
    w_out = f["w_out"][0]
    for h in range(2):
        for n in range(8):
            ks = OUT_K[2 * n:2 * n + 2]
            tiles.append(np.concatenate([w_out[P * k:P * (k + 1), HALF * h:HALF * (h + 1)] for k in ks], axis=1))
    w_tiles = np.ascontiguousarray(np.stack(tiles))

    def chan(a):
        a = np.asarray(a)
        t = a.shape[-1] // P
        return a.reshape(-1, t, P).transpose(2, 1, 0).reshape(P, -1)

    params = np.zeros((P, N_PRM), np.float32)

    def put(name, value):
        at, n = PRM[name]
        params[:, at:at + n] = value

    put("pre_g", chan(f["pre_g"][0]))
    put("ssm_w", chan(np.concatenate([f["ssm_conv_w"][0], f["ssm_conv_b"]])))
    put("conf_w", chan(np.concatenate([f["conf_conv_w"][0], f["conf_conv_b"]])))
    put("ln_g", chan(f["conf_ln_g"][0]))
    put("ln_b", chan(f["conf_ln_b"][0]))
    put("gain", 1.0)
    at = PRM["gain"][0] + N_A
    params[:, at:at + N_B] = chan(f["ssm_norm_g"][0])
    put("d_skip", np.repeat(f["d_skip"][0], HD).reshape(N_B, P).T)
    put("a_log", np.broadcast_to(f["a_log"][0], (P, HEADS)))
    put("conv_a", chan(f["conv_a_w"][0]))
    params[0:HEADS, PRM["dt_bias"][0]] = f["dt_bias"][0]
    put("norm_eps", NORM_EPS)
    put("ln_eps", LN_EPS)

    arrays = {"xT_dram": x_cm, "x_dram": x, "w_dram": w_tiles, "params_dram": params,
              "post_g_dram": np.ascontiguousarray(f["post_g"][0])}
    nc = bacc.Bacc("TRN2", target_bir_lowering=False, num_devices=1, dynamic_dma_scratch_size=1024)
    aps = [nc.dram_tensor(k, v.shape, mb.dt.from_np(v.dtype), kind="ExternalInput").ap() for k, v in arrays.items()]
    acum = nc.dram_tensor("acum_dram", (HEADS, SEQ), mb.dt.float32, kind="Internal").ap()
    out = nc.dram_tensor("out_dram", x.shape, mb.dt.from_np(x.dtype), kind="ExternalOutput").ap()
    hybrid_mixer_kernel(nc, *aps, acum, out)
    r = run_bass_kernel_spmd(nc, [arrays], core_ids=[0])
    return r.results[0]["out_dram"]
```

```python
from contextlib import ExitStack

import concourse.bass as bass
from concourse import mybir

ALU = mybir.AluOpType
ACT = mybir.ActivationFunctionType
F32 = mybir.dt.float32
F32R = mybir.dt.float32r

P = 128
D = 1024
META = 16
SEQ = 1024
L = META + SEQ
KD = D // P
TOK = SEQ // P
D_A = D_C = 512
D_B = 1024
N_A, N_B, N_C = D_A // P, D_B // P, D_C // P
N_Y = N_A + N_B + N_C
HEADS, HD = 16, 64
GROUPS = 2
HPG = HEADS // GROUPS
GT = N_B // GROUPS
KA, KS, KC = 3, 4, 31
HALF = 512
NORM_EPS, LN_EPS = 1e-6, 1e-5

FULL = [(0, 348), (348, 346), (694, 346)]
REAL = [(META, HALF), (META + HALF, HALF)]


CREDIT = 1


class Phase:

    def __init__(self, before, rounds, slots, chunks, banks=None):
        self.rounds, self.slots, self.chunks = rounds, slots, chunks
        self.tile0 = before.tile0 + before.rounds * len(before.slots) if before else 0
        self.chunk0 = before.chunk0 + before.rounds * before.per_round if before else 0
        self.loads0 = [before.loads0[s] + before.rounds * before.slots.count(s) if before else 0 for s in range(3)]
        self.per_round = sum(map(len, chunks))
        self.banks = banks or [q % 3 for q in range(self.per_round)]

    def tile(self, i, p):
        return self.tile0 + i * len(self.slots) + p

    def chunk(self, i, q):
        return self.chunk0 + i * self.per_round + q

    def first(self, p):
        return sum(map(len, self.chunks[:p]))

    def loads(self, i, p):
        s = self.slots[p]
        return self.loads0[s] + i * self.slots.count(s) + self.slots[:p + 1].count(s)


PH_FIRST = Phase(None, 1, [0, 1, 2], [FULL] * 3)
PH_XC = Phase(PH_FIRST, 3, [0, 1, 2, 0, 1], [FULL] * 5)
PH_X3 = Phase(PH_XC, 1, [0, 1, 2], [FULL] * 3)
PH_AS = Phase(PH_X3, 4, [0, 1, 0, 1], [FULL, FULL, REAL, REAL], [0, 1, 2, 0, 1, 2, 0, 1, 2, 3])
PH_Z0 = Phase(PH_AS, 1, [0, 1, 2], [REAL] * 3)
PH_Z = Phase(PH_Z0, 3, [0, 1, 2], [REAL] * 3)
PH_OUT = Phase(PH_Z, 2, [0, 1, 2, 0, 1, 0, 2, 1], [[]] * 8)
BY_TOKEN = (6, 7)
N_TILES = PH_OUT.tile(2, 0)
N_CHUNKS = PH_OUT.chunk0
OUT_K = [4, 5, 6, 7, 8, 9, 10, 11, 0, 1, 2, 3, 12, 13, 14, 15]


PRM = {}
for _name, _n in [("pre_g", KD), ("ssm_w", 12 * (KS + 1)), ("conf_w", 4 * (KC + 1)),
                  ("ln_g", 4), ("ln_b", 4), ("gain", N_Y), ("d_skip", N_B), ("a_log", HEADS),
                  ("conv_a", 4 * KA), ("dt_bias", 1), ("norm_eps", 1), ("ln_eps", 1)]:
    PRM[_name] = (sum(n for _, n in PRM.values()), _n)
N_PRM = sum(n for _, n in PRM.values())


def hybrid_mixer_kernel(nc, xT, x, w_tiles, params, post_g, acum_dram, out):
    ctx = ExitStack()

    BASE = 288

    def at(name, offset, shape, dtype=F32):
        return nc.alloc_sbuf_tensor_at(name, shape, dtype, offset=4 * (BASE + offset))

    h_hi = at("h_hi", 0, [P, KD, L], F32R)
    h_lo = at("h_lo", KD * L, [P, KD, L], F32R)
    y_hi = at("y_hi", 0, [P, N_Y, SEQ], F32R)
    o = 2 * KD * L
    PAD_C = KC - 1 - META
    U_STRIDE = (PAD_C + L + 7) // 8 * 8
    U_BEFORE = 3 * U_STRIDE - 3 * SEQ
    U = o
    YA = U + U_BEFORE
    XBC = U + 4 * U_STRIDE
    YC = XBC + 12 * L
    u4 = at("u4", U, [P, 4 * U_STRIDE])
    y_a = at("y_a", YA, [P, N_A, SEQ])
    xbc = at("xbc", XBC, [P, 12, L])
    y_c = at("y_c", YC, [P, N_C, SEQ])
    lo_a = at("lo_a", YA, [P, N_A, SEQ], F32R)
    lo_b = at("lo_b", XBC, [P, N_B, L], F32R)
    lo_c = at("lo_c", YC, [P, N_C, SEQ], F32R)
    z_c = at("z_c", XBC + N_B * L, [P, N_C, SEQ])
    part = at("part", XBC + N_B * L, [P, TOK, HALF])
    o = YC + N_C * SEQ
    w_raw = at("w_raw", o, [P, 3, 1024])
    w_lo = at("w_lo", o, [P, 3, 1024], F32R)
    w_hi = at("w_hi", o + 3072, [P, 3, 1024], F32R)
    o += 6144
    small = {}
    for name, shape in [("ones_d", [P, P]), ("ones_c", [P, P]), ("ones", [P, P]), ("tri", [P, P]), ("ident", [P, P]),
                        ("mask4", [P, 4, P]), ("prm", [P, N_PRM]), ("cur_ssm", [P, 3 * (KS + 1)]), ("cur_conf", [P, KC + 1]),
                        ("cur_a", [P, 4]), ("dts", [P, 4, TOK + 1, HEADS]), ("cur_dt", [P, 4, HEADS]),
                        ("a_neg", [P, HEADS]), ("dt_dec", [P, HEADS]), ("r_b", [P, TOK]), ("ssq", [P, 2 * TOK]),
                        ("ssq0", [P, TOK]), ("r_out", [P, TOK]), ("r_in", [P, 9]), ("r_c", [P, TOK]),
                        ("credits", [P, 16])]:
        n = 1
        for s in shape[1:]:
            n *= s
        small[name] = at(name, o, shape)
        o += (n + 7) // 8 * 8
    ones_d, ones_c, ones, tri, ident, mask4 = (small[n] for n in ("ones_d", "ones_c", "ones", "tri", "ident", "mask4"))
    prm, cur_ssm, cur_conf, cur_a = (small[n] for n in ("prm", "cur_ssm", "cur_conf", "cur_a"))
    dts, cur_dt, a_neg, dt_dec, r_b, ssq, ssq0, r_out, r_in, r_c, credits = (
        small[n] for n in ("dts", "cur_dt", "a_neg", "dt_dec", "r_b", "ssq", "ssq0", "r_out", "r_in", "r_c", "credits"))
    W = o

    x_in = at("x_in", KD * L, [P, KD, L])
    sq_in = at("sq_in", 0, [P, KD, L])
    diag_in = at("diag_in", W + 8384, [P, 3, P])
    dt_cm = at("dt_cm", W + 9088, [HEADS, L])
    acum_rows = at("acum_rows", W + 8368, [HEADS, SEQ])
    NDT = (TOK + 1) * HEADS
    sp = [at(f"sp{n}", W + 10144 + NDT * n, [P, NDT]) for n in range(6)]
    xr = [at(f"xr{b}", W + 1048 * b, [P, KS - 1 + L]) for b in range(3)]
    acc = [at(f"acc{b}", W + 3144 + 1040 * b, [P, L]) for b in range(3)]
    sg = at("sg", W + 6272, [P, L])
    odd = at("odd", W + 7312, [P, SEQ])
    b_meta = at("b_meta", W + 6272, [META, GROUPS, P])
    xdt0 = at("xdt0", W + 7312, [META, HEADS, HD])
    e = [at(f"e{g}", W + 1024 * g, [P, HPG, P]) for g in range(2)]
    xs_st = at("xs_st", W + 2048, [P, N_B, P])
    bc_st = at("bc_st", W + 3072, [P, 4, P])
    b_cb = at("b_cb", W + 3584, [P, 4, P])
    ea = at("ea", W + 4096, [P, N_B, P])
    xd = [at("xd0", W + 5120, [P, HPG, HD]), at("xd1", W + 8368, [P, HPG, HD])]
    xdd = [at("xdd0", W + 5632, [P, HPG, HD]), at("xdd1", W + 8880, [P, HPG, HD])]
    PAD_A = KA - 1
    t1 = at("t1", W + 6272, [P, PAD_A + SEQ + 8])
    t2 = at("t2", W + 7320, [P, L])
    ytmp = at("ytmp", W + 9392, [P, GT, P])
    state = at("state", W + 9904, [P, HEADS, HD])
    zt = [at(f"zt{b}", W + 1024 * b, [P, SEQ]) for b in range(2)]
    sqb = at("sqb", W + 2048, [P, SEQ])
    sqs = at("sqs", W + 3072, [P, SEQ])
    csq = at("csq", W + 4096, [P, N_C, SEQ])
    diag_c = at("diag_c", W + 8192, [P, TOK, P])
    ob = at("ob", W, [P, TOK, D])
    branches = [at(f"branches{b}", W + 8192 + 512 * b, [P, HALF]) for b in range(2)]
    junk = at("junk", W + 9216, [P, HALF])
    pg = at("pg", W + 9728, [P, D])
    x_tm = at("x_tm", N_A * SEQ, [P, TOK, D])

    ps = ctx.enter_context(nc.psum_tensor("ps", [P, 8, HALF], F32))
    bB, bX, bS, bY, bO = 3, 4, 5, 6, 7

    def prm_col(name, j=0, n=1):
        return prm[:, PRM[name][0] + j:PRM[name][0] + j + n]

    def sem(name):
        return ctx.enter_context(nc.semaphore(name))

    prm_in, w_in = sem("prm_in"), [sem(f"w_in{s}") for s in range(3)]
    xch_in = [sem(f"xch_in{n}") for n in range(3)]
    consts = sem("consts")
    sq_done, sq_summed, stat_done, sd_done, diag_done, rbc_done, hn_done, hhi_done, h_ready = map(
        sem, ("sq_done", "sq_summed", "stat_done", "sd_done", "diag_done", "rbc_done", "hn_done", "hhi_done", "h_ready"))
    whi_done, wlo_done = sem("whi_done"), sem("wlo_done")
    in_done, in_evac = sem("in_done"), sem("in_evac")
    dve_step = sem("dve_step")
    dtT_done, dt_abs, dt_act, sp_abs, dt_den, dt_ready = map(
        sem, ("dtT_done", "dt_abs", "dt_act", "sp_abs", "dt_den", "dt_ready"))
    cum_done, cum_copied, diff_done, dec_done, cumT_done, rows_ready, rows_saved = map(
        sem, ("cum_done", "cum_copied", "diff_done", "dec_done", "cumT_done", "rows_ready", "rows_saved"))
    meta_ready = sem("meta_ready")
    ssm_conv, ssm_silu, u_done, conf_done = map(sem, ("ssm_conv", "ssm_silu", "u_done", "conf_done"))
    e_in, ea_in = [sem("e_in0"), sem("e_in1")], sem("ea_in")
    staged, seg_done, exp_done, ea_exp = map(sem, ("staged", "seg_done", "exp_done", "ea_exp"))
    turn_done, bcb_done, xd_done, m_done, scan_done, y_done, st_done = map(
        sem, ("turn_done", "bcb_done", "xd_done", "m_done", "scan_done", "y_done", "st_done"))
    au_done, aconv_done, ab_done, ya_done = map(sem, ("au_done", "aconv_done", "ab_done", "ya_done"))
    cmean_done, cmid_done, csq_done, cvar_done, csd_done, cdiag_done, crbc_done, cnorm_done, csilu_done, yc_done = map(
        sem, ("cmean_done", "cmid_done", "csq_done", "cvar_done", "csd_done", "cdiag_done", "crbc_done",
              "cnorm_done", "csilu_done", "yc_done"))
    zb_done, sqs_done, bms_done, bsd_done, rb_done = map(sem, ("zb_done", "sqs_done", "bms_done", "bsd_done", "rb_done"))
    yhi_done, ylo_done, out_done, pass_done, part_done, sum_done = map(
        sem, ("yhi_done", "ylo_done", "out_done", "pass_done", "part_done", "sum_done"))
    ssq_done, ssq0_done, osd_done, x_tm_in, pg_in, scaled_done, fin_done, saved = (
        sem("ssq_done"), sem("ssq0_done"), sem("osd_done"), [sem("x_tm_in0"), sem("x_tm_in1")], sem("pg_in"),
        sem("scaled_done"), sem("fin_done"), [sem("saved0"), sem("saved1")])

    def y_f32(k, a=0, n=SEQ):
        if k < N_A:
            return y_a[:, k, a:a + n]
        if k < N_A + N_B:
            return xbc[:, k - N_A, META + a:META + a + n]
        return y_c[:, k - N_A - N_B, a:a + n]

    def y_rest(k, a=0, n=SEQ):
        if k < N_A:
            return lo_a[:, k, a:a + n]
        if k < N_A + N_B:
            return lo_b[:, k - N_A, META + a:META + a + n]
        return lo_c[:, k - N_A - N_B, a:a + n]

    def stat_tokens(a, w):
        return [a, a + P, a + w - P]

    def banks(b, n):
        return ps[:, b:b + n, :].rearrange("p b c -> p (b c)")

    block = ctx.enter_context(nc.Block())

    @block.sync
    def _(eng):
        def load_w(slot, tile):
            src = w_tiles[tile] if isinstance(tile, int) else w_tiles[bass.ds(tile, 1)].rearrange("o p n -> p (o n)")
            eng.dma_start(w_raw[:, slot, :], src).then_inc(w_in[slot], 16)

        for n, (a, w) in enumerate(FULL):
            eng.dma_start(x_in[:, :, a:a + w], xT[:, :, a:a + w]).then_inc(xch_in[n], 16)
            if n == 0:
                eng.dma_start(prm[:], params).then_inc(prm_in, 16)
            load_w(PH_FIRST.slots[n], n)

        def next_w(ph, i, p):
            eng.wait_ge(in_done, ph.chunk(i, ph.first(p)))
            last = p + 1 == len(ph.slots)
            load_w(0 if last else ph.slots[p + 1], ph.tile(i, p + 1))

        eng.wait_ge(in_done, 7)
        load_w(0, PH_XC.tile0)
        with eng.Fori(0, PH_XC.rounds) as i:
            for p in range(5):
                next_w(PH_XC, i, p)
        for p in range(3):
            next_w(PH_X3, 0, p)
        eng.wait_ge(rows_ready, 1)
        eng.dma_start(acum_dram, acum_rows[:]).then_inc(rows_saved, 16)
        eng.wait_ge(rows_saved, 16)
        eng.wait_ge(scan_done, CREDIT)

        def load_rows(m):
            for g in range(GROUPS):
                eng.wait_ge(scan_done, CREDIT + m * GROUPS)
                src = acum_dram[HPG * g:HPG * (g + 1), bass.ds(m * P, P)]
                eng.dma_start(e[g][:], src.partition_broadcast(P)).then_inc(e_in[g], 16)

        def load_rows_by_channel(m):
            eng.wait_ge(ssm_silu, CREDIT + 12)
            eng.wait_ge(y_done, CREDIT + m * GROUPS)
            for h in range(2):
                src = acum_dram[h:HEADS:2, bass.ds(m * P, P)]
                eng.dma_start(ea[HD * h:HD * (h + 1)], src.partition_broadcast(HD)).then_inc(ea_in, 16)

        with eng.Fori(0, PH_AS.rounds) as j:
            load_rows(j * 2)
            next_w(PH_AS, j, 0)
            load_rows_by_channel(j * 2)
            next_w(PH_AS, j, 1)
            load_rows(j * 2 + 1)
            next_w(PH_AS, j, 2)
            load_rows_by_channel(j * 2 + 1)
            next_w(PH_AS, j, 3)
        for p in range(3):
            next_w(PH_Z0, 0, p)
        with eng.Fori(0, PH_Z.rounds) as j:
            for p in range(3):
                next_w(PH_Z, j, p)

        def out_tile_used(h, p):
            if p in BY_TOKEN:
                eng.wait_ge(pass_done, 2 * TOK * h + 2 * TOK)
            elif p == 3:
                eng.wait_ge(pass_done, 2 * TOK * h + TOK)
            else:
                eng.wait_ge(out_done, 5 * h + (p if p < 3 else p - 1) + 1)

        slots = PH_OUT.slots * 2
        for n in range(1, 16):
            before = [b for b in range(n) if slots[b] == slots[n]]
            if before:
                out_tile_used(*divmod(before[-1], 8))
            else:
                eng.wait_ge(in_done, N_CHUNKS - (2 if n == 1 else 0))
            load_w(slots[n], PH_OUT.tile0 + n)
            if n == 4:
                eng.dma_start(pg[:], post_g.partition_broadcast(P)).then_inc(pg_in, 16)
            if n >= 14:
                eng.wait_ge(pass_done, 3 * TOK)
                t = TOK // 2 * (n - 14)
                src = x[0, t * P:(t + TOK // 2) * P, :].rearrange("(t p) d -> p t d", p=P)
                eng.dma_start(x_tm[:, t:t + TOK // 2, :], src).then_inc(x_tm_in[n - 14], 16)
        for t in range(TOK):
            eng.wait_ge(fin_done, t + 1)
            if t >= 2:
                eng.wait_ge(saved[t % 2], 16 * (t // 2))
            eng.dma_start(out[0, t * P:(t + 1) * P, :], ob[:, t, :]).then_inc(saved[t % 2], 16)
        for s in saved:
            eng.wait_ge(s, 16 * (TOK // 2))

    @block.gpsimd
    def _(eng):
        eng.memset(ones_d[:], 1.0 / D).then_inc(consts, 1)
        eng.memset(ones_c[:], 1.0 / D_C).then_inc(consts, 1)
        eng.memset(ones[:], 1.0).then_inc(consts, 1)
        eng.memset(ident[:], 0.0).then_inc(consts, 1)
        eng.memset(tri[:], 1.0).then_inc(consts, 1)
        eng.memset(mask4[:], 1.0).then_inc(consts, 1)
        eng.memset(sp[0][:], -1e4).then_inc(consts, 1)
        eng.wait_ge(consts, 7)
        eng.affine_select(out=ident[:], in_=ident[:], compare_op=ALU.not_equal, fill=1.0, base=0,
                          pattern=[[-1, P]], channel_multiplier=1).then_inc(consts, 1)
        eng.affine_select(out=tri[:], in_=tri[:], compare_op=ALU.is_ge, fill=0.0, base=0,
                          pattern=[[1, P]], channel_multiplier=-1).then_inc(consts, 1)
        eng.affine_select(out=mask4[:, 2:4, :], in_=mask4[:, 2:4, :], compare_op=ALU.is_ge, fill=0.0, base=0,
                          pattern=[[0, 2], [1, P]], channel_multiplier=-1).then_inc(consts, 1)

    @block.scalar
    def _(eng):
        act = eng.activation

        def split_w(slot, loads, n=1):
            eng.wait_ge(w_in[slot], loads * 16)
            act(w_hi[:, slot, :], w_raw[:, slot, :], ACT.Copy).then_inc(whi_done, 1)

        def split_next(ph, i, p):
            if p + 1 < len(ph.slots):
                split_w(ph.slots[p + 1], ph.loads(i, p + 1))
            else:
                split_w(0, ph.loads0[0] + (i + 1) * ph.slots.count(0) + 1)

        def evac(ph, i, q, dst, func=ACT.Copy, rows=P, bias=0.0):
            p = next(p for p in range(len(ph.slots) - 1, -1, -1) if q >= ph.first(p))
            a, w = ph.chunks[p][q - ph.first(p)]
            eng.wait_ge(in_done, ph.chunk(i, q) + 1)
            act(dst, ps[0:rows, ph.banks[q], 0:w], func, bias=bias).then_inc(in_evac, 1)

        eng.wait_ge(prm_in, 16)
        act(credits[:, 8:9], prm_col("norm_eps"), ACT.Sqrt).then_inc(ssm_silu, 1)

        def squares(n):
            a, w = FULL[n]
            eng.wait_ge(xch_in[n], 16)
            act(sq_in[:, :, a:a + w], x_in[:, :, a:a + w], ACT.Square).then_inc(sq_done, 1)

        def rms(n):
            eng.wait_ge(stat_done, n + 1)
            act(r_in[:, 3 * n:3 * n + 3], ps[:, bO, 3 * n:3 * n + 3], ACT.Sqrt, bias=prm_col("norm_eps")).then_inc(sd_done, 1)

        def head_in(n):
            a, w = FULL[n]
            eng.wait_ge(hn_done, n + 1)
            act(h_hi[:, :, a:a + w], x_in[:, :, a:a + w], ACT.Copy).then_inc(hhi_done, 1)

        def first_out(n):
            a, w = FULL[n]
            for p, (dst, func, rows, bias) in enumerate([
                    (sg[:, a:a + w], ACT.Sigmoid, P, 0.0),
                    (dt_cm[:, a:a + w], ACT.Identity, HEADS, prm[0:HEADS, PRM["dt_bias"][0]:PRM["dt_bias"][0] + 1]),
                    (u4[:, PAD_C + a:PAD_C + a + w], ACT.Copy, P, 0.0)]):
                if (n, p) == (2, 2):
                    split_w(0, 2)
                eng.wait_ge(in_done, 3 * n + p + 1)
                act(dst, ps[0:rows, p, 0:w], func, bias=bias).then_inc(in_evac, 1)

        squares(0)
        split_w(0, 1)
        rms(0)
        squares(1)
        head_in(0)
        rms(1)
        split_w(1, 1)
        squares(2)
        split_w(2, 1)
        head_in(1)
        rms(2)
        first_out(0)
        head_in(2)
        first_out(1)
        first_out(2)
        eng.wait_ge(dt_abs, 1)
        act(sp[1][:], sp[0][:], ACT.Abs).then_inc(sp_abs, 1)
        eng.wait_ge(sp_abs, 1)
        act(sp[2][:], sp[1][:], ACT.Exp, scale=-1.0).then_inc(dt_act, 1)
        act(a_neg[:], prm_col("a_log", 0, HEADS), ACT.Exp).then_inc(dt_act, 1)

        def ssm_tile(ph, i, r, n, between=None):
            split_next(ph, i, n)
            eng.wait_ge(ssm_conv, CREDIT + 3 * r)
            for q, (a, w) in enumerate(FULL):
                evac(ph, i, 3 * n + q, xr[n][:, KS - 1 + a:KS - 1 + a + w])
                if q == 0 and between:
                    between()

        def ssm_act(r, n):
            eng.wait_ge(ssm_conv, CREDIT + 3 * r + n + 1)
            act(xbc[:, bass.ds(3 * r + n, 1), :].rearrange("p o l -> p (o l)"), acc[n][:], ACT.Silu).then_inc(ssm_silu, 1)

        with eng.Fori(0, PH_XC.rounds) as i:
            ph = PH_XC
            ssm_tile(ph, i, i, 0)
            ssm_tile(ph, i, i, 1)
            ssm_tile(ph, i, i, 2, lambda: ssm_act(i, 0))
            ssm_act(i, 1)
            split_next(ph, i, 3)
            eng.wait_ge(u_done, i + 1)
            for q, (a, w) in enumerate(FULL):
                evac(ph, i, 9 + q, sg[:, a:a + w], ACT.Sigmoid)
            split_next(ph, i, 4)
            for q, (a, w) in enumerate(FULL):
                evac(ph, i, 12 + q, u4[:, bass.ds((i + 1) * U_STRIDE + (PAD_C + a), w)])
                if q == 0:
                    ssm_act(i, 2)
        ssm_tile(PH_X3, 0, 3, 0)
        eng.wait_ge(diff_done, 1)
        act(dts[:, 2], dts[:, 2], ACT.Exp).then_inc(dec_done, 1)
        act(dts[:, 3], dts[:, 3], ACT.Exp).then_inc(dec_done, 1)

        ssm_tile(PH_X3, 0, 3, 1, lambda: ssm_act(3, 0))
        ssm_tile(PH_X3, 0, 3, 2, lambda: ssm_act(3, 1))
        ssm_act(3, 2)
        eng.wait_ge(ssm_silu, CREDIT + 12)
        with eng.Fori(0, PH_AS.rounds) as j:
            ph = PH_AS

            def stage_x(m):
                eng.wait_ge(turn_done, CREDIT + m * GROUPS)
                act(xs_st[:], xbc[:, 0:N_B, bass.ds(m * P + META, P)], ACT.Copy).then_inc(staged, 1)

            def stage_bc(m):
                eng.wait_ge(scan_done, CREDIT + m * GROUPS)
                act(bc_st[:], xbc[:, N_B:12, bass.ds(m * P + META, P)], ACT.Copy).then_inc(staged, 1)

            def exps(m):
                for g in range(GROUPS):
                    eng.wait_ge(seg_done, m * GROUPS + g + 1)
                    act(e[g][:], e[g][:], ACT.Exp).then_inc(exp_done, 1)

            def exp_off(m):
                eng.wait_ge(ea_in, (m + 1) * 32)
                act(ea[:], ea[:], ACT.Exp).then_inc(ea_exp, 1)

            m = j * 2
            stage_x(m)
            stage_bc(m)
            split_next(ph, j, 0)
            eng.wait_ge(ya_done, CREDIT + j)
            for q in range(3):
                a, w = FULL[q]
                lo, s = max(a, META - PAD_A), META - PAD_A
                eng.wait_ge(in_done, ph.chunk(j, q) + 1)
                act(t1[:, lo - s:a + w - s], ps[:, ph.banks[q], lo - a:w], ACT.Copy).then_inc(in_evac, 1)
                if q == 1:
                    exps(m)
            exp_off(m)
            split_next(ph, j, 1)
            eng.wait_ge(ab_done, CREDIT + j)
            for q in range(3):
                a, w = FULL[q]
                evac(ph, j, 3 + q, t2[:, a:a + w])
                if q == 0:
                    stage_x(m + 1)
                if q == 1:
                    stage_bc(m + 1)
            split_next(ph, j, 2)
            eng.wait_ge(au_done, j + 1)
            for q in range(2):
                a, w = REAL[q]
                evac(ph, j, 6 + q, t2[:, a:a + w])
                if q == 0:
                    exps(m + 1)
            exp_off(m + 1)
            split_next(ph, j, 3)
            eng.wait_ge(aconv_done, j + 1)
            for q in range(2):
                a, w = REAL[q]
                evac(ph, j, 8 + q, t1[:, a - META:a - META + w], ACT.Silu)

        for n in range(N_C):
            eng.wait_ge(cmid_done, n + 1)
            act(csq[:, n, :], y_c[:, n, :], ACT.Square).then_inc(csq_done, 1)

        def gate_z(ph, i, r, p):
            split_next(ph, i, p)
            if p < 2:
                eng.wait_ge(zb_done, CREDIT + 2 * r)
            for q in range(2):
                a, w = REAL[q]
                if p < 2:
                    evac(ph, i, 2 * p + q, zt[p][:, a - META:a - META + w], ACT.Silu)
                else:
                    evac(ph, i, 4 + q, z_c[:, bass.ds(r, 1), a - META:a - META + w].rearrange("p o l -> p (o l)"), ACT.Silu)

        gate_z(PH_Z0, 0, 0, 0)
        gate_z(PH_Z0, 0, 0, 1)
        eng.wait_ge(cvar_done, 1)
        act(r_c[:], ps[:, bX, 0:TOK], ACT.Sqrt, bias=prm_col("ln_eps")).then_inc(csd_done, 1)
        gate_z(PH_Z0, 0, 0, 2)
        for n in range(N_C):
            eng.wait_ge(cnorm_done, n + 1)
            act(y_c[:, n, :], y_c[:, n, :], ACT.Silu, scale=prm_col("ln_g", n), bias=prm_col("ln_b", n)).then_inc(csilu_done, 1)
        with eng.Fori(0, PH_Z.rounds) as j:
            for p in range(3):
                gate_z(PH_Z, j, j + 1, p)

        def head(n):
            k = OUT_K[n]
            act(y_hi[:, k, :], y_f32(k), ACT.Copy, scale=prm_col("gain", k)).then_inc(yhi_done, 1)

        def out_w(n):
            h, p = divmod(n, 8)
            split_w(PH_OUT.slots[p], PH_OUT.loads(h, p))

        eng.wait_ge(in_done, N_CHUNKS)
        head(0)
        head(1)
        for n in range(1, 4):
            out_w(n)
            head(2 * n)
            head(2 * n + 1)
            if n == 1:
                eng.wait_ge(bms_done, 1)
                act(r_b[:], ps[:, bO, 0:TOK], ACT.Sqrt, bias=prm_col("norm_eps")).then_inc(bsd_done, 1)
        for n in range(8, 12):
            head(n)
        for n in range(12, 16):
            eng.wait_ge(yc_done, n - 11)
            head(n)
        eng.wait_ge(rb_done, 1)

        def mean_squares(h, t):
            eng.wait_ge(sum_done, CREDIT + TOK * h + t + 1)
            if TOK * h + t:
                eng.wait_ge(ssq_done, TOK * h + t)
            act(junk[:], branches[t % 2][:], ACT.Square,
                accum_out=ssq[:, TOK * h + t:TOK * h + t + 1]).then_inc(ssq_done, 1)

        for h in range(2):
            if h:
                for n in range(9, 12):
                    out_w(n)
            out_w(8 * h + 4)
            for t in range(TOK):
                eng.wait_ge(pass_done, 2 * TOK * h + t + 1)
                if h:
                    eng.wait_ge(sum_done, CREDIT + t + 1)
                act(part[:, t, :], ps[:, t, :], ACT.Copy, scale=r_b[:, t:t + 1]).then_inc(part_done, 1)
            for n in range(5, 8):
                out_w(8 * h + n)
            if h == 0:
                for t in range(TOK):
                    mean_squares(0, t)
                    if t == 2:
                        out_w(8)
                eng.wait_ge(ssq_done, TOK)
                act(ssq0[:], ssq[:, 0:TOK], ACT.Identity, scale=1.0 / D, bias=prm_col("norm_eps")).then_inc(ssq0_done, 1)
        eng.wait_ge(ssq0_done, 1)
        for t in range(TOK):
            mean_squares(1, t)
            eng.wait_ge(ssq_done, TOK + t + 1)
            act(r_out[:, t:t + 1], ssq[:, TOK + t:TOK + t + 1], ACT.Sqrt, scale=1.0 / D, bias=ssq0[:, t:t + 1]).then_inc(osd_done, 1)

    @block.tensor
    def _(eng):
        mm = eng.matmul

        def products(s, bank, a, w):
            for k in range(KD):
                hi, lo = w_hi[:, s, k * P:(k + 1) * P], w_lo[:, s, k * P:(k + 1) * P]
                dst = ps[:, bank, 0:w]
                mm(dst, hi, h_hi[:, k, a:a + w], start=(k == 0), stop=False)
                mm(dst, hi, h_lo[:, k, a:a + w], start=False, stop=False)
                last = mm(dst, lo, h_hi[:, k, a:a + w], start=False, stop=(k == KD - 1))
            last.then_inc(in_done, 1)

        def chunk(ph, i, p, q, bank, a, w):
            if q == ph.first(p):
                eng.wait_ge(wlo_done, ph.tile(i, p) + 1)
            eng.wait_ge(in_evac, ph.chunk(i, q) - 2)
            products(ph.slots[p], bank, a, w)

        def tile(ph, i, p, between=()):
            for n, (a, w) in enumerate(ph.chunks[p]):
                q = ph.first(p) + n
                chunk(ph, i, p, q, ph.banks[q], a, w)
                if n < len(between) and between[n]:
                    between[n]()

        eng.wait_ge(consts, 10)

        def stats(n):
            eng.wait_ge(sq_summed, n + 1)
            for c, a in enumerate(stat_tokens(*FULL[n])):
                last = mm(ps[:, bO, 3 * n + c:3 * n + c + 1], sq_in[:, 0, a:a + P], ones_d[:, 0:1], start=True, stop=True)
            last.then_inc(stat_done, 1)

        def spread(n):
            eng.wait_ge(diag_done, n + 1)
            for c, a in enumerate(stat_tokens(0, FULL[n][1])):
                last = mm(ps[:, 4 + n, a:a + P], ones[:], diag_in[:, c, :], start=True, stop=True)
            last.then_inc(rbc_done, 1)

        def first(n, p):
            eng.wait_ge(h_ready, n + 1)
            if n == 0:
                eng.wait_ge(wlo_done, p + 1)
            else:
                eng.wait_ge(in_evac, 3 * n + p - 2)
            products(p, p, *FULL[n])

        stats(0)
        spread(0)
        stats(1)
        spread(1)
        first(0, 0)
        first(0, 1)
        stats(2)
        first(0, 2)
        spread(2)
        for n in (1, 2):
            for p in range(3):
                first(n, p)
        eng.wait_ge(in_evac, 8)
        eng.transpose(ps[0:META, bO, 0:HEADS], dt_cm[:, 0:META], ident[0:HEADS, 0:HEADS])
        for m in range(TOK):
            last = eng.transpose(ps[:, bO, HEADS * (m + 1):HEADS * (m + 2)], dt_cm[:, META + m * P:META + (m + 1) * P],
                                 ident[0:HEADS, 0:HEADS])
        last.then_inc(dtT_done, 1)

        with eng.Fori(0, PH_XC.rounds) as i:
            for p in range(5):
                tile(PH_XC, i, p)

        def cumulate():
            eng.wait_ge(dt_ready, 1)
            mm(ps[:, bX, 0:NDT], tri[:], sp[3][:], start=True, stop=True)
            mm(ps[:, bX, 256:256 + NDT], ones[:], sp[3][:], start=True, stop=True).then_inc(cum_done, 1)

        def turn_cumulated():
            eng.wait_ge(cum_copied, 1)
            for m in range(TOK):
                last = eng.transpose(ps[0:HEADS, bS + m // 4, P * (m % 4):P * (m % 4 + 1)], dts[:, 1, m + 1, :], ident[:])
            last.then_inc(cumT_done, 1)

        def turn_meta():
            eng.wait_ge(ssm_silu, CREDIT + N_B + GROUPS)
            eng.wait_ge(diff_done, 1)
            for g in range(GROUPS):
                eng.transpose(ps[0:META, bO, P * g:P * (g + 1)], xbc[:, N_B + g, 0:META], ident[:])
            for t in range(N_B):
                last = eng.transpose(ps[0:META, bB + t // GT, P * (t % GT):P * (t % GT + 1)], xbc[:, t, 0:META], ident[:])
            last.then_inc(turn_done, 1)

        tile(PH_X3, 0, 0, [cumulate])
        tile(PH_X3, 0, 1, [turn_cumulated])
        tile(PH_X3, 0, 2, [turn_meta])
        eng.wait_ge(meta_ready, 1 + GROUPS)
        eng.wait_ge(rows_ready, 1)
        for g in range(GROUPS):
            last = mm(ps[:, bS + g, :], b_meta[:, g, :], xdt0[:, HPG * g:HPG * (g + 1), :].rearrange("p h d -> p (h d)"),
                      start=True, stop=True)
        last.then_inc(scan_done, 1)

        with eng.Fori(0, PH_AS.rounds) as j:
            def turn(m, g, first=False):
                if g == 0:
                    eng.wait_ge(staged, 2 * m + 2)
                    if first:
                        eng.wait_ge(in_evac, PH_AS.chunk(j, 0))
                    else:
                        eng.wait_ge(bcb_done, m)
                    for b in range(GROUPS):
                        eng.transpose(ps[:, bB, P * b:P * (b + 1)], bc_st[:, b, :], ident[:])
                    for b in range(GROUPS):
                        mm(ps[:, bB, P * (2 + b):P * (3 + b)], bc_st[:, b, :], bc_st[:, 2 + b, :], start=True, stop=True)
                eng.wait_ge(xd_done, CREDIT + m * GROUPS + g)
                for t in range(GT):
                    last = eng.transpose(ps[:, bX, P * t:P * (t + 1)], xs_st[:, GT * g + t, :], ident[:])
                last.then_inc(turn_done, 1)

            def scan(m, g):
                eng.wait_ge(m_done, m * GROUPS + g + 1)
                eng.wait_ge(y_done, CREDIT + m * GROUPS + g)
                for h in range(HPG):
                    mm(ps[HD * (h % 2):HD * (h % 2 + 1), bY, P * (h // 2):P * (h // 2 + 1)], xd[g][:, h, :], e[g][:, h, :],
                       start=True, stop=True)
                if g == 0:
                    eng.wait_ge(bcb_done, m + 1)
                eng.wait_ge(st_done, m * GROUPS + g + 1)
                for t in range(GT):
                    mm(ps[:, bO, P * t:P * (t + 1)],
                       state[:, HPG * g + 2 * t:HPG * g + 2 * t + 2, :].rearrange("p h d -> p (h d)"),
                       bc_st[:, 2 + g, :], start=True, stop=True)
                mm(ps[:, bS, :], b_cb[:, g, :], xdd[g][:].rearrange("p h d -> p (h d)"),
                   start=True, stop=True).then_inc(scan_done, 1)

            m = j * 2
            tile(PH_AS, j, 0, [lambda: turn(m, 0, True), lambda: turn(m, 1), None])
            tile(PH_AS, j, 1, [lambda: scan(m, 0), lambda: scan(m, 1), lambda: turn(m + 1, 0)])
            tile(PH_AS, j, 2, [lambda: turn(m + 1, 1), None])
            tile(PH_AS, j, 3, [lambda: scan(m + 1, 0), lambda: scan(m + 1, 1)])

        eng.wait_ge(conf_done, 3 + PH_AS.rounds)
        eng.wait_ge(in_evac, PH_Z0.chunk0)
        eng.wait_ge(xd_done, CREDIT + 2 * TOK)
        for h in range(2):
            for n in range(N_C):
                last = mm(ps[:, bB + h, :], ones_c[:], y_c[:, n, HALF * h:HALF * (h + 1)], start=(n == 0), stop=(n == N_C - 1))
        last.then_inc(cmean_done, 1)
        tile(PH_Z0, 0, 0)
        tile(PH_Z0, 0, 1)
        eng.wait_ge(csq_done, N_C)
        for t in range(TOK):
            for n in range(N_C):
                last = mm(ps[:, bX, t:t + 1], csq[:, n, P * t:P * (t + 1)], ones_c[:, 0:1], start=(n == 0), stop=(n == N_C - 1))
        last.then_inc(cvar_done, 1)
        tile(PH_Z0, 0, 2)
        eng.wait_ge(cdiag_done, 1)
        for h in range(2):
            last = mm(ps[:, bY + h, :], ones[:], diag_c[:, 4 * h:4 * h + 4, :].rearrange("p t l -> p (t l)"), start=True, stop=True)
        last.then_inc(crbc_done, 1)
        with eng.Fori(0, PH_Z.rounds) as j:
            for p in range(3):
                tile(PH_Z, j, p)
        eng.wait_ge(cnorm_done, N_C)
        eng.wait_ge(sqs_done, CREDIT + N_B)
        for t in range(TOK):
            last = mm(ps[:, bO, t:t + 1], sqs[:, P * t:P * (t + 1)], ones_d[:, 0:1], start=True, stop=True)
        last.then_inc(bms_done, 1)

        eng.wait_ge(in_evac, N_CHUNKS)
        with eng.Fori(0, 2) as h:
            def out_products(n, kk, t, opens=False, closes=False):
                k, s = OUT_K[2 * n + kk], PH_OUT.slots[n]
                hi, lo = w_hi[:, s, HALF * kk:HALF * (kk + 1)], w_lo[:, s, HALF * kk:HALF * (kk + 1)]
                yh = y_hi[:, k, P * t:P * (t + 1)]
                mm(ps[:, t, :], yh, hi, start=opens, stop=False)
                mm(ps[:, t, :], yh, lo, start=False, stop=False)
                return mm(ps[:, t, :], y_rest(k, P * t, P), hi, start=False, stop=closes)

            for n in range(BY_TOKEN[0]):
                eng.wait_ge(wlo_done, PH_OUT.tile(h, n) + 1)
                for kk in range(2):
                    opens, closes = (n, kk) in ((0, 0), (4, 0)), (n, kk) == (3, 1)
                    eng.wait_ge(ylo_done, 2 * n + kk + 1)
                    for t in range(TOK):
                        if opens:
                            if n == 0:
                                if t == bO:
                                    eng.wait_ge(bsd_done, 1)
                                eng.wait_ge(sum_done, CREDIT + h * (t + 1))
                            else:
                                eng.wait_ge(part_done, 8 * h + t + 1)
                        last = out_products(n, kk, t, opens, closes)
                        if closes:
                            last.then_inc(pass_done, 1)
                        elif kk == 1 and t == TOK - 1:
                            last.then_inc(out_done, 1)
            eng.wait_ge(wlo_done, PH_OUT.tile(h, BY_TOKEN[1]) + 1)
            eng.wait_ge(ylo_done, N_Y)
            for t in range(TOK):
                for n in BY_TOKEN:
                    for kk in range(2):
                        last = out_products(n, kk, t, closes=(n, kk) == (BY_TOKEN[1], 1))
                last.then_inc(pass_done, 1)

    @block.vector
    def _(eng):
        class Steps:

            def __init__(self):
                self.done, self.i, self.per, self.n = 0, None, 0, 0

            def enter(self, i, per):
                self.done, self.i, self.per, self.n = self.done + self.n, i, per, 0

            def leave(self, rounds):
                assert self.n == self.per, (self.n, self.per)
                self.done, self.i, self.n = self.done + rounds * self.per, None, 0

            def value(self, n=None):
                v = self.done + (self.n if n is None else n)
                return v if self.i is None else self.i * self.per + v

        steps = Steps()

        def step(ins):
            ins.then_inc(dve_step, 1)
            steps.n += 1

        def after(n=None):
            eng.wait_ge(dve_step, steps.value(n))

        def rest_w(slot, tile):
            eng.wait_ge(whi_done, tile + 1)
            eng.tensor_tensor(w_lo[:, slot, :], w_raw[:, slot, :], w_hi[:, slot, :].bitcast(F32), ALU.subtract).then_inc(wlo_done, 1)

        def rest_next(ph, i, p):
            rest_w(ph.slots[p + 1] if p + 1 < len(ph.slots) else 0, ph.tile(i, p + 1))

        for n, s in enumerate((y_done, xd_done, ssm_conv, ya_done, ab_done, zb_done, sum_done)):
            eng.memset(credits[:, n:n + 1], 0.0).then_inc(s, 1)
        def sum_squares(n):
            a, w = FULL[n]
            eng.wait_ge(sq_done, n + 1)
            for half in (4, 2, 1):
                ins = eng.tensor_tensor(sq_in[:, 0:half, a:a + w], sq_in[:, 0:half, a:a + w], sq_in[:, half:2 * half, a:a + w], ALU.add)
                if half > 1:
                    step(ins)
                    after()
                else:
                    ins.then_inc(sq_summed, 1)

        def inverse(n):
            r = r_in[:, 3 * n:3 * n + 3]
            eng.wait_ge(sd_done, n + 1)
            step(eng.reciprocal(r, r))
            if n:
                eng.wait_ge(rbc_done, n)
            after()
            eng.tensor_tensor(diag_in[:], ident[:].unsqueeze(1).broadcast_to([P, 3, P]),
                              r.unsqueeze(2).broadcast_to([P, 3, P]), ALU.mult).then_inc(diag_done, 1)

        def normal(n):
            a, w = FULL[n]
            eng.wait_ge(rbc_done, n + 1)
            for k in range(KD):
                last = eng.scalar_tensor_tensor(x_in[:, k, a:a + w], x_in[:, k, a:a + w], prm_col("pre_g", k), ps[:, 4 + n, 0:w],
                                                ALU.mult, ALU.mult)
            last.then_inc(hn_done, 1)

        def rest_in(n):
            a, w = FULL[n]
            eng.wait_ge(hhi_done, n + 1)
            eng.tensor_tensor(h_lo[:, :, a:a + w], x_in[:, :, a:a + w], h_hi[:, :, a:a + w].bitcast(F32),
                              ALU.subtract).then_inc(h_ready, 1)

        eng.wait_ge(prm_in, 16)
        eng.wait_ge(consts, 10)
        sum_squares(0)
        rest_w(0, 0)
        inverse(0)
        normal(0)
        sum_squares(1)
        rest_in(0)
        inverse(1)
        rest_w(1, 1)
        normal(1)
        rest_w(2, 2)
        sum_squares(2)
        rest_in(1)
        inverse(2)
        normal(2)
        rest_in(2)
        for b in range(3):
            step(eng.memset(xr[b][:, 0:KS - 1], 0.0))
        for n in range(N_C):
            step(eng.memset(u4[:, U_STRIDE * n:U_STRIDE * n + PAD_C], 0.0))

        def gated(evacuated, n):
            eng.wait_ge(in_evac, evacuated)
            u = u4[:, bass.ds(n * U_STRIDE + PAD_C, L)]
            eng.tensor_tensor(u, u, sg[:], ALU.mult).then_inc(u_done, 1)
            eng.wait_ge(u_done, n + 1)

        rest_w(0, PH_XC.tile0)
        gated(PH_XC.chunk0, 0)
        eng.wait_ge(dtT_done, 1)
        eng.wait_ge(consts, 10)
        step(eng.tensor_copy(sp[0][0:META, 0:HEADS], ps[0:META, bO, 0:HEADS]))
        eng.tensor_copy(sp[0][:, HEADS:NDT], ps[:, bO, HEADS:NDT]).then_inc(dt_abs, 1)
        eng.wait_ge(dt_abs, 1)
        after()
        step(eng.tensor_scalar(sp[5][:], sp[0][:], 0.0, None, ALU.max))
        eng.wait_ge(dt_act, 1)
        step(eng.tensor_scalar(sp[1][:], sp[2][:], 2.0, None, ALU.add))
        after()
        step(eng.reciprocal(sp[1][:], sp[1][:]))
        after()
        step(eng.tensor_tensor(sp[1][:], sp[1][:], sp[2][:], ALU.mult))
        after()
        step(eng.tensor_tensor(sp[2][:], sp[1][:], sp[1][:], ALU.mult))
        after()
        step(eng.tensor_scalar(sp[3][:], sp[2][:], 1.0 / 15, None, ALU.mult))
        for c in (13, 11, 9, 7, 5, 3):
            after()
            step(eng.scalar_tensor_tensor(sp[3][:], sp[3][:], 1.0 / c, sp[2][:], ALU.add, ALU.mult))
        after()
        step(eng.scalar_tensor_tensor(sp[3][:], sp[3][:], 1.0, sp[1][:], ALU.add, ALU.mult))
        after()
        dt_all = dts[:, 0].rearrange("p c h -> p (c h)")
        step(eng.scalar_tensor_tensor(dt_all, sp[3][:], 2.0, sp[5][:], ALU.mult, ALU.add))
        after()
        eng.wait_ge(dt_act, 2)
        eng.scalar_tensor_tensor(sp[3][:].rearrange("p (c h) -> p c h", h=HEADS), dts[:, 0], -1.0,
                                 a_neg[:].unsqueeze(1).broadcast_to([P, TOK + 1, HEADS]), ALU.mult, ALU.mult).then_inc(dt_ready, 1)

        XC_TAPS = 28
        AS_TAPS = (KC - 3) // PH_AS.rounds
        conf_at = [0, 0, 0, 0]

        def conf_tap(i, k, conf_w):
            dst = odd[:] if k % 2 else y_c[:, bass.ds(i, 1), :].rearrange("p o l -> p (o l)")
            src = u4[:, bass.ds(i * U_STRIDE + k, SEQ)]
            after(conf_at[k % 2])
            if k == 0:
                step(eng.tensor_scalar(dst, src, conf_w[:, 0:1], conf_w[:, KC:KC + 1], ALU.mult, ALU.add))
            elif k == 1:
                step(eng.tensor_scalar(dst, src, conf_w[:, 1:2], None, ALU.mult))
            else:
                step(eng.scalar_tensor_tensor(dst, src, conf_w[:, k:k + 1], dst, ALU.mult, ALU.add))
            conf_at[k % 2] = steps.n

        def late_tap(r, k):
            w = prm_col("conf_w", r * (KC + 1), KC + 1)
            dst, src = y_c[:, r, :], u4[:, U_STRIDE * r + k:U_STRIDE * r + k + SEQ]
            after(conf_at[r])
            if k == 0:
                ins = eng.tensor_scalar(dst, src, w[:, 0:1], w[:, KC:KC + 1], ALU.mult, ALU.add)
            else:
                ins = eng.scalar_tensor_tensor(dst, src, w[:, k:k + 1], dst, ALU.mult, ALU.add)
            if k == KC - 1:
                ins.then_inc(conf_done, 1)
            else:
                step(ins)
                conf_at[r] = steps.n

        ssm_at = [0]

        def ssm_start(ph, i, r, n):
            eng.wait_ge(in_evac, ph.chunk(i, 3 * n + 3))
            eng.wait_ge(ssm_silu, CREDIT + 3 * r)

        def ssm_tap(n, k, ssm_w):
            dst, src, w = acc[n][:], xr[n][:, k:k + L], ssm_w[:, n * (KS + 1):(n + 1) * (KS + 1)]
            after(ssm_at[0])
            if k == 0:
                step(eng.tensor_scalar(dst, src, w[:, 0:1], w[:, KS:KS + 1], ALU.mult, ALU.add))
            elif k < KS - 1:
                step(eng.scalar_tensor_tensor(dst, src, w[:, k:k + 1], dst, ALU.mult, ALU.add))
            else:
                eng.scalar_tensor_tensor(dst, src, w[:, k:k + 1], dst, ALU.mult, ALU.add).then_inc(ssm_conv, 1)
            ssm_at[0] = steps.n

        XC_STEPS = 3 + XC_TAPS + 3 * (KS - 1)
        with eng.Fori(0, PH_XC.rounds) as i:
            steps.enter(i, XC_STEPS)
            ph = PH_XC
            step(eng.tensor_copy(cur_conf[:], prm[:, bass.ds(i * (KC + 1) + PRM["conf_w"][0], KC + 1)]))
            eng.wait_ge(ssm_conv, CREDIT + 3 * i)
            step(eng.tensor_copy(cur_ssm[:], prm[:, bass.ds(i * (3 * (KS + 1)) + PRM["ssm_w"][0], 3 * (KS + 1))]))
            conf_at[0:2] = [steps.n, steps.n]
            ssm_at[0] = steps.n
            for k in range(0, 3):
                conf_tap(i, k, cur_conf)
            rest_next(ph, i, 0)
            for k in range(3, 8):
                conf_tap(i, k, cur_conf)
            for n in range(3):
                ssm_start(ph, i, i, n)
                for k in range(KS):
                    ssm_tap(n, k, cur_ssm)
                    conf_tap(i, 8 + KS * n + k, cur_conf)
                    if k == 1:
                        rest_next(ph, i, n + 1)
            for k in range(20, 24):
                conf_tap(i, k, cur_conf)
            rest_next(ph, i, 4)
            for k in range(24, XC_TAPS):
                conf_tap(i, k, cur_conf)
            after()
            yc = y_c[:, bass.ds(i, 1), :].rearrange("p o l -> p (o l)")
            step(eng.tensor_tensor(yc, yc, odd[:], ALU.add))
            gated(ph.chunk(i, 15), i + 1)
        steps.leave(PH_XC.rounds)
        conf_at[:], ssm_at[0] = [steps.n] * N_C, steps.n
        ssm_w = prm_col("ssm_w", 9 * (KS + 1), 3 * (KS + 1))
        ph = PH_X3
        for k in range(2):
            late_tap(3, k)
            late_tap(k, XC_TAPS)
        rest_next(ph, 0, 0)
        eng.wait_ge(cum_done, 1)
        flat = [dts[:, n].rearrange("p c h -> p (c h)") for n in range(4)]
        eng.tensor_copy(flat[1], ps[:, bX, 0:NDT]).then_inc(cum_copied, 1)
        step(eng.tensor_copy(flat[3], ps[:, bX, 256:256 + NDT]))
        eng.wait_ge(cum_copied, 1)
        after()
        eng.tensor_tensor(flat[2], flat[3], flat[1], ALU.subtract).then_inc(diff_done, 1)
        late_tap(3, 2)
        late_tap(2, XC_TAPS)
        eng.wait_ge(cumT_done, 1)
        eng.tensor_copy(acum_rows[:], ps[0:HEADS, bS:bS + 2, :].rearrange("p b c -> p (b c)")).then_inc(rows_ready, 1)
        eng.wait_ge(dec_done, 2)
        step(eng.tensor_tensor(dt_dec[0:META, :], dts[0:META, 0, 0, :], dts[0:META, 2, 0, :], ALU.mult))
        ssm_start(ph, 0, 3, 0)
        for k in range(KS):
            ssm_tap(0, k, ssm_w)
            if k < 3:
                late_tap(k, XC_TAPS + 1)
            if k == 1:
                rest_next(ph, 0, 1)
        ssm_start(ph, 0, 3, 1)
        for k in range(KS):
            ssm_tap(1, k, ssm_w)
            if k < 3:
                late_tap(k, XC_TAPS + 2)
        eng.wait_ge(turn_done, CREDIT)
        eng.tensor_copy(b_meta[:].rearrange("p g n -> p (g n)"), ps[0:META, bO, 0:2 * P]).then_inc(meta_ready, 1)
        for g in range(GROUPS):
            eng.tensor_tensor(xdt0[:, HPG * g:HPG * (g + 1), :], ps[0:META, bB + g, :].rearrange("p (h d) -> p h d", d=HD),
                              dt_dec[0:META, HPG * g:HPG * (g + 1)].unsqueeze(2).broadcast_to([META, HPG, HD]),
                              ALU.mult).then_inc(meta_ready, 1)
        rest_next(ph, 0, 2)
        ssm_start(ph, 0, 3, 2)
        for k in range(KS):
            ssm_tap(2, k, ssm_w)
        eng.wait_ge(scan_done, CREDIT)
        eng.tensor_copy(state[:].rearrange("p h d -> p (h d)"), banks(bS, 2)).then_inc(st_done, 1)

        AS_STEPS = 2 * (1 + GROUPS * (1 + 3)) + 1 + (KA - 1) + 1 + (AS_TAPS - 1)
        with eng.Fori(0, PH_AS.rounds) as j:
            steps.enter(j, AS_STEPS)
            ph = PH_AS
            m = j * 2

            def segs(m, g):
                eng.wait_ge(e_in[g], m * 16 + 16)
                for h in range(HPG):
                    ins = eng.tensor_scalar(e[g][:, h, :], e[g][:, h, :], cur_dt[:, 1, HPG * g + h:HPG * g + h + 1], 0.0,
                                            ALU.subtract, ALU.min)
                ins.then_inc(seg_done, 1)

            def expand(m, g):
                eng.wait_ge(turn_done, CREDIT + m * GROUPS + g + 1)
                hs = slice(HPG * g, HPG * (g + 1))
                eng.tensor_tensor(xd[g][:], ps[:, bX, :].rearrange("p (h d) -> p h d", d=HD),
                                  cur_dt[:, 0, hs].unsqueeze(2).broadcast_to([P, HPG, HD]), ALU.mult).then_inc(xd_done, 1)
                if g == 0:
                    eng.tensor_tensor(b_cb[:], ps[:, bB, :].rearrange("p (a c) -> p a c", a=4), mask4[:], ALU.mult).then_inc(bcb_done, 1)
                eng.wait_ge(xd_done, CREDIT + m * GROUPS + g + 1)
                step(eng.tensor_tensor(xdd[g][:], xd[g][:], cur_dt[:, 2, hs].unsqueeze(2).broadcast_to([P, HPG, HD]), ALU.mult))

            def mix(m, g):
                eng.wait_ge(exp_done, m * GROUPS + g + 1)
                eng.wait_ge(bcb_done, m + 1)
                eng.tensor_tensor(e[g][:], e[g][:], b_cb[:, 2 + g, :].unsqueeze(1).broadcast_to([P, HPG, P]), ALU.mult).then_inc(m_done, 1)

            def current(m):
                eng.wait_ge(st_done, m * GROUPS + 1)
                step(eng.tensor_copy(cur_dt[:], dts[:, :, bass.ds(m + 1, 1), :].rearrange("p a o h -> p a (o h)")))
                after()

            def finish(m, g):
                eng.wait_ge(scan_done, CREDIT + m * GROUPS + g + 1)
                if g == 0:
                    eng.wait_ge(ea_exp, m + 1)
                step(eng.tensor_tensor(ytmp[:], ps[:, bO, :].rearrange("p (t l) -> p t l", t=GT), ea[:, GT * g:GT * (g + 1), :], ALU.mult))
                st = state[:, HPG * g:HPG * (g + 1), :]
                step(eng.tensor_tensor(st, st, cur_dt[:, 3, HPG * g:HPG * (g + 1)].unsqueeze(2).broadcast_to([P, HPG, HD]), ALU.mult))
                after()
                step(eng.tensor_tensor(ytmp[:], ytmp[:], ps[:, bY, :].rearrange("p (t l) -> p t l", t=GT), ALU.add))
                eng.tensor_tensor(st, st, ps[:, bS, :].rearrange("p (h d) -> p h d", d=HD), ALU.add).then_inc(st_done, 1)
                after()
                for t in range(GT):
                    dst = xbc[:, GT * g + t, bass.ds(m * P + META, P)]
                    ins = eng.scalar_tensor_tensor(dst, dst, prm_col("d_skip", GT * g + t), ytmp[:, t, :],
                                                   ALU.mult, ALU.add)
                ins.then_inc(y_done, 1)

            def last_conf(k0, k1):
                dst = y_c[:, 3, :]
                for k in range(k0, k1):
                    if k == 0:
                        step(eng.tensor_copy(cur_conf[:, 0:AS_TAPS], prm[:, bass.ds(j * AS_TAPS + (PRM["conf_w"][0] + 3 * (KC + 1) + 3), AS_TAPS)]))
                        eng.wait_ge(conf_done, j + 3)
                        conf_at[3] = steps.n
                    after(conf_at[3])
                    ins = eng.scalar_tensor_tensor(dst, u4[:, bass.ds(j * AS_TAPS + (3 * U_STRIDE + 3 + k), SEQ)],
                                                   cur_conf[:, k:k + 1], dst, ALU.mult, ALU.add)
                    if k == AS_TAPS - 1:
                        ins.then_inc(conf_done, 1)
                    else:
                        step(ins)
                        conf_at[3] = steps.n

            current(m)
            segs(m, 0)
            expand(m, 0)
            segs(m, 1)
            rest_next(ph, j, 0)
            expand(m, 1)
            mix(m, 0)
            mix(m, 1)
            last_conf(0, 3)
            rest_next(ph, j, 1)
            finish(m, 0)
            finish(m, 1)
            current(m + 1)
            segs(m + 1, 0)
            expand(m + 1, 0)
            segs(m + 1, 1)
            last_conf(3, 5)
            rest_next(ph, j, 2)
            step(eng.tensor_copy(cur_a[:, 0:KA], prm[:, bass.ds(j * KA + PRM["conv_a"][0], KA)]))
            eng.wait_ge(in_evac, ph.chunk(j, 6))
            s = META - PAD_A
            eng.tensor_tensor(t1[:, 0:PAD_A + SEQ], t1[:, 0:PAD_A + SEQ], t2[:, s:L], ALU.mult).then_inc(au_done, 1)
            expand(m + 1, 1)
            mix(m + 1, 0)
            mix(m + 1, 1)
            last_conf(5, AS_TAPS)
            ya = y_a[:, bass.ds(j, 1), :].rearrange("p o l -> p (o l)")
            eng.wait_ge(au_done, j + 1)
            eng.wait_ge(conf_done, j + 4)
            after()
            step(eng.tensor_scalar(ya, t1[:, 0:SEQ], cur_a[:, 0:1], None, ALU.mult))
            after()
            step(eng.scalar_tensor_tensor(ya, t1[:, 1:1 + SEQ], cur_a[:, 1:2], ya, ALU.mult, ALU.add))
            after()
            eng.scalar_tensor_tensor(ya, t1[:, 2:2 + SEQ], cur_a[:, 2:3], ya, ALU.mult, ALU.add).then_inc(aconv_done, 1)
            finish(m + 1, 0)
            rest_next(ph, j, 3)
            eng.wait_ge(in_evac, ph.chunk(j, 8))
            eng.wait_ge(aconv_done, j + 1)
            eng.tensor_tensor(ya, ya, t2[:, META:L], ALU.mult).then_inc(ab_done, 1)
            finish(m + 1, 1)
            eng.wait_ge(in_evac, ph.chunk(j, 10))
            eng.wait_ge(ab_done, CREDIT + j + 1)
            eng.tensor_tensor(ya, ya, t1[:, 0:SEQ], ALU.mult).then_inc(ya_done, 1)
        steps.leave(PH_AS.rounds)

        eng.wait_ge(cmean_done, 1)
        for n in range(N_C):
            eng.tensor_tensor(y_c[:, n, :], y_c[:, n, :], banks(bB, 2), ALU.subtract).then_inc(cmid_done, 1)
        eng.memset(sqs[:], 0.0).then_inc(sqs_done, 1)

        def gate(ph, i, r):
            for p in range(2):
                rest_next(ph, i, p)
                eng.wait_ge(in_evac, ph.chunk(i, 2 * p + 2))
                yb = xbc[:, bass.ds(2 * r + p, 1), META:L].rearrange("p o l -> p (o l)")
                eng.tensor_tensor(yb, yb, zt[p][:], ALU.mult).then_inc(zb_done, 1)
                eng.wait_ge(zb_done, CREDIT + 2 * r + p + 1)
                eng.wait_ge(sqs_done, CREDIT + 2 * r + p)
                step(eng.tensor_tensor(sqb[:], yb, yb, ALU.mult))
                after()
                eng.tensor_tensor(sqs[:], sqs[:], sqb[:], ALU.add).then_inc(sqs_done, 1)

        gate(PH_Z0, 0, 0)
        eng.wait_ge(csd_done, 1)
        step(eng.reciprocal(r_c[:], r_c[:]))
        after()
        eng.tensor_tensor(diag_c[:], ident[:].unsqueeze(1).broadcast_to([P, TOK, P]),
                          r_c[:].unsqueeze(2).broadcast_to([P, TOK, P]), ALU.mult).then_inc(cdiag_done, 1)
        rest_next(PH_Z0, 0, 2)
        eng.wait_ge(crbc_done, 1)
        for n in range(N_C):
            eng.tensor_tensor(y_c[:, n, :], y_c[:, n, :], banks(bY, 2), ALU.mult).then_inc(cnorm_done, 1)
        with eng.Fori(0, PH_Z.rounds) as j:
            steps.enter(j, 2)
            gate(PH_Z, j, j + 1)
            rest_next(PH_Z, j, 2)
        steps.leave(PH_Z.rounds)

        def rest(n):
            k = OUT_K[n]
            eng.wait_ge(yhi_done, n + 1)
            eng.scalar_tensor_tensor(y_rest(k), y_f32(k), prm_col("gain", k), y_hi[:, k, :].bitcast(F32),
                                     ALU.mult, ALU.subtract).then_inc(ylo_done, 1)

        def out_w(n):
            rest_w(PH_OUT.slots[n % 8], PH_OUT.tile0 + n)

        rest(0)
        rest(1)
        for n in range(1, 4):
            out_w(n)
            rest(2 * n)
            rest(2 * n + 1)
            if n == 1:
                eng.wait_ge(bsd_done, 1)
                eng.reciprocal(r_b[:], r_b[:]).then_inc(rb_done, 1)
        for n in range(8, 12):
            rest(n)
        for n in range(N_C):
            eng.wait_ge(csilu_done, n + 1)
            eng.tensor_tensor(y_c[:, n, :], y_c[:, n, :], z_c[:, n, :], ALU.mult).then_inc(yc_done, 1)
            rest(12 + n)

        def add_branches(h, t):
            eng.wait_ge(pass_done, 2 * TOK * h + TOK + t + 1)
            eng.wait_ge(part_done, TOK * h + t + 1)
            if TOK * h + t >= 2:
                eng.wait_ge(ssq_done, TOK * h + t - 1)
            eng.tensor_tensor(branches[t % 2][:], ps[:, t, :], part[:, t, :], ALU.add).then_inc(sum_done, 1)
            eng.wait_ge(sum_done, CREDIT + TOK * h + t + 1)
            eng.tensor_tensor(ob[:, t, HALF * h:HALF * (h + 1)], branches[t % 2][:], pg[:, HALF * h:HALF * (h + 1)],
                              ALU.mult).then_inc(scaled_done, 1)

        def finish_rows(t):
            r = r_out[:, t:t + 1]
            eng.wait_ge(osd_done, t + 1)
            step(eng.reciprocal(r, r))
            eng.wait_ge(x_tm_in[t // (TOK // 2)], 16)
            eng.wait_ge(scaled_done, TOK + t + 1)
            after()
            eng.scalar_tensor_tensor(ob[:, t, :], ob[:, t, :], r, x_tm[:, t, :], ALU.mult, ALU.add).then_inc(fin_done, 1)

        eng.wait_ge(pg_in, 16)
        for h in range(2):
            for n in range(1 if h else 4, 8):
                out_w(8 * h + n)
            for t in range(TOK):
                add_branches(h, t)
                if h == 0 and t == 3:
                    out_w(8)
                if h == 1 and t >= 1:
                    finish_rows(t - 1)
        finish_rows(TOK - 1)

    ctx.close()


def kernel(**inputs):
    import numpy as np
    import concourse.bacc as bacc
    from concourse import mybir as mb
    from concourse.bass_utils import run_bass_kernel_spmd

    f = {k: np.asarray(v) for k, v in inputs.items()}
    x = np.ascontiguousarray(f["x"])
    tokens = np.concatenate([f["meta"], x[0]], axis=0)
    x_cm = np.ascontiguousarray(tokens.T.reshape(KD, P, L).transpose(1, 0, 2))

    w_in = f["w_in"][0]
    a_b, a_c, a_x, a_z, b_z, b_x, _, _, dt, c_a, c_g, c_z = (
        0, 512, 1024, 1536, 2048, 3072, 4096, 4352, 4608, 4624, 5136, 5648)
    cols = [c_g, dt, c_a]
    for i in range(4):
        cols += [b_x + P * (3 * i + n) for n in range(3)]
        if i < 3:
            cols += [c_g + P * (i + 1), c_a + P * (i + 1)]
    for j in range(4):
        cols += [a + P * j for a in (a_c, a_x, a_b, a_z)]
    for j in range(4):
        cols += [b_z + P * (2 * j), b_z + P * (2 * j + 1), c_z + P * j]
    tiles = [w_in[:, c:c + P].reshape(KD, P, P).transpose(1, 0, 2).reshape(P, KD * P) for c in cols]
    w_out = f["w_out"][0]
    for h in range(2):
        for n in range(8):
            ks = OUT_K[2 * n:2 * n + 2]
            tiles.append(np.concatenate([w_out[P * k:P * (k + 1), HALF * h:HALF * (h + 1)] for k in ks], axis=1))
    w_tiles = np.ascontiguousarray(np.stack(tiles))

    def chan(a):
        a = np.asarray(a)
        t = a.shape[-1] // P
        return a.reshape(-1, t, P).transpose(2, 1, 0).reshape(P, -1)

    params = np.zeros((P, N_PRM), np.float32)

    def put(name, value):
        at, n = PRM[name]
        params[:, at:at + n] = value

    put("pre_g", chan(f["pre_g"][0]))
    put("ssm_w", chan(np.concatenate([f["ssm_conv_w"][0], f["ssm_conv_b"]])))
    put("conf_w", chan(np.concatenate([f["conf_conv_w"][0], f["conf_conv_b"]])))
    put("ln_g", chan(f["conf_ln_g"][0]))
    put("ln_b", chan(f["conf_ln_b"][0]))
    put("gain", 1.0)
    at = PRM["gain"][0] + N_A
    params[:, at:at + N_B] = chan(f["ssm_norm_g"][0])
    put("d_skip", np.repeat(f["d_skip"][0], HD).reshape(N_B, P).T)
    put("a_log", np.broadcast_to(f["a_log"][0], (P, HEADS)))
    put("conv_a", chan(f["conv_a_w"][0]))
    params[0:HEADS, PRM["dt_bias"][0]] = f["dt_bias"][0]
    put("norm_eps", NORM_EPS)
    put("ln_eps", LN_EPS)

    arrays = {"xT_dram": x_cm, "x_dram": x, "w_dram": w_tiles, "params_dram": params,
              "post_g_dram": np.ascontiguousarray(f["post_g"][0])}
    nc = bacc.Bacc("TRN2", target_bir_lowering=False, num_devices=1, dynamic_dma_scratch_size=1024)
    aps = [nc.dram_tensor(k, v.shape, mb.dt.from_np(v.dtype), kind="ExternalInput").ap() for k, v in arrays.items()]
    acum = nc.dram_tensor("acum_dram", (HEADS, SEQ), mb.dt.float32, kind="Internal").ap()
    out = nc.dram_tensor("out_dram", x.shape, mb.dt.from_np(x.dtype), kind="ExternalOutput").ap()
    hybrid_mixer_kernel(nc, *aps, acum, out)
    r = run_bass_kernel_spmd(nc, [arrays], core_ids=[0])
    return r.results[0]["out_dram"]
```

```python
from contextlib import ExitStack

import concourse.bass as bass
from concourse import mybir

ALU = mybir.AluOpType
ACT = mybir.ActivationFunctionType
F32 = mybir.dt.float32
F32R = mybir.dt.float32r

P = 128
D = 1024
META = 16
SEQ = 1024
L = META + SEQ
KD = D // P
TOK = SEQ // P
D_A = D_C = 512
D_B = 1024
N_A, N_B, N_C = D_A // P, D_B // P, D_C // P
N_Y = N_A + N_B + N_C
HEADS, HD = 16, 64
GROUPS = 2
HPG = HEADS // GROUPS
GT = N_B // GROUPS
KA, KS, KC = 3, 4, 31
HALF = 512
NORM_EPS, LN_EPS = 1e-6, 1e-5

K_HALVES = [slice(0, KD // 2), slice(KD // 2, KD)]
FULL = [(0, 348), (348, 346), (694, 346)]
TAIL = [(META - (KA - 1), 342), (META - (KA - 1) + 342, 342), (META - (KA - 1) + 684, 342)]
REAL = [(META, HALF), (META + HALF, HALF)]


CREDIT = 1


class Phase:

    def __init__(self, before, rounds, slots, chunks, banks=None):
        self.rounds, self.slots, self.chunks = rounds, slots, chunks
        self.tile0 = before.tile0 + before.rounds * len(before.slots) if before else 0
        self.chunk0 = before.chunk0 + before.rounds * before.per_round if before else 0
        self.loads0 = [before.loads0[s] + before.rounds * before.slots.count(s) if before else 0 for s in range(3)]
        self.per_round = sum(map(len, chunks))
        self.banks = banks or [q % 3 for q in range(self.per_round)]

    def tile(self, i, p):
        return self.tile0 + i * len(self.slots) + p

    def chunk(self, i, q):
        return self.chunk0 + i * self.per_round + q

    def first(self, p):
        return sum(map(len, self.chunks[:p]))

    def loads(self, i, p):
        s = self.slots[p]
        return self.loads0[s] + i * self.slots.count(s) + self.slots[:p + 1].count(s)


PH_FIRST = Phase(None, 1, [0, 1, 2], [FULL] * 3)
PH_XC = Phase(PH_FIRST, 3, [0, 1, 2, 0, 1], [FULL] * 5)
PH_X3 = Phase(PH_XC, 1, [0, 1, 2], [FULL] * 3)
PH_AS = Phase(PH_X3, 4, [0, 1, 0, 1], [TAIL, TAIL, REAL, REAL], [0, 1, 2, 0, 1, 2, 0, 1, 2, 3])
PH_Z0 = Phase(PH_AS, 1, [0, 1, 2], [REAL] * 3)
PH_Z = Phase(PH_Z0, 3, [0, 1, 2], [REAL] * 3)
PH_OUT = Phase(PH_Z, 2, [0, 1, 2, 0, 1, 0, 2, 1], [[]] * 8)
BY_TOKEN = (6, 7)
N_TILES = PH_OUT.tile(2, 0)
N_CHUNKS = PH_OUT.chunk0
OUT_K = [4, 5, 6, 7, 8, 9, 10, 11, 0, 1, 2, 3, 12, 13, 14, 15]


PRM = {}
for _name, _n in [("pre_g", KD), ("ssm_w", 12 * (KS + 1)), ("conf_w", 4 * (KC + 1)),
                  ("ln_g", 4), ("ln_b", 4), ("gain", N_Y), ("d_skip", N_B), ("a_log", HEADS),
                  ("conv_a", 4 * KA), ("dt_bias", 1), ("norm_eps", 1), ("ln_eps", 1)]:
    PRM[_name] = (sum(n for _, n in PRM.values()), _n)
N_PRM = sum(n for _, n in PRM.values())


def hybrid_mixer_kernel(nc, xT, x, w_tiles, params, post_g, acum_dram, out):
    ctx = ExitStack()

    BASE = 288

    def at(name, offset, shape, dtype=F32):
        return nc.alloc_sbuf_tensor_at(name, shape, dtype, offset=4 * (BASE + offset))

    h_hi = at("h_hi", 0, [P, KD, L], F32R)
    h_lo = at("h_lo", KD * L, [P, KD, L], F32R)
    y_hi = at("y_hi", 0, [P, N_Y, SEQ], F32R)
    o = 2 * KD * L
    PAD_C = KC - 1 - META
    U_STRIDE = (PAD_C + L + 7) // 8 * 8
    U_BEFORE = 3 * U_STRIDE - 3 * SEQ
    U = o
    YA = U + U_BEFORE
    XBC = U + 4 * U_STRIDE
    YC = XBC + 12 * L
    u4 = at("u4", U, [P, 4 * U_STRIDE])
    y_a = at("y_a", YA, [P, N_A, SEQ])
    xbc = at("xbc", XBC, [P, 12, L])
    y_c = at("y_c", YC, [P, N_C, SEQ])
    lo_a = at("lo_a", YA, [P, N_A, SEQ], F32R)
    lo_b = at("lo_b", XBC, [P, N_B, L], F32R)
    lo_c = at("lo_c", YC, [P, N_C, SEQ], F32R)
    z_c = at("z_c", XBC + N_B * L, [P, N_C, SEQ])
    part = at("part", XBC + N_B * L, [P, TOK, HALF])
    o = YC + N_C * SEQ
    w_raw = at("w_raw", o, [P, 3, 1024])
    w_lo = at("w_lo", o, [P, 3, 1024], F32R)
    w_hi = at("w_hi", o + 3072, [P, 3, 1024], F32R)
    o += 6144
    small = {}
    for name, shape in [("ones_d", [P, P]), ("ones_c", [P, P]), ("ones", [P, P]), ("tri", [P, P]), ("ident", [P, P]),
                        ("mask4", [P, 4, P]), ("prm", [P, N_PRM]), ("cur_ssm", [P, 3 * (KS + 1)]), ("cur_conf", [P, KC + 1]),
                        ("conf_first", [P, KC + 1]), ("cur_a", [P, 4]), ("dts", [P, 4, TOK + 1, HEADS]), ("cur_dt", [P, 4, HEADS]),
                        ("a_neg", [P, HEADS]), ("dt_dec", [P, HEADS]), ("r_b", [P, TOK]), ("ssq", [P, 2 * TOK]),
                        ("ssq0", [P, TOK]), ("r_out", [P, TOK]), ("r_in", [P, 9]), ("r_c", [P, TOK]),
                        ("credits", [P, 16])]:
        n = 1
        for s in shape[1:]:
            n *= s
        small[name] = at(name, o, shape)
        o += (n + 7) // 8 * 8
    ones_d, ones_c, ones, tri, ident, mask4 = (small[n] for n in ("ones_d", "ones_c", "ones", "tri", "ident", "mask4"))
    prm, cur_ssm, cur_conf, conf_first, cur_a = (small[n] for n in ("prm", "cur_ssm", "cur_conf", "conf_first", "cur_a"))
    dts, cur_dt, a_neg, dt_dec, r_b, ssq, ssq0, r_out, r_in, r_c, credits = (
        small[n] for n in ("dts", "cur_dt", "a_neg", "dt_dec", "r_b", "ssq", "ssq0", "r_out", "r_in", "r_c", "credits"))
    W = o

    x_in = at("x_in", KD * L, [P, KD, L])
    sq_in = at("sq_in", 0, [P, KD, L])
    diag_in = at("diag_in", W + 8384, [P, 3, P])
    dt_cm = at("dt_cm", W + 9088, [HEADS, L])
    acum_rows = at("acum_rows", W + 8368, [HEADS, SEQ])
    NDT = (TOK + 1) * HEADS
    sp = [at(f"sp{n}", W + 10144 + NDT * n, [P, NDT]) for n in range(6)]
    xr = [at(f"xr{b}", W + 1048 * b, [P, KS - 1 + L]) for b in range(3)]
    acc = [at(f"acc{b}", W + 3144 + 1040 * b, [P, L]) for b in range(3)]
    sg = at("sg", W + 6272, [P, L])
    ODD_STRIDE = 1056
    odd = at("odd", W + 7312, [P, 2 * ODD_STRIDE])
    b_meta = at("b_meta", W + 6272, [META, GROUPS, P])
    xdt0 = at("xdt0", W + 7312, [META, HEADS, HD])
    e = [at(f"e{g}", W + 1024 * g, [P, HPG, P]) for g in range(2)]
    xs_st = at("xs_st", W + 2048, [P, N_B, P])
    bc_st = at("bc_st", W + 3072, [P, 4, P])
    b_cb = at("b_cb", W + 3584, [P, 4, P])
    ea = at("ea", W + 4096, [P, N_B, P])
    xd = [at("xd0", W + 5120, [P, HPG, HD]), at("xd1", W + 8368, [P, HPG, HD])]
    xdd = [at("xdd0", W + 5632, [P, HPG, HD]), at("xdd1", W + 8880, [P, HPG, HD])]
    PAD_A = KA - 1
    t1 = at("t1", W + 6272, [P, PAD_A + SEQ + 8])
    t2 = at("t2", W + 7320, [P, L])
    ytmp = at("ytmp", W + 9392, [P, GT, P])
    state = at("state", W + 9904, [P, HEADS, HD])
    zt = [at(f"zt{b}", W + 1024 * b, [P, SEQ]) for b in range(2)]
    sqb = at("sqb", W + 2048, [P, SEQ])
    sqs = at("sqs", W + 3072, [P, SEQ])
    csq = at("csq", W + 4096, [P, N_C, SEQ])
    diag_c = at("diag_c", W + 8192, [P, TOK, P])
    ob = at("ob", W, [P, TOK, D])
    branches = [at(f"branches{b}", W + 8192 + 512 * b, [P, HALF]) for b in range(2)]
    junk = at("junk", W + 9216, [P, HALF])
    pg = at("pg", W + 9728, [P, D])
    x_tm = at("x_tm", N_A * SEQ, [P, TOK, D])

    ps = ctx.enter_context(nc.psum_tensor("ps", [P, 8, HALF], F32))
    bB, bX, bS, bY, bO = 3, 4, 5, 6, 7

    def prm_col(name, j=0, n=1):
        return prm[:, PRM[name][0] + j:PRM[name][0] + j + n]

    def sem(name):
        return ctx.enter_context(nc.semaphore(name))

    prm_in, w_in = sem("prm_in"), [sem(f"w_in{s}") for s in range(3)]
    xch_in = [sem(f"xch_in{n}") for n in range(6)]
    consts = sem("consts")
    sq_done, sq_summed, stat_done, sd_done, diag_done, rbc_done, hn_done, hhi_done, h_ready = map(
        sem, ("sq_done", "sq_summed", "stat_done", "sd_done", "diag_done", "rbc_done", "hn_done", "hhi_done", "h_ready"))
    whi_done, wlo_done = sem("whi_done"), sem("wlo_done")
    in_done, in_evac = sem("in_done"), sem("in_evac")
    dve_step = sem("dve_step")
    dtT_done, dt_abs, dt_act, sp_abs, dt_ready = map(sem, ("dtT_done", "dt_abs", "dt_act", "sp_abs", "dt_ready"))
    cum_done, cum_copied, diff_done, dec_done, cumT_done, rows_ready, rows_saved = map(
        sem, ("cum_done", "cum_copied", "diff_done", "dec_done", "cumT_done", "rows_ready", "rows_saved"))
    meta_ready = sem("meta_ready")
    conf_w_in, conf_started = map(sem, ("conf_w_in", "conf_started"))
    ssm_w_in, ssm_conv, ssm_silu, u_done, conf_done = map(sem, ("ssm_w_in", "ssm_conv", "ssm_silu", "u_done", "conf_done"))
    e_in, ea_in = [sem("e_in0"), sem("e_in1")], sem("ea_in")
    staged, seg_done, exp_done, ea_exp = map(sem, ("staged", "seg_done", "exp_done", "ea_exp"))
    turn_done, bcb_done, xd_done, m_done, scan_done, y_read, y_done, st_done = map(
        sem, ("turn_done", "bcb_done", "xd_done", "m_done", "scan_done", "y_read", "y_done", "st_done"))
    au_done, aconv_done, ab_done, ya_done = map(sem, ("au_done", "aconv_done", "ab_done", "ya_done"))
    cmean_done, cmid_done, csq_done, cvar_done, csd_done, cdiag_done, crbc_done, cnorm_done, csilu_done, yc_done = map(
        sem, ("cmean_done", "cmid_done", "csq_done", "cvar_done", "csd_done", "cdiag_done", "crbc_done",
              "cnorm_done", "csilu_done", "yc_done"))
    zb_done, sqs_done, bms_done, bsd_done, rb_done = map(sem, ("zb_done", "sqs_done", "bms_done", "bsd_done", "rb_done"))
    yhi_half, ylo_half = map(sem, ("yhi_half", "ylo_half"))
    yhi_done, ylo_done, out_done, pass_done, part_done, sum_done = map(
        sem, ("yhi_done", "ylo_done", "out_done", "pass_done", "part_done", "sum_done"))
    ssq_done, ssq0_done, osd_done, x_tm_in, pg_in, scaled_done, fin_done, saved = (
        sem("ssq_done"), sem("ssq0_done"), sem("osd_done"), [sem("x_tm_in0"), sem("x_tm_in1")], sem("pg_in"),
        sem("scaled_done"), sem("fin_done"), [sem("saved0"), sem("saved1")])

    def y_f32(k, a=0, n=SEQ):
        if k < N_A:
            return y_a[:, k, a:a + n]
        if k < N_A + N_B:
            return xbc[:, k - N_A, META + a:META + a + n]
        return y_c[:, k - N_A - N_B, a:a + n]

    def y_rest(k, a=0, n=SEQ):
        if k < N_A:
            return lo_a[:, k, a:a + n]
        if k < N_A + N_B:
            return lo_b[:, k - N_A, META + a:META + a + n]
        return lo_c[:, k - N_A - N_B, a:a + n]

    def stat_tokens(a, w):
        return [a, a + P, a + w - P]

    def banks(b, n):
        return ps[:, b:b + n, :].rearrange("p b c -> p (b c)")

    block = ctx.enter_context(nc.Block())

    @block.sync
    def _(eng):
        def load_w(slot, tile):
            src = w_tiles[tile] if isinstance(tile, int) else w_tiles[bass.ds(tile, 1)].rearrange("o p n -> p (o n)")
            eng.dma_start(w_raw[:, slot, :], src).then_inc(w_in[slot], 16)

        for n, (a, w) in enumerate(FULL):
            for half, ks in enumerate(K_HALVES):
                eng.dma_start(x_in[:, ks, a:a + w], xT[:, ks, a:a + w]).then_inc(xch_in[2 * n + half], 16)
            if n == 0:
                eng.dma_start(prm[:], params).then_inc(prm_in, 16)
            load_w(PH_FIRST.slots[n], n)

        def next_w(ph, i, p):
            eng.wait_ge(in_done, ph.chunk(i, ph.first(p)))
            last = p + 1 == len(ph.slots)
            load_w(0 if last else ph.slots[p + 1], ph.tile(i, p + 1))

        eng.wait_ge(in_done, 7)
        load_w(0, PH_XC.tile0)
        with eng.Fori(0, PH_XC.rounds) as i:
            for p in range(5):
                next_w(PH_XC, i, p)
        for p in range(3):
            next_w(PH_X3, 0, p)
        eng.wait_ge(rows_ready, 1)
        eng.dma_start(acum_dram, acum_rows[:]).then_inc(rows_saved, 16)
        eng.wait_ge(rows_saved, 16)
        eng.wait_ge(ssm_conv, CREDIT + 11)

        def load_rows(m):
            for g in range(GROUPS):
                eng.wait_ge(scan_done, CREDIT + m * GROUPS)
                src = acum_dram[HPG * g:HPG * (g + 1), bass.ds(m * P, P)]
                eng.dma_start(e[g][:], src.partition_broadcast(P)).then_inc(e_in[g], 16)

        def load_rows_by_channel(m):
            eng.wait_ge(ssm_silu, CREDIT + 12)
            eng.wait_ge(y_done, CREDIT + m * GROUPS)
            for h in range(2):
                src = acum_dram[h:HEADS:2, bass.ds(m * P, P)]
                eng.dma_start(ea[HD * h:HD * (h + 1)], src.partition_broadcast(HD)).then_inc(ea_in, 16)

        with eng.Fori(0, PH_AS.rounds) as j:
            load_rows(j * 2)
            next_w(PH_AS, j, 0)
            load_rows_by_channel(j * 2)
            next_w(PH_AS, j, 1)
            load_rows(j * 2 + 1)
            next_w(PH_AS, j, 2)
            load_rows_by_channel(j * 2 + 1)
            next_w(PH_AS, j, 3)
        for p in range(3):
            next_w(PH_Z0, 0, p)
        with eng.Fori(0, PH_Z.rounds) as j:
            for p in range(3):
                next_w(PH_Z, j, p)

        def out_tile_used(h, p):
            if p in BY_TOKEN:
                eng.wait_ge(pass_done, 2 * TOK * h + 2 * TOK)
            elif p == 3:
                eng.wait_ge(pass_done, 2 * TOK * h + TOK)
            else:
                eng.wait_ge(out_done, 5 * h + (p if p < 3 else p - 1) + 1)

        slots = PH_OUT.slots * 2
        for n in range(1, 16):
            before = [b for b in range(n) if slots[b] == slots[n]]
            if before:
                out_tile_used(*divmod(before[-1], 8))
            else:
                eng.wait_ge(in_done, N_CHUNKS - (2 if n == 1 else 0))
            load_w(slots[n], PH_OUT.tile0 + n)
            if n == 4:
                eng.dma_start(pg[:], post_g.partition_broadcast(P)).then_inc(pg_in, 16)
            if n >= 14:
                eng.wait_ge(pass_done, 3 * TOK)
                t = TOK // 2 * (n - 14)
                src = x[0, t * P:(t + TOK // 2) * P, :].rearrange("(t p) d -> p t d", p=P)
                eng.dma_start(x_tm[:, t:t + TOK // 2, :], src).then_inc(x_tm_in[n - 14], 16)
        for t in range(TOK):
            eng.wait_ge(fin_done, t + 1)
            if t >= 2:
                eng.wait_ge(saved[t % 2], 16 * (t // 2))
            eng.dma_start(out[0, t * P:(t + 1) * P, :], ob[:, t, :]).then_inc(saved[t % 2], 16)
        for s in saved:
            eng.wait_ge(s, 16 * (TOK // 2))

    @block.gpsimd
    def _(eng):
        eng.memset(ones_d[:], 1.0 / D).then_inc(consts, 1)
        eng.memset(ones_c[:], 1.0 / D_C).then_inc(consts, 1)
        eng.memset(ones[:], 1.0).then_inc(consts, 1)
        eng.memset(ident[:], 0.0).then_inc(consts, 1)
        eng.memset(tri[:], 1.0).then_inc(consts, 1)
        eng.memset(mask4[:], 1.0).then_inc(consts, 1)
        eng.memset(sp[0][:], -1e4).then_inc(consts, 1)
        eng.wait_ge(consts, 7)
        eng.affine_select(out=ident[:], in_=ident[:], compare_op=ALU.not_equal, fill=1.0, base=0,
                          pattern=[[-1, P]], channel_multiplier=1).then_inc(consts, 1)
        eng.affine_select(out=tri[:], in_=tri[:], compare_op=ALU.is_ge, fill=0.0, base=0,
                          pattern=[[1, P]], channel_multiplier=-1).then_inc(consts, 1)
        eng.affine_select(out=mask4[:, 2:4, :], in_=mask4[:, 2:4, :], compare_op=ALU.is_ge, fill=0.0, base=0,
                          pattern=[[0, 2], [1, P]], channel_multiplier=-1).then_inc(consts, 1)

        eng.wait_ge(pg_in, 16)
        for h in range(2):
            cols = slice(HALF * h, HALF * (h + 1))
            for t in range(TOK):
                eng.wait_ge(sum_done, CREDIT + TOK * h + t + 1)
                eng.tensor_tensor(ob[:, t, cols], branches[t % 2][:], pg[:, cols], ALU.mult).then_inc(scaled_done, 1)

    @block.scalar
    def _(eng):
        act = eng.activation

        def split_w(slot, loads):
            eng.wait_ge(w_in[slot], loads * 16)
            act(w_hi[:, slot, :], w_raw[:, slot, :], ACT.Copy).then_inc(whi_done, 1)

        def split_next(ph, i, p):
            if p + 1 < len(ph.slots):
                split_w(ph.slots[p + 1], ph.loads(i, p + 1))
            else:
                split_w(0, ph.loads0[0] + (i + 1) * ph.slots.count(0) + 1)

        def evac(ph, i, q, dst, func=ACT.Copy):
            p = next(p for p in range(len(ph.slots) - 1, -1, -1) if q >= ph.first(p))
            _, w = ph.chunks[p][q - ph.first(p)]
            eng.wait_ge(in_done, ph.chunk(i, q) + 1)
            act(dst, ps[:, ph.banks[q], 0:w], func).then_inc(in_evac, 1)

        eng.wait_ge(prm_in, 16)
        act(credits[:, 8:9], prm_col("norm_eps"), ACT.Sqrt).then_inc(ssm_silu, 1)

        def squares(n):
            a, w = FULL[n]
            for half, ks in enumerate(K_HALVES):
                eng.wait_ge(xch_in[2 * n + half], 16)
                act(sq_in[:, ks, a:a + w], x_in[:, ks, a:a + w], ACT.Square).then_inc(sq_done, 1)

        def rms(n):
            eng.wait_ge(stat_done, n + 1)
            act(r_in[:, 3 * n:3 * n + 3], ps[:, bO, 3 * n:3 * n + 3], ACT.Sqrt, bias=prm_col("norm_eps")).then_inc(sd_done, 1)

        def head_in(n):
            a, w = FULL[n]
            for half, ks in enumerate(K_HALVES):
                eng.wait_ge(hn_done, 2 * n + half + 1)
                act(h_hi[:, ks, a:a + w], x_in[:, ks, a:a + w], ACT.Copy).then_inc(hhi_done, 1)

        def first_out(n):
            a, w = FULL[n]
            for p, (dst, func, rows, bias) in enumerate([
                    (dt_cm[:, a:a + w], ACT.Identity, HEADS, prm[0:HEADS, PRM["dt_bias"][0]:PRM["dt_bias"][0] + 1]),
                    (sg[:, a:a + w], ACT.Sigmoid, P, 0.0),
                    (u4[:, PAD_C + a:PAD_C + a + w], ACT.Copy, P, 0.0)]):
                if (n, p) == (2, 2):
                    eng.wait_ge(dt_abs, 1)
                    act(sp[1][:], sp[0][:], ACT.Abs).then_inc(sp_abs, 1)
                    eng.wait_ge(sp_abs, 1)
                    act(sp[2][:], sp[1][:], ACT.Exp, scale=-1.0).then_inc(dt_act, 1)
                    act(a_neg[:], prm_col("a_log", 0, HEADS), ACT.Exp).then_inc(dt_act, 1)
                    split_w(0, 2)
                eng.wait_ge(in_done, 3 * n + p + 1)
                act(dst, ps[0:rows, p, 0:w], func, bias=bias).then_inc(in_evac, 1)

        squares(0)
        split_w(0, 1)
        rms(0)
        squares(1)
        head_in(0)
        split_w(1, 1)
        split_w(2, 1)
        squares(2)
        rms(1)
        head_in(1)
        rms(2)
        first_out(0)
        head_in(2)
        first_out(1)
        first_out(2)

        def ssm_tile(ph, i, r, n, ssm_w, between=None):
            split_next(ph, i, n)
            eng.wait_ge(ssm_conv, CREDIT + 3 * r)
            eng.wait_ge(ssm_silu, CREDIT + 3 * r)
            w_last, bias = (ssm_w[:, n * (KS + 1) + k:n * (KS + 1) + k + 1] for k in (KS - 1, KS))
            for q, (a, w) in enumerate(FULL):
                eng.wait_ge(in_done, ph.chunk(i, 3 * n + q) + 1)
                act(xr[n][:, KS - 1 + a:KS - 1 + a + w], ps[:, q, 0:w], ACT.Copy)
                act(acc[n][:, a:a + w], ps[:, q, 0:w], ACT.Identity, scale=w_last, bias=bias).then_inc(in_evac, 1)
                if q == 0 and between:
                    between()

        def ssm_act(r, n):
            eng.wait_ge(ssm_conv, CREDIT + 3 * r + n + 1)
            act(xbc[:, bass.ds(3 * r + n, 1), :].rearrange("p o l -> p (o l)"), acc[n][:], ACT.Silu).then_inc(ssm_silu, 1)

        def conf_start(i):
            eng.wait_ge(u_done, i + 1)
            act(conf_first[:], prm[:, bass.ds(i * (KC + 1) + PRM["conf_w"][0], KC + 1)], ACT.Copy).then_inc(conf_w_in, 1)
            eng.wait_ge(conf_w_in, i + 1)
            act(y_c[:, bass.ds(i, 1), :].rearrange("p o l -> p (o l)"), u4[:, bass.ds(i * U_STRIDE, SEQ)],
                ACT.Identity, scale=conf_first[:, 0:1], bias=conf_first[:, KC:KC + 1])
            act(odd[:, bass.ds((i % 2) * ODD_STRIDE, SEQ)], u4[:, bass.ds(i * U_STRIDE + 1, SEQ)],
                ACT.Copy, scale=conf_first[:, 1:2]).then_inc(conf_started, 1)

        with eng.Fori(0, PH_XC.rounds) as i:
            ph = PH_XC
            conf_start(i)
            eng.wait_ge(ssm_conv, CREDIT + 3 * i)
            act(cur_ssm[:], prm[:, bass.ds(i * (3 * (KS + 1)) + PRM["ssm_w"][0], 3 * (KS + 1))], ACT.Copy).then_inc(ssm_w_in, 1)
            eng.wait_ge(ssm_w_in, i + 1)
            ssm_tile(ph, i, i, 0, cur_ssm)
            ssm_tile(ph, i, i, 1, cur_ssm)
            ssm_tile(ph, i, i, 2, cur_ssm, lambda: ssm_act(i, 0))
            ssm_act(i, 1)
            split_next(ph, i, 3)
            eng.wait_ge(u_done, i + 1)
            for q, (a, w) in enumerate(FULL):
                evac(ph, i, 9 + q, sg[:, a:a + w], ACT.Sigmoid)
            split_next(ph, i, 4)
            for q, (a, w) in enumerate(FULL):
                evac(ph, i, 12 + q, u4[:, bass.ds((i + 1) * U_STRIDE + (PAD_C + a), w)])
                if q == 0:
                    ssm_act(i, 2)
        ssm_w = prm_col("ssm_w", 9 * (KS + 1), 3 * (KS + 1))
        ssm_tile(PH_X3, 0, 3, 0, ssm_w)
        eng.wait_ge(diff_done, 1)
        act(dts[:, 2], dts[:, 2], ACT.Exp).then_inc(dec_done, 1)
        act(dts[:, 3], dts[:, 3], ACT.Exp).then_inc(dec_done, 1)
        ssm_tile(PH_X3, 0, 3, 1, ssm_w, lambda: ssm_act(3, 0))
        ssm_tile(PH_X3, 0, 3, 2, ssm_w, lambda: ssm_act(3, 1))
        ssm_act(3, 2)
        eng.wait_ge(ssm_silu, CREDIT + 12)
        with eng.Fori(0, PH_AS.rounds) as j:
            ph = PH_AS

            def stage_x(m):
                eng.wait_ge(turn_done, CREDIT + m * GROUPS)
                act(xs_st[:], xbc[:, 0:N_B, bass.ds(m * P + META, P)], ACT.Copy).then_inc(staged, 1)

            def stage_bc(m):
                eng.wait_ge(scan_done, CREDIT + m * GROUPS)
                act(bc_st[:], xbc[:, N_B:12, bass.ds(m * P + META, P)], ACT.Copy).then_inc(staged, 1)

            def exps(m):
                for g in range(GROUPS):
                    eng.wait_ge(seg_done, m * GROUPS + g + 1)
                    act(e[g][:], e[g][:], ACT.Exp).then_inc(exp_done, 1)

            def exp_off(m):
                eng.wait_ge(ea_in, (m + 1) * 32)
                act(ea[:], ea[:], ACT.Exp).then_inc(ea_exp, 1)

            m = j * 2
            stage_x(m)
            stage_bc(m)
            split_next(ph, j, 0)
            eng.wait_ge(ya_done, CREDIT + j)
            for q in range(3):
                a, w = TAIL[q]
                evac(ph, j, q, t1[:, a - TAIL[0][0]:a - TAIL[0][0] + w])
                if q == 1:
                    exps(m)
            exp_off(m)
            split_next(ph, j, 1)
            eng.wait_ge(ab_done, CREDIT + j)
            for q in range(3):
                a, w = TAIL[q]
                evac(ph, j, 3 + q, t2[:, a:a + w])
                if q == 0:
                    stage_x(m + 1)
                if q == 1:
                    stage_bc(m + 1)
            split_next(ph, j, 2)
            eng.wait_ge(au_done, j + 1)
            for q in range(2):
                a, w = REAL[q]
                evac(ph, j, 6 + q, t2[:, a:a + w])
                if q == 0:
                    exps(m + 1)
            exp_off(m + 1)
            split_next(ph, j, 3)
            eng.wait_ge(aconv_done, j + 1)
            for q in range(2):
                a, w = REAL[q]
                evac(ph, j, 8 + q, t1[:, a - META:a - META + w], ACT.Silu)

        for n in range(N_C):
            eng.wait_ge(cmid_done, n + 1)
            act(csq[:, n, :], y_c[:, n, :], ACT.Square).then_inc(csq_done, 1)

        def gate_z(ph, i, r, p):
            split_next(ph, i, p)
            if p < 2:
                eng.wait_ge(zb_done, CREDIT + 2 * r)
            for q in range(2):
                a, w = REAL[q]
                if p < 2:
                    evac(ph, i, 2 * p + q, zt[p][:, a - META:a - META + w], ACT.Silu)
                else:
                    evac(ph, i, 4 + q, z_c[:, bass.ds(r, 1), a - META:a - META + w].rearrange("p o l -> p (o l)"), ACT.Silu)

        gate_z(PH_Z0, 0, 0, 0)
        gate_z(PH_Z0, 0, 0, 1)
        eng.wait_ge(cvar_done, 1)
        act(r_c[:], ps[:, bX, 0:TOK], ACT.Sqrt, bias=prm_col("ln_eps")).then_inc(csd_done, 1)
        gate_z(PH_Z0, 0, 0, 2)
        for n in range(N_C):
            eng.wait_ge(cnorm_done, n + 1)
            act(y_c[:, n, :], y_c[:, n, :], ACT.Silu, scale=prm_col("ln_g", n), bias=prm_col("ln_b", n)).then_inc(csilu_done, 1)
        with eng.Fori(0, PH_Z.rounds) as j:
            for p in range(3):
                gate_z(PH_Z, j, j + 1, p)

        def head(n):
            k, done = OUT_K[n], 0
            if n == 0:
                done = SEQ // 2
                act(y_hi[:, k, 0:done], y_f32(k, 0, done), ACT.Copy, scale=prm_col("gain", k)).then_inc(yhi_half, 1)
            act(y_hi[:, k, done:SEQ], y_f32(k, done, SEQ - done), ACT.Copy, scale=prm_col("gain", k)).then_inc(yhi_done, 1)

        def out_w(n):
            h, p = divmod(n, 8)
            split_w(PH_OUT.slots[p], PH_OUT.loads(h, p))

        eng.wait_ge(in_done, N_CHUNKS)
        head(0)
        eng.wait_ge(bms_done, 1)
        act(r_b[:], ps[:, bO, 0:TOK], ACT.Sqrt, bias=prm_col("norm_eps")).then_inc(bsd_done, 1)
        head(1)
        for n in range(1, 4):
            out_w(n)
            head(2 * n)
            head(2 * n + 1)
        for n in range(8, 12):
            head(n)
        for n in range(12, 16):
            eng.wait_ge(yc_done, n - 11)
            head(n)
        eng.wait_ge(rb_done, 1)

        def mean_squares(h, t):
            eng.wait_ge(sum_done, CREDIT + TOK * h + t + 1)
            if TOK * h + t:
                eng.wait_ge(ssq_done, TOK * h + t)
            act(junk[:], branches[t % 2][:], ACT.Square,
                accum_out=ssq[:, TOK * h + t:TOK * h + t + 1]).then_inc(ssq_done, 1)

        for h in range(2):
            if h:
                for n in range(9, 12):
                    out_w(n)
            out_w(8 * h + 4)
            for t in range(TOK):
                eng.wait_ge(pass_done, 2 * TOK * h + t + 1)
                if h:
                    eng.wait_ge(sum_done, CREDIT + t + 1)
                act(part[:, t, :], ps[:, t, :], ACT.Copy, scale=r_b[:, t:t + 1]).then_inc(part_done, 1)
            for n in range(5, 8):
                out_w(8 * h + n)
            if h == 0:
                for t in range(TOK):
                    mean_squares(0, t)
                    if t == 2:
                        out_w(8)
                eng.wait_ge(ssq_done, TOK)
                act(ssq0[:], ssq[:, 0:TOK], ACT.Identity, scale=1.0 / D, bias=prm_col("norm_eps")).then_inc(ssq0_done, 1)
        eng.wait_ge(ssq0_done, 1)
        for t in range(TOK):
            mean_squares(1, t)
            eng.wait_ge(ssq_done, TOK + t + 1)
            act(r_out[:, t:t + 1], ssq[:, TOK + t:TOK + t + 1], ACT.Sqrt, scale=1.0 / D, bias=ssq0[:, t:t + 1]).then_inc(osd_done, 1)

    @block.tensor
    def _(eng):
        mm = eng.matmul

        def products(s, bank, a, w, first_chunk=None):
            for k in range(KD):
                if first_chunk is not None and k % (KD // 2) == 0:
                    eng.wait_ge(h_ready, 2 * first_chunk + k // (KD // 2) + 1)
                hi, lo = w_hi[:, s, k * P:(k + 1) * P], w_lo[:, s, k * P:(k + 1) * P]
                dst = ps[:, bank, 0:w]
                mm(dst, hi, h_hi[:, k, a:a + w], start=(k == 0), stop=False)
                mm(dst, hi, h_lo[:, k, a:a + w], start=False, stop=False)
                last = mm(dst, lo, h_hi[:, k, a:a + w], start=False, stop=(k == KD - 1))
            last.then_inc(in_done, 1)

        def chunk(ph, i, p, q, bank, a, w):
            if q == ph.first(p):
                eng.wait_ge(wlo_done, ph.tile(i, p) + 1)
            eng.wait_ge(in_evac, ph.chunk(i, q) - 2)
            products(ph.slots[p], bank, a, w)

        def tile(ph, i, p, between=()):
            for n, (a, w) in enumerate(ph.chunks[p]):
                q = ph.first(p) + n
                chunk(ph, i, p, q, ph.banks[q], a, w)
                if n < len(between) and between[n]:
                    between[n]()

        eng.wait_ge(consts, 10)

        def stats(n):
            eng.wait_ge(sq_summed, n + 1)
            for c, a in enumerate(stat_tokens(*FULL[n])):
                last = mm(ps[:, bO, 3 * n + c:3 * n + c + 1], sq_in[:, 0, a:a + P], ones_d[:, 0:1], start=True, stop=True)
            last.then_inc(stat_done, 1)

        def spread(n):
            eng.wait_ge(diag_done, n + 1)
            for c, a in enumerate(stat_tokens(0, FULL[n][1])):
                last = mm(ps[:, 4 + n, a:a + P], ones[:], diag_in[:, c, :], start=True, stop=True)
            last.then_inc(rbc_done, 1)

        def first(n, p):
            if n == 0:
                eng.wait_ge(wlo_done, p + 1)
            else:
                eng.wait_ge(in_evac, 3 * n + p - 2)
            products(p, p, *FULL[n], first_chunk=n)

        stats(0)
        spread(0)
        first(0, 0)
        stats(1)
        spread(1)
        first(0, 1)
        first(0, 2)
        stats(2)
        first(1, 0)
        spread(2)
        first(1, 1)
        first(1, 2)
        first(2, 0)
        first(2, 1)
        eng.wait_ge(in_evac, 7)
        eng.transpose(ps[0:META, bO, 0:HEADS], dt_cm[:, 0:META], ident[0:HEADS, 0:HEADS])
        for m in range(TOK):
            last = eng.transpose(ps[:, bO, HEADS * (m + 1):HEADS * (m + 2)], dt_cm[:, META + m * P:META + (m + 1) * P],
                                 ident[0:HEADS, 0:HEADS])
        last.then_inc(dtT_done, 1)
        first(2, 2)
        with eng.Fori(0, PH_XC.rounds) as i:
            for p in range(5):
                tile(PH_XC, i, p)

        def cumulate():
            eng.wait_ge(dt_ready, 1)
            mm(ps[:, bX, 0:NDT], tri[:], sp[3][:], start=True, stop=True)
            mm(ps[:, bX, 256:256 + NDT], ones[:], sp[3][:], start=True, stop=True).then_inc(cum_done, 1)

        def turn_cumulated():
            eng.wait_ge(cum_copied, 1)
            for m in range(TOK):
                last = eng.transpose(ps[0:HEADS, bS + m // 4, P * (m % 4):P * (m % 4 + 1)], dts[:, 1, m + 1, :], ident[:])
            last.then_inc(cumT_done, 1)

        def turn_meta():
            eng.wait_ge(ssm_silu, CREDIT + N_B + GROUPS)
            eng.wait_ge(diff_done, 1)
            for g in range(GROUPS):
                eng.transpose(ps[0:META, bO, P * g:P * (g + 1)], xbc[:, N_B + g, 0:META], ident[:])
            for t in range(N_B):
                last = eng.transpose(ps[0:META, bB + t // GT, P * (t % GT):P * (t % GT + 1)], xbc[:, t, 0:META], ident[:])
            last.then_inc(turn_done, 1)

        tile(PH_X3, 0, 0, [cumulate])
        tile(PH_X3, 0, 1, [turn_cumulated])
        tile(PH_X3, 0, 2, [turn_meta])
        eng.wait_ge(meta_ready, 1 + GROUPS)
        eng.wait_ge(rows_ready, 1)
        for g in range(GROUPS):
            last = mm(ps[:, bS + g, :], b_meta[:, g, :], xdt0[:, HPG * g:HPG * (g + 1), :].rearrange("p h d -> p (h d)"),
                      start=True, stop=True)
        last.then_inc(scan_done, 1)

        with eng.Fori(0, PH_AS.rounds) as j:
            def turn(m, g, first=False):
                if g == 0:
                    eng.wait_ge(staged, 2 * m + 2)
                    if first:
                        eng.wait_ge(in_evac, PH_AS.chunk(j, 0))
                    else:
                        eng.wait_ge(bcb_done, m)
                    for b in range(GROUPS):
                        eng.transpose(ps[:, bB, P * b:P * (b + 1)], bc_st[:, b, :], ident[:])
                    for b in range(GROUPS):
                        mm(ps[:, bB, P * (2 + b):P * (3 + b)], bc_st[:, b, :], bc_st[:, 2 + b, :], start=True, stop=True)
                eng.wait_ge(xd_done, CREDIT + m * GROUPS + g)
                for t in range(GT):
                    last = eng.transpose(ps[:, bX, P * t:P * (t + 1)], xs_st[:, GT * g + t, :], ident[:])
                last.then_inc(turn_done, 1)

            def scan(m, g):
                eng.wait_ge(m_done, m * GROUPS + g + 1)
                eng.wait_ge(y_read, CREDIT + m * GROUPS + g)
                for h in range(HPG):
                    mm(ps[HD * (h % 2):HD * (h % 2 + 1), bY, P * (h // 2):P * (h // 2 + 1)], xd[g][:, h, :], e[g][:, h, :],
                       start=True, stop=True)
                if g == 0:
                    eng.wait_ge(bcb_done, m + 1)
                eng.wait_ge(st_done, m * GROUPS + g + 1)
                for t in range(GT):
                    mm(ps[:, bO, P * t:P * (t + 1)],
                       state[:, HPG * g + 2 * t:HPG * g + 2 * t + 2, :].rearrange("p h d -> p (h d)"),
                       bc_st[:, 2 + g, :], start=True, stop=True)
                mm(ps[:, bS, :], b_cb[:, g, :], xdd[g][:].rearrange("p h d -> p (h d)"),
                   start=True, stop=True).then_inc(scan_done, 1)

            m = j * 2
            tile(PH_AS, j, 0, [None, lambda: turn(m, 0, True), lambda: turn(m, 1)])
            tile(PH_AS, j, 1, [lambda: scan(m, 0), lambda: scan(m, 1), lambda: turn(m + 1, 0)])
            tile(PH_AS, j, 2, [lambda: turn(m + 1, 1), None])
            tile(PH_AS, j, 3, [lambda: scan(m + 1, 0), lambda: scan(m + 1, 1)])

        eng.wait_ge(conf_done, 3 + PH_AS.rounds)
        eng.wait_ge(in_evac, PH_Z0.chunk0)
        eng.wait_ge(xd_done, CREDIT + 2 * TOK)
        for h in range(2):
            for n in range(N_C):
                last = mm(ps[:, bB + h, :], ones_c[:], y_c[:, n, HALF * h:HALF * (h + 1)], start=(n == 0), stop=(n == N_C - 1))
        last.then_inc(cmean_done, 1)
        tile(PH_Z0, 0, 0)
        tile(PH_Z0, 0, 1)
        eng.wait_ge(csq_done, N_C)
        for t in range(TOK):
            for n in range(N_C):
                last = mm(ps[:, bX, t:t + 1], csq[:, n, P * t:P * (t + 1)], ones_c[:, 0:1], start=(n == 0), stop=(n == N_C - 1))
        last.then_inc(cvar_done, 1)
        tile(PH_Z0, 0, 2)
        eng.wait_ge(cdiag_done, 1)
        for h in range(2):
            last = mm(ps[:, bY + h, :], ones[:], diag_c[:, 4 * h:4 * h + 4, :].rearrange("p t l -> p (t l)"), start=True, stop=True)
        last.then_inc(crbc_done, 1)
        with eng.Fori(0, PH_Z.rounds) as j:
            for p in range(3):
                tile(PH_Z, j, p)
        eng.wait_ge(cnorm_done, N_C)
        eng.wait_ge(sqs_done, CREDIT + N_B)
        for t in range(TOK):
            last = mm(ps[:, bO, t:t + 1], sqs[:, P * t:P * (t + 1)], ones_d[:, 0:1], start=True, stop=True)
        last.then_inc(bms_done, 1)

        eng.wait_ge(in_evac, N_CHUNKS)
        with eng.Fori(0, 2) as h:
            def out_products(n, kk, t, opens=False, closes=False):
                k, s = OUT_K[2 * n + kk], PH_OUT.slots[n]
                hi, lo = w_hi[:, s, HALF * kk:HALF * (kk + 1)], w_lo[:, s, HALF * kk:HALF * (kk + 1)]
                yh = y_hi[:, k, P * t:P * (t + 1)]
                mm(ps[:, t, :], yh, hi, start=opens, stop=False)
                mm(ps[:, t, :], yh, lo, start=False, stop=False)
                return mm(ps[:, t, :], y_rest(k, P * t, P), hi, start=False, stop=closes)

            for n in range(BY_TOKEN[0]):
                eng.wait_ge(wlo_done, PH_OUT.tile(h, n) + 1)
                for kk in range(2):
                    opens, closes = (n, kk) in ((0, 0), (4, 0)), (n, kk) == (3, 1)
                    if (n, kk) == (0, 0):
                        eng.wait_ge(ylo_half, 1)
                    for t in range(TOK):
                        if t == (TOK // 2 if (n, kk) == (0, 0) else 0):
                            eng.wait_ge(ylo_done, 2 * n + kk + 1)
                        if opens:
                            if n == 0:
                                if t == bO:
                                    eng.wait_ge(bsd_done, 1)
                                eng.wait_ge(sum_done, CREDIT + h * (t + 1))
                            else:
                                eng.wait_ge(part_done, 8 * h + t + 1)
                        last = out_products(n, kk, t, opens, closes)
                        if closes:
                            last.then_inc(pass_done, 1)
                        elif kk == 1 and t == TOK - 1:
                            last.then_inc(out_done, 1)
            eng.wait_ge(wlo_done, PH_OUT.tile(h, BY_TOKEN[1]) + 1)
            eng.wait_ge(ylo_done, N_Y)
            for t in range(TOK):
                for n in BY_TOKEN:
                    for kk in range(2):
                        last = out_products(n, kk, t, closes=(n, kk) == (BY_TOKEN[1], 1))
                last.then_inc(pass_done, 1)

    @block.vector
    def _(eng):
        class Steps:

            def __init__(self):
                self.done, self.i, self.per, self.n = 0, None, 0, 0

            def enter(self, i, per):
                self.done, self.i, self.per, self.n = self.done + self.n, i, per, 0

            def leave(self, rounds):
                assert self.n == self.per, (self.n, self.per)
                self.done, self.i, self.n = self.done + rounds * self.per, None, 0

            def value(self, n=None):
                v = self.done + (self.n if n is None else n)
                return v if self.i is None else self.i * self.per + v

        steps = Steps()

        def step(ins):
            ins.then_inc(dve_step, 1)
            steps.n += 1

        def after(n=None):
            eng.wait_ge(dve_step, steps.value(n))

        def rest_w(slot, tile):
            eng.wait_ge(whi_done, tile + 1)
            eng.tensor_tensor(w_lo[:, slot, :], w_raw[:, slot, :], w_hi[:, slot, :].bitcast(F32), ALU.subtract).then_inc(wlo_done, 1)

        def rest_next(ph, i, p):
            rest_w(ph.slots[p + 1] if p + 1 < len(ph.slots) else 0, ph.tile(i, p + 1))

        for n, s in enumerate((y_done, y_read, xd_done, ssm_conv, ya_done, ab_done, zb_done, sum_done)):
            eng.memset(credits[:, n:n + 1], 0.0).then_inc(s, 1)

        def sum_squares(n):
            a, w = FULL[n]

            def add(to, src, k):
                return eng.tensor_tensor(sq_in[:, to:to + k, a:a + w], sq_in[:, to:to + k, a:a + w], sq_in[:, src:src + k, a:a + w], ALU.add)

            eng.wait_ge(sq_done, 2 * n + 1)
            step(add(0, 2, 2))
            eng.wait_ge(sq_done, 2 * n + 2)
            step(add(4, 6, 2))
            after()
            step(add(0, 4, 2))
            after()
            add(0, 1, 1).then_inc(sq_summed, 1)

        def inverse(n):
            r = r_in[:, 3 * n:3 * n + 3]
            eng.wait_ge(sd_done, n + 1)
            step(eng.reciprocal(r, r))
            if n:
                eng.wait_ge(rbc_done, n)
            after()
            eng.tensor_tensor(diag_in[:], ident[:].unsqueeze(1).broadcast_to([P, 3, P]),
                              r.unsqueeze(2).broadcast_to([P, 3, P]), ALU.mult).then_inc(diag_done, 1)

        def normal(n):
            a, w = FULL[n]
            eng.wait_ge(rbc_done, n + 1)
            for k in range(KD):
                last = eng.scalar_tensor_tensor(x_in[:, k, a:a + w], x_in[:, k, a:a + w], prm_col("pre_g", k), ps[:, 4 + n, 0:w],
                                                ALU.mult, ALU.mult)
                if k % (KD // 2) == KD // 2 - 1:
                    last.then_inc(hn_done, 1)

        def rest_in(n):
            a, w = FULL[n]
            for half, ks in enumerate(K_HALVES):
                eng.wait_ge(hhi_done, 2 * n + half + 1)
                eng.tensor_tensor(h_lo[:, ks, a:a + w], x_in[:, ks, a:a + w], h_hi[:, ks, a:a + w].bitcast(F32),
                                  ALU.subtract).then_inc(h_ready, 1)

        eng.wait_ge(prm_in, 16)
        eng.wait_ge(consts, 10)
        sum_squares(0)
        rest_w(0, 0)
        inverse(0)
        normal(0)
        rest_in(0)
        sum_squares(1)
        rest_w(1, 1)
        inverse(1)
        rest_w(2, 2)
        normal(1)
        sum_squares(2)
        rest_in(1)
        inverse(2)
        normal(2)
        rest_in(2)
        for b in range(3):
            step(eng.memset(xr[b][:, 0:KS - 1], 0.0))
        for n in range(N_C):
            step(eng.memset(u4[:, U_STRIDE * n:U_STRIDE * n + PAD_C], 0.0))

        def gated(evacuated, n):
            eng.wait_ge(in_evac, evacuated)
            u = u4[:, bass.ds(n * U_STRIDE + PAD_C, L)]
            eng.tensor_tensor(u, u, sg[:], ALU.mult).then_inc(u_done, 1)

        eng.wait_ge(dtT_done, 1)
        eng.wait_ge(consts, 10)
        step(eng.tensor_copy(sp[0][0:META, 0:HEADS], ps[0:META, bO, 0:HEADS]))
        eng.tensor_copy(sp[0][:, HEADS:NDT], ps[:, bO, HEADS:NDT]).then_inc(dt_abs, 1)
        eng.wait_ge(dt_abs, 1)
        after()
        step(eng.tensor_scalar(sp[5][:], sp[0][:], 0.0, None, ALU.max))
        rest_w(0, PH_XC.tile0)
        gated(PH_XC.chunk0, 0)
        eng.wait_ge(dt_act, 1)
        step(eng.tensor_scalar(sp[1][:], sp[2][:], 2.0, None, ALU.add))
        after()
        step(eng.reciprocal(sp[1][:], sp[1][:]))
        after()
        step(eng.tensor_tensor(sp[1][:], sp[1][:], sp[2][:], ALU.mult))
        after()
        step(eng.tensor_tensor(sp[2][:], sp[1][:], sp[1][:], ALU.mult))
        after()
        step(eng.tensor_scalar(sp[3][:], sp[2][:], 1.0 / 15, None, ALU.mult))
        for c in (13, 11, 9, 7, 5, 3):
            after()
            step(eng.scalar_tensor_tensor(sp[3][:], sp[3][:], 1.0 / c, sp[2][:], ALU.add, ALU.mult))
        after()
        step(eng.scalar_tensor_tensor(sp[3][:], sp[3][:], 1.0, sp[1][:], ALU.add, ALU.mult))
        after()
        dt_all = dts[:, 0].rearrange("p c h -> p (c h)")
        step(eng.scalar_tensor_tensor(dt_all, sp[3][:], 2.0, sp[5][:], ALU.mult, ALU.add))
        after()
        eng.wait_ge(dt_act, 2)
        eng.scalar_tensor_tensor(sp[3][:].rearrange("p (c h) -> p c h", h=HEADS), dts[:, 0], -1.0,
                                 a_neg[:].unsqueeze(1).broadcast_to([P, TOK + 1, HEADS]), ALU.mult, ALU.mult).then_inc(dt_ready, 1)

        XC_TAPS = 28
        AS_TAPS = (KC - 3) // PH_AS.rounds
        conf_at = [0, 0, 0, 0]

        def conf_tap(i, k, conf_w):
            dst = odd[:, bass.ds((i % 2) * ODD_STRIDE, SEQ)] if k % 2 else y_c[:, bass.ds(i, 1), :].rearrange("p o l -> p (o l)")
            src = u4[:, bass.ds(i * U_STRIDE + k, SEQ)]
            after(conf_at[k % 2])
            step(eng.scalar_tensor_tensor(dst, src, conf_w[:, k:k + 1], dst, ALU.mult, ALU.add))
            conf_at[k % 2] = steps.n

        def late_tap(r, k):
            w = prm_col("conf_w", r * (KC + 1), KC + 1)
            dst, src = y_c[:, r, :], u4[:, U_STRIDE * r + k:U_STRIDE * r + k + SEQ]
            after(conf_at[r])
            if k == 0:
                ins = eng.tensor_scalar(dst, src, w[:, 0:1], w[:, KC:KC + 1], ALU.mult, ALU.add)
            else:
                ins = eng.scalar_tensor_tensor(dst, src, w[:, k:k + 1], dst, ALU.mult, ALU.add)
            if k == KC - 1:
                ins.then_inc(conf_done, 1)
            else:
                step(ins)
                conf_at[r] = steps.n

        ssm_at = [0]

        def ssm_start(ph, i, r, n):
            eng.wait_ge(in_evac, ph.chunk(i, 3 * n + 3))

        def ssm_tap(n, k, ssm_w):
            dst, src = acc[n][:], xr[n][:, k:k + L]
            if k:
                after(ssm_at[0])
            ins = eng.scalar_tensor_tensor(dst, src, ssm_w[:, n * (KS + 1) + k:n * (KS + 1) + k + 1], dst, ALU.mult, ALU.add)
            if k < KS - 2:
                step(ins)
            else:
                ins.then_inc(ssm_conv, 1)
            ssm_at[0] = steps.n

        XC_STEPS = 2 + XC_TAPS - 2 + 3 * (KS - 2)
        with eng.Fori(0, PH_XC.rounds) as i:
            steps.enter(i, XC_STEPS)
            ph = PH_XC
            step(eng.tensor_copy(cur_conf[:], prm[:, bass.ds(i * (KC + 1) + PRM["conf_w"][0], KC + 1)]))
            conf_at[0:2] = [steps.n, steps.n]
            eng.wait_ge(conf_started, i + 1)
            conf_tap(i, 2, cur_conf)
            rest_next(ph, i, 0)
            for k in range(3, 8):
                conf_tap(i, k, cur_conf)
            for n in range(3):
                if n == 0:
                    eng.wait_ge(ssm_w_in, i + 1)
                ssm_start(ph, i, i, n)
                for k in range(KS):
                    if k < KS - 1:
                        ssm_tap(n, k, cur_ssm)
                    conf_tap(i, 8 + KS * n + k, cur_conf)
                    if k == 0:
                        rest_next(ph, i, n + 1)
            for k in range(20, 24):
                conf_tap(i, k, cur_conf)
            rest_next(ph, i, 4)
            for k in range(24, XC_TAPS):
                conf_tap(i, k, cur_conf)
                if k == XC_TAPS - 3:
                    gated(ph.chunk(i, 15), i + 1)
            after()
            yc = y_c[:, bass.ds(i, 1), :].rearrange("p o l -> p (o l)")
            step(eng.tensor_tensor(yc, yc, odd[:, bass.ds((i % 2) * ODD_STRIDE, SEQ)], ALU.add))
        steps.leave(PH_XC.rounds)
        conf_at[:], ssm_at[0] = [steps.n] * N_C, steps.n
        ssm_w = prm_col("ssm_w", 9 * (KS + 1), 3 * (KS + 1))
        ph = PH_X3
        eng.wait_ge(u_done, N_C)
        late_tap(3, 0)
        late_tap(0, XC_TAPS)
        rest_next(ph, 0, 0)
        eng.wait_ge(cum_done, 1)
        flat = [dts[:, n].rearrange("p c h -> p (c h)") for n in range(4)]
        eng.tensor_copy(flat[1], ps[:, bX, 0:NDT]).then_inc(cum_copied, 1)
        step(eng.tensor_copy(flat[3], ps[:, bX, 256:256 + NDT]))
        eng.wait_ge(cum_copied, 1)
        after()
        eng.tensor_tensor(flat[2], flat[3], flat[1], ALU.subtract).then_inc(diff_done, 1)
        late_tap(3, 1)
        late_tap(1, XC_TAPS)
        late_tap(3, 2)
        ssm_start(ph, 0, 3, 0)
        ssm_tap(0, 0, ssm_w)
        late_tap(2, XC_TAPS)
        ssm_tap(0, 1, ssm_w)
        eng.wait_ge(cumT_done, 1)
        eng.tensor_copy(acum_rows[:], ps[0:HEADS, bS:bS + 2, :].rearrange("p b c -> p (b c)")).then_inc(rows_ready, 1)
        ssm_tap(0, 2, ssm_w)
        rest_next(ph, 0, 1)
        eng.wait_ge(dec_done, 2)
        step(eng.tensor_tensor(dt_dec[0:META, :], dts[0:META, 0, 0, :], dts[0:META, 2, 0, :], ALU.mult))
        dt_dec_at = steps.n
        for r in range(3):
            late_tap(r, XC_TAPS + 1)
        ssm_start(ph, 0, 3, 1)
        ssm_tap(1, 0, ssm_w)
        late_tap(0, XC_TAPS + 2)
        ssm_tap(1, 1, ssm_w)
        eng.wait_ge(turn_done, CREDIT)
        eng.tensor_copy(b_meta[:].rearrange("p g n -> p (g n)"), ps[0:META, bO, 0:2 * P]).then_inc(meta_ready, 1)
        after(dt_dec_at)
        for g in range(GROUPS):
            eng.tensor_tensor(xdt0[:, HPG * g:HPG * (g + 1), :], ps[0:META, bB + g, :].rearrange("p (h d) -> p h d", d=HD),
                              dt_dec[0:META, HPG * g:HPG * (g + 1)].unsqueeze(2).broadcast_to([META, HPG, HD]),
                              ALU.mult).then_inc(meta_ready, 1)
        ssm_tap(1, 2, ssm_w)
        late_tap(1, XC_TAPS + 2)
        late_tap(2, XC_TAPS + 2)
        rest_next(ph, 0, 2)
        ssm_start(ph, 0, 3, 2)
        for k in range(KS - 1):
            ssm_tap(2, k, ssm_w)
        eng.wait_ge(scan_done, CREDIT)
        eng.tensor_copy(state[:].rearrange("p h d -> p (h d)"), banks(bS, 2)).then_inc(st_done, 1)

        AS_STEPS = 2 * (1 + GROUPS * (1 + 2)) + 1 + (KA - 1) + 1 + (AS_TAPS - 1)
        with eng.Fori(0, PH_AS.rounds) as j:
            steps.enter(j, AS_STEPS)
            ph = PH_AS
            m = j * 2

            def segs(m, g):
                eng.wait_ge(e_in[g], m * 16 + 16)
                for h in range(HPG):
                    ins = eng.tensor_scalar(e[g][:, h, :], e[g][:, h, :], cur_dt[:, 1, HPG * g + h:HPG * g + h + 1], 0.0,
                                            ALU.subtract, ALU.min)
                ins.then_inc(seg_done, 1)

            def expand(m, g):
                eng.wait_ge(turn_done, CREDIT + m * GROUPS + g + 1)
                hs = slice(HPG * g, HPG * (g + 1))
                eng.tensor_tensor(xd[g][:], ps[:, bX, :].rearrange("p (h d) -> p h d", d=HD),
                                  cur_dt[:, 0, hs].unsqueeze(2).broadcast_to([P, HPG, HD]), ALU.mult).then_inc(xd_done, 1)
                if g == 0:
                    eng.tensor_tensor(b_cb[:], ps[:, bB, :].rearrange("p (a c) -> p a c", a=4), mask4[:], ALU.mult).then_inc(bcb_done, 1)
                eng.wait_ge(xd_done, CREDIT + m * GROUPS + g + 1)
                step(eng.tensor_tensor(xdd[g][:], xd[g][:], cur_dt[:, 2, hs].unsqueeze(2).broadcast_to([P, HPG, HD]), ALU.mult))

            def mix(m, g):
                eng.wait_ge(exp_done, m * GROUPS + g + 1)
                eng.wait_ge(bcb_done, m + 1)
                eng.tensor_tensor(e[g][:], e[g][:], b_cb[:, 2 + g, :].unsqueeze(1).broadcast_to([P, HPG, P]), ALU.mult).then_inc(m_done, 1)

            def current(m):
                eng.wait_ge(st_done, m * GROUPS + 1)
                step(eng.tensor_copy(cur_dt[:], dts[:, :, bass.ds(m + 1, 1), :].rearrange("p a o h -> p a (o h)")))
                after()

            def finish(m, g):
                eng.wait_ge(y_done, CREDIT + m * GROUPS + g)
                eng.wait_ge(scan_done, CREDIT + m * GROUPS + g + 1)
                if g == 0:
                    eng.wait_ge(ea_exp, m + 1)
                step(eng.tensor_tensor(ytmp[:], ps[:, bO, :].rearrange("p (t l) -> p t l", t=GT), ea[:, GT * g:GT * (g + 1), :], ALU.mult))
                st = state[:, HPG * g:HPG * (g + 1), :]
                step(eng.tensor_tensor(st, st, cur_dt[:, 3, HPG * g:HPG * (g + 1)].unsqueeze(2).broadcast_to([P, HPG, HD]), ALU.mult))
                after()
                eng.tensor_tensor(ytmp[:], ytmp[:], ps[:, bY, :].rearrange("p (t l) -> p t l", t=GT), ALU.add).then_inc(y_read, 1)
                eng.tensor_tensor(st, st, ps[:, bS, :].rearrange("p (h d) -> p h d", d=HD), ALU.add).then_inc(st_done, 1)
                eng.wait_ge(y_read, CREDIT + m * GROUPS + g + 1)
                for t in range(GT):
                    dst = xbc[:, GT * g + t, bass.ds(m * P + META, P)]
                    ins = eng.scalar_tensor_tensor(dst, dst, prm_col("d_skip", GT * g + t), ytmp[:, t, :],
                                                   ALU.mult, ALU.add)
                ins.then_inc(y_done, 1)

            def last_conf(k0, k1):
                dst = y_c[:, 3, :]
                for k in range(k0, k1):
                    if k == 0:
                        w0 = PRM["conf_w"][0] + 3 * (KC + 1) + 3
                        step(eng.tensor_copy(cur_conf[:, 0:AS_TAPS], prm[:, bass.ds(j * AS_TAPS + w0, AS_TAPS)]))
                        eng.wait_ge(conf_done, j + 3)
                        conf_at[3] = steps.n
                    after(conf_at[3])
                    ins = eng.scalar_tensor_tensor(dst, u4[:, bass.ds(j * AS_TAPS + (3 * U_STRIDE + 3 + k), SEQ)],
                                                   cur_conf[:, k:k + 1], dst, ALU.mult, ALU.add)
                    if k == AS_TAPS - 1:
                        ins.then_inc(conf_done, 1)
                    else:
                        step(ins)
                        conf_at[3] = steps.n

            current(m)
            segs(m, 0)
            segs(m, 1)
            rest_next(ph, j, 0)
            expand(m, 0)
            mix(m, 0)
            expand(m, 1)
            mix(m, 1)
            last_conf(0, 2)
            finish(m, 0)
            rest_next(ph, j, 1)
            last_conf(2, 4)
            finish(m, 1)
            current(m + 1)
            segs(m + 1, 0)
            expand(m + 1, 0)
            segs(m + 1, 1)
            last_conf(4, 5)
            rest_next(ph, j, 2)
            step(eng.tensor_copy(cur_a[:, 0:KA], prm[:, bass.ds(j * KA + PRM["conv_a"][0], KA)]))
            eng.wait_ge(in_evac, ph.chunk(j, 6))
            s = META - PAD_A
            eng.tensor_tensor(t1[:, 0:PAD_A + SEQ], t1[:, 0:PAD_A + SEQ], t2[:, s:L], ALU.mult).then_inc(au_done, 1)
            expand(m + 1, 1)
            mix(m + 1, 0)
            mix(m + 1, 1)
            last_conf(5, AS_TAPS)
            ya = y_a[:, bass.ds(j, 1), :].rearrange("p o l -> p (o l)")
            eng.wait_ge(au_done, j + 1)
            eng.wait_ge(conf_done, j + 4)
            after()
            step(eng.tensor_scalar(ya, t1[:, 0:SEQ], cur_a[:, 0:1], None, ALU.mult))
            after()
            step(eng.scalar_tensor_tensor(ya, t1[:, 1:1 + SEQ], cur_a[:, 1:2], ya, ALU.mult, ALU.add))
            after()
            eng.scalar_tensor_tensor(ya, t1[:, 2:2 + SEQ], cur_a[:, 2:3], ya, ALU.mult, ALU.add).then_inc(aconv_done, 1)
            finish(m + 1, 0)
            rest_next(ph, j, 3)
            eng.wait_ge(in_evac, ph.chunk(j, 8))
            eng.wait_ge(aconv_done, j + 1)
            eng.tensor_tensor(ya, ya, t2[:, META:L], ALU.mult).then_inc(ab_done, 1)
            finish(m + 1, 1)
            eng.wait_ge(in_evac, ph.chunk(j, 10))
            eng.wait_ge(ab_done, CREDIT + j + 1)
            eng.tensor_tensor(ya, ya, t1[:, 0:SEQ], ALU.mult).then_inc(ya_done, 1)
        steps.leave(PH_AS.rounds)

        eng.wait_ge(cmean_done, 1)
        for n in range(N_C):
            eng.tensor_tensor(y_c[:, n, :], y_c[:, n, :], banks(bB, 2), ALU.subtract).then_inc(cmid_done, 1)
        eng.memset(sqs[:], 0.0).then_inc(sqs_done, 1)

        def gate(ph, i, r):
            for p in range(2):
                rest_next(ph, i, p)
                eng.wait_ge(in_evac, ph.chunk(i, 2 * p + 2))
                yb = xbc[:, bass.ds(2 * r + p, 1), META:L].rearrange("p o l -> p (o l)")
                eng.tensor_tensor(yb, yb, zt[p][:], ALU.mult).then_inc(zb_done, 1)
                eng.wait_ge(zb_done, CREDIT + 2 * r + p + 1)
                eng.wait_ge(sqs_done, CREDIT + 2 * r + p)
                step(eng.tensor_tensor(sqb[:], yb, yb, ALU.mult))
                after()
                eng.tensor_tensor(sqs[:], sqs[:], sqb[:], ALU.add).then_inc(sqs_done, 1)

        gate(PH_Z0, 0, 0)
        eng.wait_ge(csd_done, 1)
        step(eng.reciprocal(r_c[:], r_c[:]))
        after()
        eng.tensor_tensor(diag_c[:], ident[:].unsqueeze(1).broadcast_to([P, TOK, P]),
                          r_c[:].unsqueeze(2).broadcast_to([P, TOK, P]), ALU.mult).then_inc(cdiag_done, 1)
        rest_next(PH_Z0, 0, 2)
        eng.wait_ge(crbc_done, 1)
        for n in range(N_C):
            eng.tensor_tensor(y_c[:, n, :], y_c[:, n, :], banks(bY, 2), ALU.mult).then_inc(cnorm_done, 1)
        with eng.Fori(0, PH_Z.rounds) as j:
            steps.enter(j, 2)
            gate(PH_Z, j, j + 1)
            rest_next(PH_Z, j, 2)
        steps.leave(PH_Z.rounds)

        def rest(n):
            k, done = OUT_K[n], 0
            if n == 0:
                done = SEQ // 2
                eng.wait_ge(yhi_half, 1)
                eng.scalar_tensor_tensor(y_rest(k, 0, done), y_f32(k, 0, done), prm_col("gain", k), y_hi[:, k, 0:done].bitcast(F32),
                                         ALU.mult, ALU.subtract).then_inc(ylo_half, 1)
            eng.wait_ge(yhi_done, n + 1)
            eng.scalar_tensor_tensor(y_rest(k, done, SEQ - done), y_f32(k, done, SEQ - done), prm_col("gain", k),
                                     y_hi[:, k, done:SEQ].bitcast(F32), ALU.mult, ALU.subtract).then_inc(ylo_done, 1)

        def out_w(n):
            rest_w(PH_OUT.slots[n % 8], PH_OUT.tile0 + n)

        rest(0)
        rest(1)
        for n in range(1, 4):
            out_w(n)
            rest(2 * n)
            rest(2 * n + 1)
            if n == 1:
                eng.wait_ge(bsd_done, 1)
                eng.reciprocal(r_b[:], r_b[:]).then_inc(rb_done, 1)
        for n in range(8, 12):
            rest(n)
        for n in range(N_C):
            eng.wait_ge(csilu_done, n + 1)
            eng.tensor_tensor(y_c[:, n, :], y_c[:, n, :], z_c[:, n, :], ALU.mult).then_inc(yc_done, 1)
            rest(12 + n)

        def add_branches(h, t):
            eng.wait_ge(pass_done, 2 * TOK * h + TOK + t + 1)
            eng.wait_ge(part_done, TOK * h + t + 1)
            if TOK * h + t >= 2:
                eng.wait_ge(ssq_done, TOK * h + t - 1)
                eng.wait_ge(scaled_done, TOK * h + t - 1)
            eng.tensor_tensor(branches[t % 2][:], ps[:, t, :], part[:, t, :], ALU.add).then_inc(sum_done, 1)

        def finish_rows(t):
            r = r_out[:, t:t + 1]
            eng.wait_ge(osd_done, t + 1)
            step(eng.reciprocal(r, r))
            eng.wait_ge(x_tm_in[t // (TOK // 2)], 16)
            eng.wait_ge(scaled_done, TOK + t + 1)
            after()
            eng.scalar_tensor_tensor(ob[:, t, :], ob[:, t, :], r, x_tm[:, t, :], ALU.mult, ALU.add).then_inc(fin_done, 1)

        for h in range(2):
            for n in range(1 if h else 4, 8):
                out_w(8 * h + n)
            for t in range(TOK):
                add_branches(h, t)
                if h == 0 and t == 3:
                    out_w(8)
                if h == 1 and t >= 1:
                    finish_rows(t - 1)
        finish_rows(TOK - 1)

    ctx.close()


def kernel(**inputs):
    import numpy as np
    import concourse.bacc as bacc
    from concourse import mybir as mb
    from concourse.bass_utils import run_bass_kernel_spmd

    f = {k: np.asarray(v) for k, v in inputs.items()}
    x = np.ascontiguousarray(f["x"])
    tokens = np.concatenate([f["meta"], x[0]], axis=0)
    x_cm = np.ascontiguousarray(tokens.T.reshape(KD, P, L).transpose(1, 0, 2))

    w_in = f["w_in"][0]
    a_b, a_c, a_x, a_z, b_z, b_x, _, _, dt, c_a, c_g, c_z = (
        0, 512, 1024, 1536, 2048, 3072, 4096, 4352, 4608, 4624, 5136, 5648)
    cols = [dt, c_g, c_a]
    for i in range(4):
        cols += [b_x + P * (3 * i + n) for n in range(3)]
        if i < 3:
            cols += [c_g + P * (i + 1), c_a + P * (i + 1)]
    for j in range(4):
        cols += [a + P * j for a in (a_c, a_x, a_b, a_z)]
    for j in range(4):
        cols += [b_z + P * (2 * j), b_z + P * (2 * j + 1), c_z + P * j]
    tiles = [w_in[:, c:c + P].reshape(KD, P, P).transpose(1, 0, 2).reshape(P, KD * P) for c in cols]
    w_out = f["w_out"][0]
    for h in range(2):
        for n in range(8):
            ks = OUT_K[2 * n:2 * n + 2]
            tiles.append(np.concatenate([w_out[P * k:P * (k + 1), HALF * h:HALF * (h + 1)] for k in ks], axis=1))
    w_tiles = np.ascontiguousarray(np.stack(tiles))

    def chan(a):
        a = np.asarray(a)
        t = a.shape[-1] // P
        return a.reshape(-1, t, P).transpose(2, 1, 0).reshape(P, -1)

    params = np.zeros((P, N_PRM), np.float32)

    def put(name, value):
        at, n = PRM[name]
        params[:, at:at + n] = value

    put("pre_g", chan(f["pre_g"][0]))
    put("ssm_w", chan(np.concatenate([f["ssm_conv_w"][0], f["ssm_conv_b"]])))
    put("conf_w", chan(np.concatenate([f["conf_conv_w"][0], f["conf_conv_b"]])))
    put("ln_g", chan(f["conf_ln_g"][0]))
    put("ln_b", chan(f["conf_ln_b"][0]))
    put("gain", 1.0)
    at = PRM["gain"][0] + N_A
    params[:, at:at + N_B] = chan(f["ssm_norm_g"][0])
    put("d_skip", np.repeat(f["d_skip"][0], HD).reshape(N_B, P).T)
    put("a_log", np.broadcast_to(f["a_log"][0], (P, HEADS)))
    put("conv_a", chan(f["conv_a_w"][0]))
    params[0:HEADS, PRM["dt_bias"][0]] = f["dt_bias"][0]
    put("norm_eps", NORM_EPS)
    put("ln_eps", LN_EPS)

    arrays = {"xT_dram": x_cm, "x_dram": x, "w_dram": w_tiles, "params_dram": params,
              "post_g_dram": np.ascontiguousarray(f["post_g"][0])}
    nc = bacc.Bacc("TRN2", target_bir_lowering=False, num_devices=1, dynamic_dma_scratch_size=1024)
    aps = [nc.dram_tensor(k, v.shape, mb.dt.from_np(v.dtype), kind="ExternalInput").ap() for k, v in arrays.items()]
    acum = nc.dram_tensor("acum_dram", (HEADS, SEQ), mb.dt.float32, kind="Internal").ap()
    out = nc.dram_tensor("out_dram", x.shape, mb.dt.from_np(x.dtype), kind="ExternalOutput").ap()
    hybrid_mixer_kernel(nc, *aps, acum, out)
    r = run_bass_kernel_spmd(nc, [arrays], core_ids=[0])
    return r.results[0]["out_dram"]
```
